# Optimizing a Trainium2 kernel written in Bass

```python
import math
import jax, jax.numpy as jnp
from jax import lax
import numpy as np

D_MODEL = 1024
BATCH = 1
SEQ = 512
DEPTH = 2

CHUNK = 64
N_MIXERS = 2
S5_GROUP = 16
S5_GROUPS = D_MODEL // S5_GROUP
S5_STATE = 64
S5_DT_MIN = 0.001
S5_DT_MAX = 0.1
S5_LAMBDA_RE_MAX = -1e-4
DA_HEADS = 8
DA_HEAD_DIM = D_MODEL // DA_HEADS // 2
DA_V_DIM = 2 * DA_HEAD_DIM
ROPE_THETA = 10000.0
Q_BLOCK = 128
MAX_POS_OFFSET = 65536
D_FF = 2816
CONV_WIDTH = 3
EPS = 1e-6

N_S5 = (DEPTH + 1) // 2
N_DA = DEPTH // 2

kernel_name = "hybrid_s5_diffattn_convffn_block"

def rms_norm(h, g):
    hf = h.astype(jnp.float32)
    hf = hf * lax.rsqrt(jnp.mean(hf * hf, axis=-1, keepdims=True) + EPS)
    return (hf * g.astype(jnp.float32)).astype(h.dtype)

def modulate(h, shift, scale):
    return h * (1.0 + scale[:, None, :]) + shift[:, None, :]

def rope(t, pos):
    half = t.shape[-1] // 2
    inv = ROPE_THETA ** (-jnp.arange(half, dtype=jnp.float32) / half)
    ang = pos.astype(jnp.float32)[..., None] * inv
    cos = jnp.cos(ang)[:, :, None, :]
    sin = jnp.sin(ang)[:, :, None, :]
    tf = t.astype(jnp.float32)
    t1, t2 = tf[..., :half], tf[..., half:]
    return jnp.concatenate([t1 * cos - t2 * sin, t2 * cos + t1 * sin], axis=-1).astype(t.dtype)

def s5_mixer(u, a_re, a_im, log_dt, b_re, b_im, c_re, c_im, d_skip, w_glu):
    bsz, seq_len, d = u.shape
    f32 = jnp.float32
    lam_re = jnp.minimum(a_re.astype(f32), S5_LAMBDA_RE_MAX)
    lam_im = a_im.astype(f32)
    dt = jnp.exp(log_dt.astype(f32))[:, None]
    dre, dimg = lam_re * dt, lam_im * dt
    mag = jnp.exp(dre)
    lb_re, lb_im = mag * jnp.cos(dimg), mag * jnp.sin(dimg)
    den = lam_re * lam_re + lam_im * lam_im
    nr = lb_re - 1.0
    f_re = (nr * lam_re + lb_im * lam_im) / den
    f_im = (lb_im * lam_re - nr * lam_im) / den
    br, bi = b_re.astype(f32), b_im.astype(f32)
    bb_re = f_re[..., None] * br - f_im[..., None] * bi
    bb_im = f_re[..., None] * bi + f_im[..., None] * br
    cr, ci = c_re.astype(f32), c_im.astype(f32)
    k = jnp.arange(1, CHUNK + 1, dtype=f32)[:, None, None]
    pmag = jnp.exp(k * dre)
    pw_re, pw_im = pmag * jnp.cos(k * dimg), pmag * jnp.sin(k * dimg)

    u32 = u.astype(f32)
    n_chunks = seq_len // CHUNK
    u_c = jnp.moveaxis(u32.reshape(bsz, n_chunks, CHUNK, S5_GROUPS, S5_GROUP), 1, 0)

    def combine(e1, e2):
        a1r, a1i, b1r, b1i = e1
        a2r, a2i, b2r, b2i = e2
        return (a1r * a2r - a1i * a2i, a1r * a2i + a1i * a2r,
                a2r * b1r - a2i * b1i + b2r, a2r * b1i + a2i * b1r + b2i)

    def chunk_step(carry, uc):
        h_re, h_im = carry
        bu_re = jnp.einsum("btgc,gpc->btgp", uc, bb_re)
        bu_im = jnp.einsum("btgc,gpc->btgp", uc, bb_im)
        ar = jnp.broadcast_to(lb_re, bu_re.shape)
        ai = jnp.broadcast_to(lb_im, bu_im.shape)
        _, _, hl_re, hl_im = lax.associative_scan(combine, (ar, ai, bu_re, bu_im), axis=1)
        hp_re, hp_im = h_re[:, None], h_im[:, None]
        ht_re = hl_re + pw_re * hp_re - pw_im * hp_im
        ht_im = hl_im + pw_re * hp_im + pw_im * hp_re
        y = (jnp.einsum("btgp,gcp->btgc", ht_re, cr)
             - jnp.einsum("btgp,gcp->btgc", ht_im, ci))
        return (ht_re[:, -1], ht_im[:, -1]), y

    h0 = jnp.zeros((bsz, S5_GROUPS, S5_STATE), f32)
    _, ys = lax.scan(chunk_step, (h0, h0), u_c)
    y = jnp.moveaxis(ys, 0, 1).reshape(bsz, seq_len, d)
    y = y + d_skip.astype(f32) * u32
    z = jax.nn.gelu(y).astype(u.dtype)
    val, gate = jnp.split(z @ w_glu, 2, axis=-1)
    return val * jax.nn.sigmoid(gate)

def diff_attention(h, pos, w_qkv, w_o, lq1, lk1, lq2, lk2, subln_g, lambda_init):
    bsz, seq_len, d = h.shape
    f32 = jnp.float32
    q, k, v = jnp.split(h @ w_qkv, 3, axis=-1)
    q = rope(q.reshape(bsz, seq_len, 2 * DA_HEADS, DA_HEAD_DIM), pos)
    k = rope(k.reshape(bsz, seq_len, 2 * DA_HEADS, DA_HEAD_DIM), pos)
    q = (q * (DA_HEAD_DIM ** -0.5)).reshape(bsz, seq_len, DA_HEADS, 2, DA_HEAD_DIM)
    k = k.reshape(bsz, seq_len, DA_HEADS, 2, DA_HEAD_DIM)
    v = v.reshape(bsz, seq_len, DA_HEADS, DA_V_DIM)
    lam = (jnp.exp(jnp.sum(lq1.astype(f32) * lk1.astype(f32)))
           - jnp.exp(jnp.sum(lq2.astype(f32) * lk2.astype(f32))) + lambda_init)
    outs = []
    for qb in range(seq_len // Q_BLOCK):
        q0, kend = qb * Q_BLOCK, (qb + 1) * Q_BLOCK
        s = jnp.einsum("bqhcd,bkhcd->bhcqk", q[:, q0:kend], k[:, :kend]).astype(f32)
        q_idx = q0 + jnp.arange(Q_BLOCK)
        chunk_end = (q_idx // CHUNK + 1) * CHUNK
        mask = jnp.arange(kend)[None, :] < chunk_end[:, None]
        p = jax.nn.softmax(jnp.where(mask, s, -jnp.inf), axis=-1)
        attn = (p[:, :, 0] - lam * p[:, :, 1]).astype(v.dtype)
        outs.append(jnp.einsum("bhqk,bkhe->bqhe", attn, v[:, :kend]))
    o = jnp.concatenate(outs, axis=1)
    o = rms_norm(o, subln_g) * (1.0 - lambda_init)
    return o.reshape(bsz, seq_len, d) @ w_o

def conv_ffn(h, w_in, conv_w, conv_b, w_out):
    seq_len = h.shape[1]
    u = h @ w_in
    up = jnp.pad(u, ((0, 0), (CONV_WIDTH - 1, 0), (0, 0)))
    u = conv_b + sum(conv_w[j] * up[:, j:j + seq_len] for j in range(CONV_WIDTH))
    a, b = jnp.split(u, 2, axis=-1)
    return (jax.nn.gelu(a) * b) @ w_out

def setup_inputs(seed: int = 0) -> dict:
    key = jax.random.key(seed)
    ks = jax.random.split(key, 26)
    f32 = jnp.float32

    def nrm(k, shape, s):
        return jax.random.normal(k, shape, f32) * s

    G, P, Cg = S5_GROUPS, S5_STATE, S5_GROUP
    x = nrm(ks[0], (BATCH, SEQ, D_MODEL), 1.0)
    c = nrm(ks[1], (BATCH, D_MODEL), 1.0)
    offset = jax.random.randint(ks[2], (BATCH, 1), 0, MAX_POS_OFFSET, dtype=jnp.int32)
    positions = offset + jnp.arange(SEQ, dtype=jnp.int32)[None, :]
    ada_w = nrm(ks[3], (DEPTH, D_MODEL, 6 * D_MODEL), 0.5 * D_MODEL ** -0.5)
    ada_b = nrm(ks[4], (DEPTH, 6 * D_MODEL), 0.02)
    norm_g = 1.0 + nrm(ks[5], (DEPTH, 4, D_MODEL), 0.05)
    s5_a_re = -0.5 + nrm(ks[6], (N_S5, G, P), 0.01)
    s5_a_im = math.pi * jnp.arange(P, dtype=f32) + nrm(ks[7], (N_S5, G, P), 0.01)
    s5_log_dt = jax.random.uniform(ks[8], (N_S5, G), f32, math.log(S5_DT_MIN), math.log(S5_DT_MAX))
    s5_b_re = nrm(ks[9], (N_S5, G, P, Cg), (2 * Cg) ** -0.5)
    s5_b_im = nrm(ks[10], (N_S5, G, P, Cg), (2 * Cg) ** -0.5)
    s5_c_re = nrm(ks[11], (N_S5, G, Cg, P), P ** -0.5)
    s5_c_im = nrm(ks[12], (N_S5, G, Cg, P), P ** -0.5)
    s5_d = nrm(ks[13], (N_S5, D_MODEL), 1.0)
    s5_w_glu = nrm(ks[14], (N_S5, D_MODEL, 2 * D_MODEL), D_MODEL ** -0.5)
    da_w_qkv = nrm(ks[15], (N_DA, D_MODEL, 3 * D_MODEL), D_MODEL ** -0.5)
    da_w_o = nrm(ks[16], (N_DA, D_MODEL, D_MODEL), D_MODEL ** -0.5)
    da_lq1 = nrm(ks[17], (N_DA, DA_HEAD_DIM), 0.1)
    da_lk1 = nrm(ks[18], (N_DA, DA_HEAD_DIM), 0.1)
    da_lq2 = nrm(ks[19], (N_DA, DA_HEAD_DIM), 0.1)
    da_lk2 = nrm(ks[20], (N_DA, DA_HEAD_DIM), 0.1)
    da_subln_g = 1.0 + nrm(ks[21], (N_DA, DA_V_DIM), 0.05)
    ffn_w_in = nrm(ks[22], (DEPTH, D_MODEL, 2 * D_FF), D_MODEL ** -0.5)
    ffn_conv_w = nrm(ks[23], (DEPTH, CONV_WIDTH, 2 * D_FF), CONV_WIDTH ** -0.5)
    ffn_conv_b = nrm(ks[24], (DEPTH, 2 * D_FF), 0.02)
    ffn_w_out = nrm(ks[25], (DEPTH, D_FF, D_MODEL), D_FF ** -0.5)
    return {"x": x, "c": c, "positions": positions, "ada_w": ada_w, "ada_b": ada_b,
            "norm_g": norm_g, "s5_a_re": s5_a_re, "s5_a_im": s5_a_im, "s5_log_dt": s5_log_dt,
            "s5_b_re": s5_b_re, "s5_b_im": s5_b_im, "s5_c_re": s5_c_re, "s5_c_im": s5_c_im,
            "s5_d": s5_d, "s5_w_glu": s5_w_glu, "da_w_qkv": da_w_qkv, "da_w_o": da_w_o,
            "da_lq1": da_lq1, "da_lk1": da_lk1, "da_lq2": da_lq2, "da_lk2": da_lk2,
            "da_subln_g": da_subln_g, "ffn_w_in": ffn_w_in, "ffn_conv_w": ffn_conv_w,
            "ffn_conv_b": ffn_conv_b, "ffn_w_out": ffn_w_out}

def reference(x, c, positions, ada_w, ada_b, norm_g, s5_a_re, s5_a_im, s5_log_dt,
              s5_b_re, s5_b_im, s5_c_re, s5_c_im, s5_d, s5_w_glu, da_w_qkv, da_w_o,
              da_lq1, da_lk1, da_lq2, da_lk2, da_subln_g, ffn_w_in, ffn_conv_w,
              ffn_conv_b, ffn_w_out):
    cond = jax.nn.silu(c)
    for i in range(DEPTH):
        mod = cond @ ada_w[i] + ada_b[i]
        sh_t, sc_t, g_t, sh_c, sc_c, g_c = jnp.split(mod, 6, axis=-1)
        h = modulate(rms_norm(x, norm_g[i, 0]), sh_t, sc_t)
        j = i // N_MIXERS
        if i % N_MIXERS == 0:
            h = s5_mixer(h, s5_a_re[j], s5_a_im[j], s5_log_dt[j], s5_b_re[j], s5_b_im[j],
                         s5_c_re[j], s5_c_im[j], s5_d[j], s5_w_glu[j])
        else:
            lambda_init = 0.8 - 0.6 * math.exp(-0.3 * i)
            h = diff_attention(h, positions, da_w_qkv[j], da_w_o[j], da_lq1[j], da_lk1[j],
                               da_lq2[j], da_lk2[j], da_subln_g[j], lambda_init)
        x = x + g_t[:, None, :] * rms_norm(h, norm_g[i, 1])
        h = modulate(rms_norm(x, norm_g[i, 2]), sh_c, sc_c)
        h = conv_ffn(h, ffn_w_in[i], ffn_conv_w[i], ffn_conv_b[i], ffn_w_out[i])
        x = x + g_c[:, None, :] * rms_norm(h, norm_g[i, 3])
    return x


_drawn_inputs = setup_inputs


def setup_inputs(seed=0):
    import zlib

    import numpy as np

    out = dict(_drawn_inputs(seed))
    spreads = {}
    factors = {'s5_a_re': 8.0,
     's5_b_re': 2.668,
     's5_b_im': 2.691,
     's5_c_re': 2.819,
     's5_c_im': 2.731,
     'da_lq1': 4.935,
     'da_lk1': 8.0,
     'da_lq2': 8.0,
     'da_lk2': 8.0,
     'da_subln_g': 4.201,
     'ffn_conv_b': 5.468}
    for name, (base, spread) in spreads.items():
        noise = np.random.default_rng([zlib.crc32(name.encode()), seed]).standard_normal(out[name].shape)
        drawn = base * np.exp(spread * noise) if base else spread * noise
        out[name] = __import__('jax').numpy.asarray(drawn.astype(out[name].dtype))
    for name, factor in factors.items():
        out[name] = (out[name] * factor).astype(out[name].dtype)
    return out
```

```python
import math
from contextlib import ExitStack
from functools import partial

import numpy as np

import concourse.bass as bass
from concourse import mybir

F32 = mybir.dt.float32
F32R = mybir.dt.float32r
I32 = mybir.dt.int32
ALU = mybir.AluOpType
ACT = mybir.ActivationFunctionType
AXX = mybir.AxisListType.X

P = 128
D = 1024
SEQ = 512
KT = D // P
UNIT = 2048
DFF = 2816
JT = DFF // P
EPS = 1e-6

CG = 16
GROUPS = D // CG
PAIRS = GROUPS // 2
BL = 8
NB = SEQ // BL
OCTS = 4
PO = PAIRS // OCTS
LAM_MAX = -1e-4

HEADS = 8
HD = 64
QT = SEQ // P
LAMBDA_INIT = 0.8 - 0.6 * math.exp(-0.3)
ROPE_THETA = 10000.0
MASKED = -1e30

N_GLU, N_FIN, N_FOUT, N_V, N_QK, N_WO = KT, JT, 12, 4, HEADS, 4
U_GLU = 0
U_FIN = (N_GLU, N_GLU + N_FIN + N_FOUT + N_V + N_QK + N_WO)
U_FOUT = (U_FIN[0] + N_FIN, U_FIN[1] + N_FIN)
U_V = U_FOUT[0] + N_FOUT
U_QK = U_V + N_V
U_WO = U_QK + N_QK
N_UNITS = U_FOUT[1] + N_FOUT
N_ADA_PE = 8
THIRD = UNIT // P
FOUT_K = 4

TWO_PI = 2.0 * math.pi
PI_A = 6.28125
PI_B = float(np.float32(round((TWO_PI - PI_A) * 2.0 ** 19) / 2.0 ** 19))
PI_C = float(np.float32(TWO_PI - PI_A - PI_B))
PI_CLAMP = float(np.nextafter(np.float32(math.pi), np.float32(0)))
ROUND = 1.5 * 2.0 ** 23
HEAD_STEPS = 20
RSQRT_MAGIC = float(0x5F3759DF)


def build(nc, a, out_t):
    ctx = ExitStack()
    with ctx:
        base = [nc.sbuf_base]

        def at(name, shape, dt, offset):
            return nc.alloc_sbuf_tensor_at(name, shape, dt, offset=offset)

        def place(nbytes):
            o = (base[0] + 31) // 32 * 32
            base[0] = o + nbytes
            return o

        def sb(name, shape, dt=F32):
            n = int(np.prod(shape[1:])) * 4
            return at(name, shape, dt, place(n))

        def sem(name):
            return ctx.enter_context(nc.semaphore(name))

        raw_at = place(2 * UNIT * 4)
        raw = at("raw", [P, 2, UNIT], F32, raw_at)
        w_at = place(4 * UNIT * 4)
        whi = at("whi", [P, 2, UNIT], F32R, w_at)
        wlo = at("wlo", [P, 2, UNIT], F32R, w_at + 2 * UNIT * 4)
        x_at = place(KT * SEQ * 4)
        x = at("x", [P, KT, SEQ], F32, x_at)
        h_at = place(2 * KT * SEQ * 4)
        hhi = at("hhi", [P, KT, SEQ], F32R, h_at)
        hlo = at("hlo", [P, KT, SEQ], F32R, h_at + KT * SEQ * 4)
        big_at = place(2 * JT * SEQ * 4)

        ghi = at("ghi", [P, JT, SEQ], F32R, big_at)
        glo = at("glo", [P, JT, SEQ], F32R, big_at + JT * SEQ * 4)
        y_late = at("y_late", [P, KT, SEQ], F32, h_at + KT * SEQ * 4)
        y_glu = at("y_glu", [P, KT, SEQ], F32, big_at)
        ada_ring = at("ada_ring", [P, 2, UNIT], F32, big_at + (JT - 8) * SEQ * 4)
        ada_acc = at("ada_acc", [P, 2, UNIT], F32, big_at + (2 * JT - 8) * SEQ * 4)

        ada0_raw = at("ada0_raw", [P, 2, UNIT], F32, raw_at)
        inb_re = at("inb_re", [P, PAIRS, P], F32, w_at)
        inb_im = at("inb_im", [P, PAIRS, P], F32, w_at + PAIRS * P * 4)
        rot_c = at("rot_c", [P, PAIRS, NB], F32, x_at)
        rot_s = at("rot_s", [P, PAIRS, NB], F32, x_at + PAIRS * NB * 4)
        lb_re = at("lb_re", [P, PAIRS, BL, CG], F32, h_at)
        lb_im = at("lb_im", [P, PAIRS, BL, CG], F32, h_at + PAIRS * BL * CG * 4)
        o = big_at
        u = at("u", [P, GROUPS, NB], F32, o); o += GROUPS * NB * 4
        cl_re = at("cl_re", [P, PAIRS, BL + 1, CG], F32, o); o += PAIRS * (BL + 1) * CG * 4
        cl_im = at("cl_im", [P, PAIRS, BL + 1, CG], F32, o); o += PAIRS * (BL + 1) * CG * 4
        toep, kpad, bd = [], None, []
        for i in range(2):
            toep.append(at(f"toep{i}", [P, 2 * PO, BL * CG], F32, o))
            if i == 0:
                bd = [at("bd_re", [P, PAIRS, 2 * CG], F32, o),
                      at("bd_im", [P, PAIRS, 2 * CG], F32, o + PAIRS * 2 * CG * 4)]
            else:
                kpad = at("kpad", [P, KT, (2 * BL - 1) * CG], F32, o)
            o += 2 * PO * BL * CG * 4
        pw_re = at("pw_re", [P, BL + 1, PAIRS], F32, o)
        pw_im = at("pw_im", [P, BL + 1, PAIRS], F32, o + (BL + 1) * PAIRS * 4)
        v_re = at("v_re", [P, PO * NB], F32, o); o += PO * NB * 4
        v_ni = at("v_ni", [P, PO * NB], F32, o); o += PO * NB * 4
        bc_par = at("bc_par", [P, 4, PAIRS, CG], F32, o)
        hx = []
        for i in range(2):
            hx.append(at(f"hx{i}", [P, 2, PO, NB + 1], F32, o)); o += 2 * PO * (NB + 1) * 4
        bb = at("bb", [P, 2, PAIRS, CG], F32, o)
        z = at("z", [P, BL, PO, CG], F32, o); o += BL * PO * CG * 4
        decay = at("decay", [P, PO, NB], F32, o); o += PO * NB * 4
        sel16 = at("sel16", [P, BL, CG], F32, o); o += P * 4
        blk16 = at("blk16", [P, KT, CG], F32, o); o += P * 4
        assert o <= big_at + 2 * JT * SEQ * 4

        o = big_at
        cosb = at("cosb", [P, SEQ], F32, o); o += SEQ * 4
        sinb = at("sinb", [P, SEQ], F32, o); o += SEQ * 4
        v_sb = at("v_sb", [P, QT, D], F32, o); o += QT * D * 4
        ohi = at("ohi", [P, HEADS, SEQ], F32R, o); o += HEADS * SEQ * 4
        olo = at("olo", [P, HEADS, SEQ], F32R, o); o += HEADS * SEQ * 4
        qk = at("qk", [P, 2, 2, SEQ], F32, o); o += 4 * SEQ * 4
        qk_sw = at("qk_sw", [P, 2, SEQ], F32, o); o += 2 * SEQ * 4
        prob = at("prob", [P, 2, 2, SEQ], F32, o); o += 4 * SEQ * 4
        att = at("att", [P, 2, SEQ], F32, o); o += 2 * SEQ * 4
        att_t = at("att_t", [P, 2, SEQ], F32, o); o += 2 * SEQ * 4
        pos_i = at("pos_i", [P, SEQ], I32, o); o += SEQ * 4
        lam_par = at("lam_par", [P, 4 * HD], F32, o); o += 4 * HD * 4
        maskw = at("maskw", [1, 2, P], F32, o); o += 2 * P * 4
        assert o <= big_at + 2 * JT * SEQ * 4

        ca = sb("ca", [P, 2, SEQ])
        cb = sb("cb", [P, 2, SEQ])
        sq = sb("sq", [P, 2, SEQ])
        ssum = sb("ssum", [P, SEQ])
        s5_at = place(2 * SEQ * 4)
        s5s = at("s5s", [P, 32, PAIRS], F32, s5_at)
        diag = at("diag", [P, QT, P], F32, s5_at)
        on = at("on", [P, QT, P], F32, s5_at + SEQ * 4)
        ident = sb("ident", [P, P])
        ones = sb("ones", [P, P])
        modt = sb("modt", [P, 2, 48])
        ada_b = sb("ada_b", [P, 2, 48])
        norm_g = sb("norm_g", [P, 2, 4, KT])
        pre_a = sb("pre_a", [P, 4, KT])
        gate = sb("gate", [P, 4, KT])
        convp = sb("convp", [P, 2, JT, 2, 4])
        cond = sb("cond", [P, 2, KT])
        dskip = sb("dskip", [P, KT])
        col = sb("col", [P, 8])
        nwt = sb("nwt", [P, 4, NB])
        stat = sb("stat", [P, 48])
        gmask = sb("gmask", [P, BL])
        sub_g = sb("sub_g", [P, 1])
        rope_c = sb("rope_c", [P, 2])
        assert base[0] <= nc.sbuf_usable_end, (base[0], nc.sbuf_usable_end)

        psum = ctx.enter_context(nc.psum_tensor("psum", [P, 8, 512], F32))
        krows = nc.dram_tensor("toeplitz_rows", [D, (2 * BL - 1) * CG], F32).ap()

        raw_landed = [sem("raw_landed0"), sem("raw_landed1")]
        split_hi, split_lo, unit_done = sem("split_hi"), sem("split_lo"), sem("unit_done")
        ada_landed = [sem("ada_landed0"), sem("ada_landed1")]
        ada_used, ada_added, acc_clear = sem("ada_used"), sem("ada_added"), sem("acc_clear")
        par_in, small_in, u_in, x_in, bc_in = (sem("par_in"), sem("small_in"), sem("u_in"),
                                               sem("x_in"), sem("bc_in"))
        pos_in, lam_in = sem("pos_in"), sem("lam_in")
        out_stored = sem("out_stored")
        dve_step, act_step, pool_step = sem("dve_step"), sem("act_step"), sem("pool_step")
        ident_ready, const_ready, cond_ready = (sem("ident_ready"), sem("const_ready"),
                                                sem("cond_ready"))
        tanh_ready, sine_arg, sine_ready = sem("tanh_ready"), sem("sine_arg"), sem("sine_ready")
        tanh_arg = sem("tanh_arg")
        pw_ready, bb_ready, bd_ready, cl_ready = (sem("pw_ready"), sem("bb_ready"),
                                                  sem("bd_ready"), sem("cl_ready"))
        lb_ready, rot_ready = sem("lb_ready"), sem("rot_ready")
        inb_psum, inb_ready = sem("inb_psum"), sem("inb_ready")
        k_psum, k_copied, k_ready, k_stored = (sem("k_psum"), sem("k_copied"), sem("k_ready"),
                                               sem("k_stored"))
        kzero = sem("kzero")
        toep_in = [sem("toep_in0"), sem("toep_in1")]
        usq_ready, usq_added, usum_ready, uvar_psum = (sem("usq_ready"), sem("usq_added"),
                                                       sem("usum_ready"), sem("uvar_psum"))
        mod_psum, mod_ready = sem("mod_psum"), sem("mod_ready")
        umod_rhs, umod_psum, u_ready = sem("umod_rhs"), sem("umod_psum"), sem("u_ready")
        in_psum, in_read, hx_ready = sem("in_psum"), sem("in_read"), sem("hx_ready")
        y5_psum, z_ready, zt_psum, zt_hi, zt_lo = (sem("y5_psum"), sem("z_ready"),
                                                   sem("zt_psum"), sem("zt_hi"), sem("zt_lo"))
        sig_ready, y_ready = sem("sig_ready"), sem("y_ready")
        sq_ready, sq_added, stat_psum, diag_ready, rs_psum = (
            sem("sq_ready"), sem("sq_added"), sem("stat_psum"), sem("diag_ready"), sem("rs_psum"))
        x_ready, t_ready, h_aff, h_hi, h_lo = (sem("x_ready"), sem("t_ready"), sem("h_aff"),
                                               sem("h_hi"), sem("h_lo"))
        tap2, conv_done, gelu_done, g_ready, g_hi, g_lo = (
            sem("tap2"), sem("conv_done"), sem("gelu_done"), sem("g_ready"), sem("g_hi"),
            sem("g_lo"))
        conv_step = sem("conv_step")
        v_copied = sem("v_copied")
        rope_arg, rope_sin, rope_table, lam_exp, lam_arg, lam_ready = (
            sem("rope_arg"), sem("rope_sin"), sem("rope_table"), sem("lam_exp"), sem("lam_arg"),
            sem("lam_ready"))
        sw_copied, sw_mul, cos_mul, qk_ready = (sem("sw_copied"), sem("sw_mul"),
                                                sem("cos_mul"), sem("qk_ready"))
        s_psum, nmax_ready, exp_done, att_ready = (sem("s_psum"), sem("nmax_ready"),
                                                   sem("exp_done"), sem("att_ready"))
        mask_ready = sem("mask_ready")
        att_step, smax, hn_step = sem("att_step"), sem("smax"), sem("hn_step")
        rot_init, rot_first, rot_copy = sem("rot_init"), sem("rot_first"), sem("rot_copy")
        attt_psum, attt_copied, o_psum, osq_done = (sem("attt_psum"), sem("attt_copied"),
                                                    sem("o_psum"), sem("osq_done"))
        on_ready, ot_psum, ot_copied, ot_hi, ot_lo = (sem("on_ready"), sem("ot_psum"),
                                                      sem("ot_copied"), sem("ot_hi"),
                                                      sem("ot_lo"))

        def wait(eng, s, n):
            if isinstance(n, int) and n <= 0:
                return
            eng.wait_ge(s, n)

        def pairs(eng, lo, hi, body):
            with eng.Fori(0, (hi - lo) // 2) as i:
                for s in range(2):
                    body(2 * i + (lo + s), s, i + lo // 2)

        def y_of(r):
            return y_glu if r == 0 else y_late

        def shift_col(r):
            layer, ffn = (r + 1) // 2, (r + 1) % 2
            return layer, 24 * ffn

        block = ctx.enter_context(nc.Block())

        @block.sync
        def _(sp):
            sp.dma_start(s5s[:, 0:3, :], a["s5_par"]).then_inc(par_in, 16)
            sp.dma_start(bc_par[:], a["s5_bc"]).then_inc(bc_in, 16)
            sp.dma_start(u[:], a["x_blocks"].rearrange("p (g b) -> p g b", g=GROUPS)).then_inc(u_in, 16)

            def load_ada0(n):
                wait(sp, ada_used, n - 1)
                sp.dma_start(ada0_raw[:, n % 2, :], a["ada_w"][n]).then_inc(ada_landed[n % 2], 16)

            for n in range(N_ADA_PE):
                load_ada0(n)
            sp.wait_ge(k_ready, 1)
            sp.dma_start(krows.rearrange("(t p) k -> p t k", p=P), kpad[:]).then_inc(k_stored, 16)
            sp.wait_ge(k_stored, 16)

            def load_toeplitz(piece):
                wait(sp, y5_psum, piece - 1)
                for s in range(BL):
                    src = krows[2 * PO * CG * piece:2 * PO * CG * (piece + 1), CG * s:CG * s + BL * CG]
                    sp.dma_start(toep[piece % 2][CG * s:CG * (s + 1), :, :],
                                 src.rearrange("(g c) k -> c g k", c=CG)).then_inc(toep_in[piece % 2], 16)

            load_toeplitz(0)
            load_toeplitz(1)
            sp.wait_ge(ada_used, N_ADA_PE)
            for n in range(2):
                sp.dma_start(raw[:, n, :], a["units"][n]).then_inc(raw_landed[n], 16)
            for piece in range(2, OCTS):
                load_toeplitz(piece)
            sp.wait_ge(hx_ready, OCTS)
            sp.dma_start(x[:], a["x_t"].rearrange("(t p) s -> p t s", p=P)).then_inc(x_in, 16)

            def load_unit(n, s, half):
                sp.wait_ge(split_lo, n - 1)
                sp.dma_start(raw[:, s, :], a["units"][n]).then_inc(raw_landed[s], 16)

            def load_ada(m, s):
                wait(sp, ada_added, m - 1)
                sp.dma_start(ada_ring[:, s, :], a["ada_w"][m + N_ADA_PE]).then_inc(ada_landed[s], 16)

            sp.wait_ge(y5_psum, OCTS)
            load_ada(0, 0)
            load_ada(1, 1)
            load_unit(2, 0, None)
            load_unit(3, 1, None)

            def load_both(i, s, half):
                load_unit(i + 4, s, half)
                for e in range(2):
                    load_ada(2 * i + (2 + e), e)

            pairs(sp, 0, N_GLU + 10, load_both)
            load_both(N_GLU + 10, 0, None)
            load_unit(N_GLU + 15, 1, None)
            pairs(sp, N_GLU + 16, U_V + 2, load_unit)
            sp.wait_ge(unit_done, U_V)
            sp.dma_start(pos_i[:], a["positions"].partition_broadcast(P)).then_inc(pos_in, 16)
            sp.dma_start(lam_par[:], a["lam_par"].partition_broadcast(P)).then_inc(lam_in, 16)
            pairs(sp, U_V + 2, N_UNITS, load_unit)
            for f in range(KT):
                sp.wait_ge(x_ready, 3 * KT + f + 1)
                sp.dma_start(out_t[P * f:P * (f + 1), :], x[:, f, :]).then_inc(out_stored, 16)
            sp.wait_ge(out_stored, 16 * KT)

        @block.gpsimd
        def _(pool):
            steps = [0]

            def link(ins):
                steps[0] += 1
                ins.then_inc(pool_step, 1)
                pool.wait_ge(pool_step, steps[0])

            link(nc.gpsimd.memset(ident[:], 0.0))
            nc.gpsimd.affine_select(out=ident[:], in_=ident[:], compare_op=ALU.not_equal, fill=1.0,
                                    base=0, pattern=[[-1, P]], channel_multiplier=1).then_inc(ident_ready, 1)
            nc.gpsimd.memset(ones[:], 1.0).then_inc(const_ready, 1)
            nc.gpsimd.memset(col[:, 0:1], 1.0 / D).then_inc(const_ready, 1)
            nc.gpsimd.memset(rot_c[:, :, 0], 1.0).then_inc(rot_init, 1)
            nc.gpsimd.memset(rot_s[:, :, 0], 0.0).then_inc(rot_init, 1)

            for q in range(8):
                pool.wait_ge(usq_ready, q + 1)
                if q == 0:
                    nc.gpsimd.tensor_copy(ssum[:], sq[:, 0, :]).then_inc(usq_added, 1)
                else:
                    pool.wait_ge(usq_added, q)
                    nc.gpsimd.tensor_tensor(ssum[:], ssum[:], sq[:, q % 2, :], ALU.add).then_inc(usq_added, 1)

            pool.wait_ge(pw_ready, 1)
            pool.wait_ge(bb_ready, 1)
            ta = cb[:, 0, :].rearrange("p (g c) -> p g c", c=CG)
            tb = cb[:, 1, :].rearrange("p (g c) -> p g c", c=CG)

            def over_c(v):
                return v.unsqueeze(2).broadcast_to([P, PAIRS, CG])

            for s in range(BL):
                pr, pi = over_c(pw_re[:, s, :]), over_c(pw_im[:, s, :])
                nc.gpsimd.tensor_tensor(lb_re[:, :, s, :], pr, bb[:, 0], ALU.mult).then_inc(pool_step, 1)
                nc.gpsimd.tensor_tensor(ta, pi, bb[:, 1], ALU.mult).then_inc(pool_step, 1)
                nc.gpsimd.tensor_tensor(lb_im[:, :, s, :], pr, bb[:, 1], ALU.mult).then_inc(pool_step, 1)
                steps[0] += 3
                link(nc.gpsimd.tensor_tensor(tb, pi, bb[:, 0], ALU.mult))
                nc.gpsimd.tensor_tensor(lb_re[:, :, s, :], lb_re[:, :, s, :], ta, ALU.subtract).then_inc(lb_ready, 1)
                nc.gpsimd.tensor_tensor(lb_im[:, :, s, :], lb_im[:, :, s, :], tb, ALU.add).then_inc(lb_ready, 1)
                pool.wait_ge(lb_ready, 2 * s + 2)

            pool.wait_ge(rot_first, 1)
            pool.wait_ge(rot_init, 2)
            m = 1
            while m < NB:
                n = min(m, NB - 1 - m)
                t = cb[:, :, :].rearrange("p a s -> p (a s)")[:, 0:PAIRS * n].rearrange("p (g b) -> p g b", b=n)
                em_c = rot_c[:, :, m:m + 1].broadcast_to([P, PAIRS, n])
                em_s = rot_s[:, :, m:m + 1].broadcast_to([P, PAIRS, n])
                oc, os = rot_c[:, :, m + 1:m + 1 + n], rot_s[:, :, m + 1:m + 1 + n]
                ic, is_ = rot_c[:, :, 1:1 + n], rot_s[:, :, 1:1 + n]
                if n > 0:
                    link(nc.gpsimd.tensor_tensor(oc, ic, em_c, ALU.mult))
                    link(nc.gpsimd.tensor_tensor(t, is_, em_s, ALU.mult))
                    link(nc.gpsimd.tensor_tensor(oc, oc, t, ALU.subtract))
                    link(nc.gpsimd.tensor_tensor(os, ic, em_s, ALU.mult))
                    link(nc.gpsimd.tensor_tensor(t, is_, em_c, ALU.mult))
                    link(nc.gpsimd.tensor_tensor(os, os, t, ALU.add))
                m *= 2
            nc.gpsimd.memset(col[:, 7:8], 0.0).then_inc(rot_ready, 1)

            def add_squares(stat_):
                for f in range(KT):
                    q = KT * stat_ + f
                    pool.wait_ge(sq_ready, q + 1)
                    if f == 0:
                        wait(pool, stat_psum, stat_)
                        nc.gpsimd.tensor_copy(ssum[:], sq[:, q % 2, :]).then_inc(sq_added, 1)
                    else:
                        pool.wait_ge(sq_added, q)
                        nc.gpsimd.tensor_tensor(ssum[:], ssum[:], sq[:, q % 2, :], ALU.add).then_inc(sq_added, 1)

            def h_low(k):
                for f in range(KT):
                    pool.wait_ge(h_hi, KT * k + f + 1)
                    nc.gpsimd.tensor_tensor(hlo[:, f, :], cb[:, f % 2, :], hhi[:, f, :].bitcast(F32),
                                            ALU.subtract).then_inc(h_lo, 1)

            def ffn_low(layer, lo=0, hi=JT):
                def body(j, s, half):
                    pool.wait_ge(g_hi, j + (layer * JT + 1))
                    nc.gpsimd.tensor_tensor(glo[:, j, :], ca[:, s, :], ghi[:, j, :].bitcast(F32),
                                            ALU.subtract).then_inc(g_lo, 1)
                pairs(pool, lo, hi, body)

            pool.wait_ge(zt_psum, OCTS)
            for i in range(2):
                nc.gpsimd.memset(ada_acc[:, i, :], 0.0).then_inc(acc_clear, 1)
            add_squares(0)
            pool.wait_ge(mod_psum, 2)
            for i in range(2):
                nc.gpsimd.memset(ada_acc[:, i, :], 0.0).then_inc(acc_clear, 1)
            add_squares(1)
            h_low(0)
            ffn_low(0, 0, 6)
            pool.wait_ge(mod_psum, 3)
            nc.gpsimd.memset(ada_acc[:, 0, :], 0.0).then_inc(acc_clear, 1)
            ffn_low(0, 6, JT)
            add_squares(2)
            add_squares(3)
            h_low(1)
            nc.gpsimd.memset(maskw[0:1, 0, 0:HD], MASKED).then_inc(mask_ready, 1)
            nc.gpsimd.memset(maskw[0:1, 0, HD:P], 0.0).then_inc(mask_ready, 1)
            nc.gpsimd.memset(maskw[0:1, 1, :], 1.0).then_inc(mask_ready, 1)

            def rope_sines(h):
                for i in range(2):
                    pool.wait_ge(sw_copied, 2 * h + (i + 1))
                    nc.gpsimd.tensor_tensor(qk_sw[:, i, :], qk_sw[:, i, :], sinb[:], ALU.mult).then_inc(sw_mul, 1)

            def o_low(h, s):
                pool.wait_ge(ot_hi, h + 1)
                nc.gpsimd.tensor_tensor(olo[:, h, :], cb[:, s, :], ohi[:, h, :].bitcast(F32),
                                        ALU.subtract).then_inc(ot_lo, 1)

            pool.sem_inc(ot_lo, 2)
            pool.wait_ge(rope_table, 1)
            rope_sines(0)
            rope_sines(1)

            def head(h, s, half):
                o_low(h - 2, s)
                rope_sines(h)

            pairs(pool, 2, HEADS, head)
            o_low(HEADS - 2, 0)
            o_low(HEADS - 1, 1)
            add_squares(4)
            add_squares(5)
            h_low(2)
            ffn_low(1)
            add_squares(6)

        @block.scalar
        def _(act):
            A = nc.scalar.activation
            for i, (dst, name) in enumerate(((cond[:, 0, :], "c_cols"), (ada_b[:], "ada_b"),
                                             (norm_g[:], "norm_g"), (dskip[:], "d_cols"),
                                             (convp[:], "conv_par"), (sub_g[:], "sub_g"),
                                             (rope_c[:], "rope_c"))):
                act.dma_start(dst, a[name]).then_inc(small_in, 16)
            act.wait_ge(par_in, 16)
            A(s5s[:, 3, :], s5s[:, 2, :], ACT.Tanh, scale=1.0 / 16).then_inc(tanh_ready, 1)
            act.wait_ge(small_in, 16 * 7)
            A(cond[:, 1, :], cond[:, 0, :], ACT.Silu).then_inc(cond_ready, 1)
            act.wait_ge(u_in, 16)
            uf = u[:, :, :].rearrange("p g b -> p (g b)")
            for q in range(8):
                wait(act, usq_added, q - 1)
                A(sq[:, q % 2, :], uf[:, SEQ * q:SEQ * (q + 1)], ACT.Square).then_inc(usq_ready, 1)
            act.wait_ge(tanh_arg, 1)
            A(s5s[:, 8, :], s5s[:, 6, :], ACT.Tanh, scale=0.5).then_inc(tanh_ready, 1)
            act.wait_ge(sine_arg, 1)
            A(s5s[:, 13:17, :], s5s[:, 9:13, :], ACT.Sin).then_inc(sine_ready, 1)
            act.wait_ge(k_psum, 1)
            act.wait_ge(kzero, 1)
            for b in range(2):
                A(kpad[:, 4 * b:4 * b + 4, (BL - 1) * CG:],
                  psum[:, 4 + b, :].rearrange("p (t k) -> p t k", t=4), ACT.Copy).then_inc(k_copied, 1)
            for t in range(16):
                act.wait_ge(inb_psum, t + 1)
                dst = (inb_re if t < 8 else inb_im)[:, 4 * (t % 8):4 * (t % 8) + 4, :]
                A(dst, psum[:, 2 + t % 2, :].rearrange("p (g k) -> p g k", g=4), ACT.Copy).then_inc(inb_ready, 1)

            def split_high(n, s, half):
                act.wait_ge(raw_landed[s], 16 * half + 16)
                if not isinstance(n, int) or n >= 2:
                    act.wait_ge(unit_done, n - 1)
                A(whi[:, s, :], raw[:, s, :], ACT.Copy).then_inc(split_hi, 1)

            def z_steps(piece):
                act.wait_ge(y5_psum, piece + 1)
                wait(act, zt_psum, piece)
                for b in range(2):
                    A(z[:, :, 4 * b:4 * b + 4, :].rearrange("p t g c -> p g t c"),
                      psum[:, 4 + b, :].rearrange("p (g t c) -> p g t c", g=4, t=BL),
                      ACT.Gelu_apprx_tanh).then_inc(z_ready, 1)

            def zt_steps(piece):
                for b in range(2):
                    act.wait_ge(zt_psum, piece + 1)
                    for g2 in range(2):
                        dst = hhi[:, 2 * piece + g2, :].rearrange("p (b t) -> p t b", t=BL)
                        src = psum[:, 2 + b, :].rearrange("p (t g b) -> p g t b", t=4, g=2)
                        ins = A(dst[:, 4 * b:4 * b + 4, :], src[:, g2], ACT.Copy)
                    ins.then_inc(zt_hi, 1)

            for piece in range(OCTS):
                z_steps(piece)
                zt_steps(piece)
            act.wait_ge(in_psum, OCTS)
            for n in range(2):
                split_high(n, n, 0)

            def square(q, src):
                wait(act, sq_added, q - 1)
                A(sq[:, q % 2, :], src, ACT.Square).then_inc(sq_ready, 1)

            def glu(i, s, half):
                act.wait_ge(unit_done, i + 1)
                if not isinstance(i, int) or i >= 2:
                    act.wait_ge(y_ready, i - 1)
                A(ca[:, s, :], psum[:, 2 * s + 1, :], ACT.Sigmoid).then_inc(sig_ready, 1)
                split_high(i + 2, s, half + 1)
                act.wait_ge(y_ready, i + 1)
                if not isinstance(i, int) or i >= 2:
                    act.wait_ge(sq_added, i - 1)
                A(sq[:, s, :], y_glu[:, i, :], ACT.Square).then_inc(sq_ready, 1)

            glu(0, 0, 0)
            glu(1, 1, 0)
            pairs(act, 2, N_GLU, glu)

            def next_input(r):
                k = r
                for f in range(KT):
                    act.wait_ge(x_ready, KT * r + f + 1)
                    square(KT * (2 * r + 1) + f, x[:, f, :])
                layer, c0 = shift_col(r)
                for f in range(KT):
                    n = KT * k + f
                    act.wait_ge(t_ready, n + 1)
                    wait(act, h_lo, n - 1)
                    A(cb[:, f % 2, :], ca[:, f % 2, :], ACT.Identity, scale=pre_a[:, r + 1, f:f + 1],
                      bias=modt[:, layer, c0 + f:c0 + f + 1]).then_inc(h_aff, 1)
                    act.wait_ge(h_aff, n + 1)
                    A(hhi[:, f, :], cb[:, f % 2, :], ACT.Copy).then_inc(h_hi, 1)

            def ffn(layer):
                n0, g0 = U_FIN[layer], layer * JT

                def body(j, s, half):
                    act.wait_ge(unit_done, j + (n0 + 1))
                    if not isinstance(j, int) or j >= 2:
                        act.wait_ge(g_lo, j + (g0 - 1))
                    for i, dst in enumerate((ca, cb)):
                        A(dst[:, s, :], psum[:, 2 * s + i, :], ACT.Identity,
                          scale=convp[:, layer, j, i, 2:3], bias=convp[:, layer, j, i, 3:4]).then_inc(tap2, 1)
                    split_high(j + (n0 + 2), s, half + n0 // 2 + 1)
                    act.wait_ge(conv_done, 2 * j + (2 * g0 + 1))
                    A(ca[:, s, :], ca[:, s, :], ACT.Gelu_apprx_tanh).then_inc(gelu_done, 1)
                    act.wait_ge(g_ready, j + (g0 + 1))
                    A(ghi[:, j, :], ca[:, s, :], ACT.Copy).then_inc(g_hi, 1)

                body(0, 0, 0)
                body(1, 1, 0)
                pairs(act, 2, JT, body)
                r, m0 = 2 * layer + 1, U_FOUT[layer]
                for hf in range(2):
                    last = min(m0 + 6 * hf + 8, N_UNITS)
                    pairs(act, m0 + 6 * hf + 2, last, split_high)
                    for f in range(4):
                        act.wait_ge(y_ready, KT * r + 4 * hf + f + 1)
                        square(KT * 2 * r + 4 * hf + f, y_late[:, 4 * hf + f, :])

            next_input(0)
            ffn(0)
            next_input(1)

            n = U_V
            split_high(n + 2, 0, (n + 2) // 2)
            act.wait_ge(rope_arg, 1)
            A(sinb[:], sinb[:], ACT.Sin).then_inc(rope_sin, 1)
            A(cosb[:], cosb[:], ACT.Sin).then_inc(rope_sin, 1)
            act.wait_ge(lam_arg, 1)
            A(col[:, 3:5], col[:, 1:3], ACT.Exp).then_inc(lam_exp, 1)
            for m in range(1, N_V):
                split_high(n + m + 2, m % 2, (n + m + 2) // 2)

            def swap_copies(h, s, half):
                act.wait_ge(unit_done, h + (U_QK + 1))
                for i in range(2):
                    if not isinstance(h, int) or h >= 1:
                        act.wait_ge(qk_ready, 2 * h + (i - 1))
                    if i == 1:
                        act.wait_ge(cos_mul, 2 * h + 1)
                    for q in range(4):
                        ins = A(qk_sw[32 * (q ^ 1):32 * (q ^ 1) + 32, i, :],
                                psum[32 * q:32 * q + 32, 2 * s + i, :], ACT.Copy)
                    ins.then_inc(sw_copied, 1)
                split_high(h + (U_QK + 2), s, half + U_QK // 2 + 1)

            def out_high(h, s):
                act.wait_ge(ot_psum, h + 1)
                act.wait_ge(ot_lo, h + 1)
                A(cb[:, s, :], psum[:, 6, :], ACT.Copy, scale=sub_g[:, 0:1]).then_inc(ot_copied, 1)
                act.wait_ge(ot_copied, h + 1)
                A(ohi[:, h, :], cb[:, s, :], ACT.Copy).then_inc(ot_hi, 1)

            def soft(h):
                for qt in range(QT):
                    pb, width = qt % 2, (qt + 1) * P
                    act.wait_ge(nmax_ready, 4 * h + (qt + 1))
                    if not isinstance(h, int) or 4 * h + qt >= 2:
                        act.wait_ge(att_ready, 4 * h + (qt - 1))
                    for c in range(2):
                        ins = A(prob[:, pb, c, 0:width], psum[:, 4 + c, 0:width], ACT.Exp,
                                scale=HD ** -0.5, bias=stat[:, 8 * pb + 2 + c:8 * pb + 3 + c],
                                accum_out=stat[:, 8 * pb + 4 + c:8 * pb + 5 + c])
                        ins.then_inc(exp_done, 1)
                    act.wait_ge(attt_psum, 4 * h + (qt + 1))
                    if not isinstance(h, int) or 4 * h + qt >= 2:
                        act.wait_ge(o_psum, 4 * h + (qt - 1))
                    A(att_t[:, pb, 0:width], psum[:, 6, 0:width], ACT.Copy).then_inc(attt_copied, 1)

            def o_square(h):
                act.wait_ge(o_psum, 4 * h + 4)
                if not isinstance(h, int) or h >= 1:
                    act.wait_ge(on_ready, h)
                A(sq[:, 0, :], psum[:, 7, :], ACT.Square).then_inc(osq_done, 1)

            swap_copies(0, 0, 0)
            soft(0)
            swap_copies(1, 1, 0)
            o_square(0)

            def head(h, s, half):
                out_high(h - 2, s)
                soft(h - 1)
                swap_copies(h, s, half)
                o_square(h - 1)

            act.wait_ge(lam_ready, 1)
            pairs(act, 2, HEADS, head)
            out_high(HEADS - 2, 0)
            soft(HEADS - 1)
            o_square(HEADS - 1)
            out_high(HEADS - 1, 1)
            for m in range(N_WO):
                n = U_WO + m
                for i in range(2):
                    act.wait_ge(y_ready, KT * 2 + 2 * m + i + 1)
                    square(KT * 4 + 2 * m + i, y_late[:, 2 * m + i, :])
                split_high(n + 2, m % 2, (n + 2) // 2)
            next_input(2)
            ffn(1)

        @block.vector
        def _(dve):
            steps = [0]
            TT, TS, STT = nc.vector.tensor_tensor, nc.vector.tensor_scalar, nc.vector.scalar_tensor_tensor

            def count(ins):
                steps[0] += 1
                return ins.then_inc(dve_step, 1)

            def here():
                dve.wait_ge(dve_step, steps[0])

            def link(ins):
                count(ins)
                here()

            def signal(s):
                here()
                dve.sem_inc(s, 1)

            def rsqrt(dst, src, scale, lk):
                w = dst.shape[1]
                v, t = nwt[:, 0, 0:w], nwt[:, 1, 0:w]
                lk(TS(v, src, scale, EPS, ALU.mult, ALU.add))
                lk(TS(t.bitcast(I32), v.bitcast(I32), 1, None, ALU.logical_shift_right))
                lk(TS(dst.bitcast(I32), t.bitcast(I32), -1.0, RSQRT_MAGIC, ALU.mult, ALU.add))
                for i in range(4):
                    lk(TT(t, dst, dst, ALU.mult))
                    lk(TT(t, t, v, ALU.mult))
                    lk(TS(t, t, -0.5, 1.5, ALU.mult, ALU.add))
                    lk(TT(dst, dst, t, ALU.mult))

            def reduced(dst_sin, dst_cos, ang, t, lk):
                lk(TS(t, ang, 1.0 / TWO_PI, ROUND, ALU.mult, ALU.add))
                lk(TS(t, t, -ROUND, None, ALU.add))
                lk(STT(dst_sin, t, -PI_A, ang, ALU.mult, ALU.add))
                lk(STT(dst_sin, t, -PI_B, dst_sin, ALU.mult, ALU.add))
                lk(STT(dst_sin, t, -PI_C, dst_sin, ALU.mult, ALU.add))
                lk(TS(dst_sin, dst_sin, PI_CLAMP, -PI_CLAMP, ALU.min, ALU.max))
                lk(STT(dst_cos, dst_sin, -1.0, dst_sin, ALU.mult, ALU.max))
                lk(TS(dst_cos, dst_cos, -1.0, math.pi / 2, ALU.mult, ALU.add))

            dve.wait_ge(ident_ready, 1)
            link(nc.vector.tensor_reduce(sel16[:, 0, :], ident[:].rearrange("p (b c) -> p c b", c=CG), AXX, ALU.add))
            link(nc.vector.tensor_copy(sel16[:, 1:, :], sel16[:, 0:1, :].broadcast_to([P, BL - 1, CG])))
            link(nc.vector.tensor_reduce(gmask[:], ident[:].rearrange("p (b c) -> p b c", c=CG), AXX, ALU.add))
            count(TS(blk16[:], gmask[:].unsqueeze(2).broadcast_to([P, KT, CG]), 1.0 / D, None, ALU.mult))
            count(nc.vector.memset(bd[0][:], 0.0))
            count(nc.vector.memset(bd[1][:], 0.0))
            nc.vector.memset(kpad[:, :, 0:(BL - 1) * CG], 0.0).then_inc(kzero, 1)

            S = [s5s[:, i, :] for i in range(32)]
            a_re, a_im = S[0], S[1]
            dt, lam_re, dre, dim_ = S[4], S[5], S[6], S[7]
            t0, t1, t2, t3 = S[28], S[29], S[30], S[31]

            def exp_from_tanh(dst, t):
                link(TS(t0, t, -1.0, 1.0, ALU.mult, ALU.add))
                link(nc.vector.reciprocal(t1, t0))
                link(TS(t0, t, 1.0, None, ALU.add))
                link(TT(dst, t0, t1, ALU.mult))

            dve.wait_ge(tanh_ready, 1)
            exp_from_tanh(dt, S[3])
            for i in range(3):
                link(TT(dt, dt, dt, ALU.mult))
            link(TS(lam_re, a_re, LAM_MAX, None, ALU.min))
            TT(dre, lam_re, dt, ALU.mult).then_inc(tanh_arg, 1)
            link(TT(dim_, a_im, dt, ALU.mult))
            link(TS(S[27], dim_, float(BL), None, ALU.mult))
            reduced(S[9], S[10], dim_, t0, link)
            reduced(S[11], S[12], S[27], t0, link)
            signal(sine_arg)
            dve.wait_ge(tanh_ready, 2)
            mag = S[17]
            exp_from_tanh(mag, S[8])
            link(TT(S[18], mag, mag, ALU.mult))
            link(TT(S[18], S[18], S[18], ALU.mult))
            link(TT(S[18], S[18], S[18], ALU.mult))
            dve.wait_ge(sine_ready, 1)
            count(nc.vector.memset(pw_re[:, 0, :], 1.0))
            count(nc.vector.memset(pw_im[:, 0, :], 0.0))
            count(TT(pw_re[:, 1, :], mag, S[14], ALU.mult))
            link(TT(pw_im[:, 1, :], mag, S[13], ALU.mult))
            dve.wait_ge(rot_init, 2)
            nc.vector.tensor_copy(rot_s[:, :, 1], S[15]).then_inc(rot_copy, 1)
            dve.wait_ge(rot_copy, 1)
            nc.vector.tensor_copy(rot_c[:, :, 1], S[16]).then_inc(rot_first, 1)
            for m in (1, 2, 4):
                def over(v):
                    return v.broadcast_to([P, m, PAIRS])
                qr, qi = over(pw_re[:, m:m + 1, :]), over(pw_im[:, m:m + 1, :])
                pr, pi = pw_re[:, 1:1 + m, :], pw_im[:, 1:1 + m, :]
                nr, ni = pw_re[:, m + 1:2 * m + 1, :], pw_im[:, m + 1:2 * m + 1, :]
                ta, tb = s5s[:, 20:20 + m, :], s5s[:, 24:24 + m, :]
                count(TT(nr, pr, qr, ALU.mult))
                count(TT(ta, pi, qi, ALU.mult))
                count(TT(ni, pr, qi, ALU.mult))
                link(TT(tb, pi, qr, ALU.mult))
                count(TT(nr, nr, ta, ALU.subtract))
                link(TT(ni, ni, tb, ALU.add))
            f_re, f_im = S[20], S[21]
            count(TT(t0, lam_re, lam_re, ALU.mult))
            link(TT(t1, a_im, a_im, ALU.mult))
            link(TT(t0, t0, t1, ALU.add))
            link(nc.vector.reciprocal(t0, t0))
            link(TS(t1, pw_re[:, 1, :], -1.0, None, ALU.add))
            count(TT(f_re, t1, lam_re, ALU.mult))
            link(TT(t2, pw_im[:, 1, :], a_im, ALU.mult))
            link(TT(f_re, f_re, t2, ALU.add))
            count(TT(f_re, f_re, t0, ALU.mult))
            count(TT(f_im, pw_im[:, 1, :], lam_re, ALU.mult))
            link(TT(t2, t1, a_im, ALU.mult))
            link(TT(f_im, f_im, t2, ALU.subtract))
            link(TT(f_im, f_im, t0, ALU.mult))
            signal(pw_ready)

            def over_c(v):
                return v.unsqueeze(2).broadcast_to([P, PAIRS, CG])

            ta = ca[:, 0, :].rearrange("p (g c) -> p g c", c=CG)
            tb = ca[:, 1, :].rearrange("p (g c) -> p g c", c=CG)

            def complex_rows(dr, di, pr, pi, vr, vi, done=None):
                count(TT(dr, pr, vr, ALU.mult))
                count(TT(ta, pi, vi, ALU.mult))
                count(TT(di, pr, vi, ALU.mult))
                link(TT(tb, pi, vr, ALU.mult))
                count(TT(dr, dr, ta, ALU.subtract))
                link(TT(di, di, tb, ALU.add))

            dve.wait_ge(bc_in, 16)
            complex_rows(bb[:, 0], bb[:, 1], over_c(f_re), over_c(f_im), bc_par[:, 0], bc_par[:, 1])
            for g2 in range(2):
                rows = slice(64 * g2, 64 * g2 + 64)
                cols = slice(CG * g2, CG * g2 + CG)
                nc.vector.tensor_copy(bd[0][rows, :, cols], bb[rows, 0]).then_inc(bd_ready, 1)
                TS(bd[1][rows, :, cols], bb[rows, 1], -1.0, None, ALU.mult).then_inc(bd_ready, 1)
            dve.wait_ge(bd_ready, 4)
            signal(bb_ready)
            dve.wait_ge(usq_added, 8)
            us = nwt[:, 2, :]
            nc.vector.tensor_reduce(us, ssum[:].rearrange("p (g b) -> p b g", g=8), AXX, ALU.add).then_inc(usum_ready, 1)
            dve.wait_ge(uvar_psum, 1)
            urs = nwt[:, 3, :]
            rsqrt(urs, psum[:, 6, 0:NB], 1.0, link)
            G = 2 * PO
            for piece in range(OCTS):
                g = slice(G * piece, G * piece + G)
                count(TT(u[:, g, :], u[:, g, :], urs.unsqueeze(1).broadcast_to([P, G, NB]), ALU.mult))

            for k in range(BL + 1):
                complex_rows(cl_re[:, :, k, :], cl_im[:, :, k, :], over_c(pw_re[:, k, :]),
                             over_c(pw_im[:, k, :]), bc_par[:, 2], bc_par[:, 3])
                if k == BL - 1:
                    signal(cl_ready)
            dve.wait_ge(k_copied, 2)
            dve.wait_ge(small_in, 16 * 7)
            tk = ca[:, 0, 0:KT * CG].rearrange("p (t c) -> p t c", c=CG)
            link(TT(tk, sel16[:, 0:1, :].broadcast_to([P, KT, CG]),
                    dskip[:].unsqueeze(2).broadcast_to([P, KT, CG]), ALU.mult))
            k0 = kpad[:, :, (BL - 1) * CG:BL * CG]
            TT(k0, k0, tk, ALU.add).then_inc(k_ready, 1)

            def modulation(layer, chunks):
                for ch in chunks:
                    c = slice(KT * ch, KT * ch + KT)
                    link(TT(modt[:, layer, c], psum[:, 7, 48 * layer + KT * ch:48 * layer + KT * ch + KT],
                            ada_b[:, layer, c], ALU.add))
                for ch in chunks:
                    sub, kind = ch // 3, ch % 3
                    c = slice(KT * ch, KT * ch + KT)
                    if kind == 1:
                        link(STT(pre_a[:, 2 * layer + sub, :], modt[:, layer, c], 1.0,
                                 norm_g[:, layer, 2 * sub, :], ALU.add, ALU.mult))
                    if kind == 2:
                        link(TT(gate[:, 2 * layer + sub, :], modt[:, layer, c],
                                norm_g[:, layer, 2 * sub + 1, :], ALU.mult))

            dve.wait_ge(ada_used, N_ADA_PE)
            modulation(0, (0, 1))
            um = ca[:, 0, 0:2 * GROUPS].rearrange("p (a t g) -> p a t g", a=2, t=KT)
            for i, v in enumerate((pre_a[:, 0, :], modt[:, 0, 0:KT])):
                TT(um[:, i], v.unsqueeze(2).broadcast_to([P, KT, BL]),
                   gmask[:].unsqueeze(1).broadcast_to([P, KT, BL]), ALU.mult).then_inc(umod_rhs, 1)
            dve.wait_ge(umod_psum, 1)
            here()
            for piece in range(OCTS):
                g = slice(G * piece, G * piece + G)
                for i, op in enumerate((ALU.mult, ALU.add)):
                    c0 = NB + GROUPS * i + G * piece
                    ins = TT(u[:, g, :], u[:, g, :],
                             psum[:, 6, c0:c0 + G].unsqueeze(2).broadcast_to([P, G, NB]), op)
                    if i == 0:
                        link(ins)
                    else:
                        ins.then_inc(u_ready, 1)

            for i in range(2):
                count(nc.vector.memset(hx[i][:, :, :, 0], 0.0))
            dve.wait_ge(rot_ready, 1)
            W = PO * NB

            def flat(v):
                return v.rearrange("p g b -> p (g b)")

            def split_low(n, s, half):
                dve.wait_ge(split_hi, n + 1)
                TT(wlo[:, s, :], raw[:, s, :], whi[:, s, :].bitcast(F32), ALU.subtract).then_inc(split_lo, 1)

            def zt_low(piece):
                for b in range(2):
                    dve.wait_ge(zt_hi, 2 * piece + b + 1)
                    for g2 in range(2):
                        src = psum[:, 2 + b, :].rearrange("p (t g b) -> p g t b", t=4, g=2)[:, g2]
                        dst = hlo[:, 2 * piece + g2, :].rearrange("p (b t) -> p t b", t=BL)
                        hi = hhi[:, 2 * piece + g2, :].bitcast(F32).rearrange("p (b t) -> p t b", t=BL)
                        ins = TT(dst[:, 4 * b:4 * b + 4, :], src, hi[:, 4 * b:4 * b + 4, :], ALU.subtract)
                    ins.then_inc(zt_lo, 1)

            for piece in range(OCTS):
                g = slice(PO * piece, PO * piece + PO)
                rc, rs = rot_c[:, g, :], rot_s[:, g, :]
                here()
                link(nc.vector.tensor_copy(decay[:], S[18][:, g].unsqueeze(2).broadcast_to([P, PO, NB])))
                count(nc.vector.memset(decay[:, :, 0], 0.0))
                dve.wait_ge(in_psum, piece + 1)
                ire = psum[:, 0, :].rearrange("p (g b) -> p g b", g=PO)
                iim = psum[:, 1, :].rearrange("p (g b) -> p g b", g=PO)
                vr = v_re[:].rearrange("p (g b) -> p g b", g=PO)
                vn = v_ni[:].rearrange("p (g b) -> p g b", g=PO)
                t_a = ca[:, 0, :].rearrange("p (g b) -> p g b", g=PO)
                t_b = ca[:, 1, :].rearrange("p (g b) -> p g b", g=PO)
                count(TT(vr, ire, rc, ALU.mult))
                count(TT(t_a, iim, rs, ALU.mult))
                count(TT(vn, ire, rs, ALU.mult))
                TT(t_b, iim, rc, ALU.mult).then_inc(in_read, 1)
                dve.wait_ge(in_read, piece + 1)
                here()
                count(TT(vr, vr, t_a, ALU.add))
                link(TT(vn, vn, t_b, ALU.subtract))
                count(nc.vector.tensor_tensor_scan(v_re[:], flat(decay[:]), v_re[:], 0.0, ALU.mult, ALU.add))
                link(nc.vector.tensor_tensor_scan(v_ni[:], flat(decay[:]), v_ni[:], 0.0, ALU.mult, ALU.add))
                wait(dve, y5_psum, piece - 1)
                n1 = NB - 1
                hr, hn = hx[piece % 2][:, 0, :, 1:NB], hx[piece % 2][:, 1, :, 1:NB]
                vr1, vn1, rc1, rs1 = vr[:, :, 0:n1], vn[:, :, 0:n1], rc[:, :, 0:n1], rs[:, :, 0:n1]
                ta1, tb1 = t_a[:, :, 0:n1], t_b[:, :, 0:n1]
                count(TT(hr, vr1, rc1, ALU.mult))
                count(TT(ta1, vn1, rs1, ALU.mult))
                count(TT(hn, vn1, rc1, ALU.mult))
                link(TT(tb1, vr1, rs1, ALU.mult))
                link(TT(hr, hr, ta1, ALU.add))
                TT(hn, hn, tb1, ALU.subtract).then_inc(hx_ready, 1)
                dve.wait_ge(hx_ready, piece + 1)
                if piece >= 1:
                    zt_low(piece - 1)
            zt_low(OCTS - 1)
            for n in range(2):
                split_low(n, n, 0)

            def ada_step(m, e, k, slot):
                dve.wait_ge(ada_landed[e], 16 * k[1])
                wait(dve, ada_added, m)
                STT(ada_acc[:, slot, :], ada_ring[:, e, :], cond[:, 1, bass.ds(k[0], 1)],
                    ada_acc[:, slot, :], ALU.mult, ALU.add).then_inc(ada_added, 1)

            dve.wait_ge(acc_clear, 2)

            def glu(i, s, half):
                for e in range(2):
                    ada_step(2 * i + e, e, (i, i + (N_ADA_PE // 2 + 1)), e)
                dve.wait_ge(sig_ready, i + 1)
                TT(y_glu[:, i, :], psum[:, 2 * s, :], ca[:, s, :], ALU.mult).then_inc(y_ready, 1)
                split_low(i + 2, s, half)

            glu(0, 0, 0)
            glu(1, 1, 0)
            pairs(dve, 2, N_GLU, glu)

            def spread_rsqrt(stat_):
                dve.wait_ge(stat_psum, stat_ + 1)
                rsqrt(stat[:, 16:16 + QT], psum[:, 4, 0:QT], 1.0, link)
                TT(diag[:], ident[:].unsqueeze(1).broadcast_to([P, QT, P]),
                   stat[:, 16:16 + QT].unsqueeze(2).broadcast_to([P, QT, P]), ALU.mult).then_inc(diag_ready, 1)
                dve.wait_ge(rs_psum, stat_ + 1)

            def post_norm(r):
                spread_rsqrt(2 * r)
                if r == 0:
                    dve.wait_ge(mod_psum, 2)
                    modulation(0, (2, 3, 4, 5))
                y = y_of(r)
                if r == 0:
                    dve.wait_ge(x_in, 16)
                dve.wait_ge(y_ready, KT * (r + 1))
                dve.wait_ge(sq_ready, KT * (2 * r + 1))
                count(TT(y[:, 0, :], y[:, 0, :], psum[:, 5, :], ALU.mult))
                for f in range(KT):
                    if f + 1 < KT:
                        count(TT(y[:, f + 1, :], y[:, f + 1, :], psum[:, 5, :], ALU.mult))
                    dve.wait_ge(dve_step, steps[0] - (1 if f + 1 < KT else 0))
                    STT(x[:, f, :], y[:, f, :], gate[:, r, f:f + 1], x[:, f, :], ALU.mult,
                        ALU.add).then_inc(x_ready, 1)

            def pre_norm(r):
                spread_rsqrt(2 * r + 1)
                for f in range(KT):
                    n = KT * r + f
                    wait(dve, h_aff, n - 1)
                    dve.wait_ge(x_ready, n + 1)
                    TT(ca[:, f % 2, :], x[:, f, :], psum[:, 5, :], ALU.mult).then_inc(t_ready, 1)

            def ffn(layer):
                n0, g0 = U_FIN[layer], layer * JT

                def body(j, s, half, third=None):
                    for i, dst in enumerate((ca, cb)):
                        dve.wait_ge(tap2, 2 * j + (2 * g0 + i + 1))
                        STT(dst[:, s, 1:], psum[:, 2 * s + i, 0:SEQ - 1], convp[:, layer, j, i, 1:2],
                            dst[:, s, 1:], ALU.mult, ALU.add).then_inc(conv_step, 1)
                    for i, dst in enumerate((ca, cb)):
                        dve.wait_ge(conv_step, 2 * j + (2 * g0 + i + 1))
                        STT(dst[:, s, 2:], psum[:, 2 * s + i, 0:SEQ - 2], convp[:, layer, j, i, 0:1],
                            dst[:, s, 2:], ALU.mult, ALU.add).then_inc(conv_done, 1)
                    split_low(j + (n0 + 2), s, half)
                    dve.wait_ge(gelu_done, j + (g0 + 1))
                    dve.wait_ge(conv_done, 2 * j + (2 * g0 + 2))
                    if third is not None:
                        for e in range(2):
                            k = 2 * j + (e - 8 * third)
                            ada_step(2 * j + (2 * N_GLU + e), e, (k, j + (N_ADA_PE // 2 + N_GLU + 1)), third % 2)
                    TT(ca[:, s, :], ca[:, s, :], cb[:, s, :], ALU.mult).then_inc(g_ready, 1)

                if layer == 0:
                    for third in range(3):
                        dve.wait_ge(acc_clear, (4, 4, 5)[third])
                        pairs(dve, 4 * third, 4 * third + 4, partial(body, third=third))
                    pairs(dve, 12, 16, body)
                    dve.wait_ge(mod_psum, 5)
                    modulation(1, range(6))
                    signal(mod_ready)
                    pairs(dve, 16, JT, body)
                else:
                    pairs(dve, 0, JT, body)
                r, m0 = 2 * layer + 1, U_FOUT[layer]
                for hf in range(2):
                    last = min(m0 + 6 * hf + 8, N_UNITS)
                    pairs(dve, m0 + 6 * hf + 2, last, split_low)
                    dve.wait_ge(unit_done, m0 + 6 * (hf + 1))
                    for f in range(4):
                        nc.vector.tensor_copy(y_late[:, 4 * hf + f, :], psum[:, 4 * (1 - hf) + f, :]).then_inc(y_ready, 1)

            post_norm(0)
            pre_norm(0)
            ffn(0)
            post_norm(1)
            pre_norm(1)

            def value_copies(m):
                dve.wait_ge(unit_done, U_V + m + 1)
                for b in range(2):
                    nc.vector.tensor_copy(v_sb[:, 2 * b:2 * b + 2, 256 * m:256 * m + 256],
                                          psum[:, 2 * (m % 2) + b, :].rearrange("p (t e) -> p t e", t=2)).then_inc(v_copied, 1)

            split_low(U_V + 2, 0, None)
            dve.wait_ge(pos_in, 16)
            ang, rt = prob[:, 0, 0, :], prob[:, 0, 1, :]
            link(nc.vector.tensor_copy(ang, pos_i[:]))
            link(TS(ang, ang, rope_c[:, 0:1], None, ALU.mult))
            reduced(sinb[:], cosb[:], ang, rt, link)
            signal(rope_arg)
            dve.wait_ge(lam_in, 16)
            lp = prob[:, 1, 0, 0:2 * HD].rearrange("p (a d) -> p a d", a=2)
            lq = lam_par[:].rearrange("p (a b d) -> p a b d", a=2, b=2)
            link(TT(lp, lq[:, :, 0, :], lq[:, :, 1, :], ALU.mult))
            nc.vector.tensor_reduce(col[:, 1:3], lp, AXX, ALU.add).then_inc(lam_arg, 1)
            value_copies(0)
            dve.wait_ge(rope_sin, 2)
            TS(sinb[:], sinb[:], rope_c[:, 1:2], None, ALU.mult).then_inc(rope_table, 1)
            dve.wait_ge(lam_exp, 1)
            link(TT(col[:, 5:6], col[:, 4:5], col[:, 3:4], ALU.subtract))
            link(TS(col[:, 6:7], col[:, 5:6], -LAMBDA_INIT, None, ALU.add))
            TS(sub_g[:], sub_g[:], 1.0 - LAMBDA_INIT, None, ALU.mult).then_inc(lam_ready, 1)
            for m in range(1, N_V):
                split_low(U_V + m + 2, m % 2, None)
                value_copies(m)

            def rotate(h, s, half):
                for i in (1, 0):
                    dve.wait_ge(unit_done, h + (U_QK + 1))
                    if not isinstance(h, int) or h >= 2:
                        dve.wait_ge(s_psum, 4 * h - 4)
                    if i == 0:
                        dve.wait_ge(sw_copied, 2 * h + 1)
                    TT(qk[:, s, i, :], psum[:, 2 * s + i, :], cosb[:], ALU.mult).then_inc(cos_mul, 1)
                split_low(h + (U_QK + 2), s, half)

            def rotate_add(h, s):
                for i in range(2):
                    dve.wait_ge(sw_mul, 2 * h + (i + 1))
                    dve.wait_ge(cos_mul, 2 * h + (2 - i))
                    TT(qk[:, s, i, :], qk[:, s, i, :], qk_sw[:, i, :], ALU.add).then_inc(qk_ready, 1)

            def soft(h):
                for qt in range(QT):
                    pb, width = qt % 2, (qt + 1) * P
                    st = stat[:, 8 * pb:8 * pb + 8]
                    dve.wait_ge(s_psum, 4 * h + (qt + 1))
                    nc.vector.tensor_reduce(st[:, 0:2], psum[:, 4:6, 0:width], AXX, ALU.max).then_inc(smax, 1)
                    dve.wait_ge(smax, 4 * h + (qt + 1))
                    TS(st[:, 2:4], st[:, 0:2], -HD ** -0.5, None, ALU.mult).then_inc(nmax_ready, 1)
                    dve.wait_ge(exp_done, 8 * h + (2 * qt + 2))
                    nc.vector.reciprocal(st[:, 6:8], st[:, 4:6]).then_inc(att_step, 1)
                    dve.wait_ge(att_step, 12 * h + (3 * qt + 1))
                    TT(st[:, 5:6], st[:, 7:8], col[:, 6:7], ALU.mult).then_inc(att_step, 1)
                    dve.wait_ge(att_step, 12 * h + (3 * qt + 2))
                    TS(prob[:, pb, 1, 0:width], prob[:, pb, 1, 0:width], st[:, 5:6], None,
                       ALU.mult).then_inc(att_step, 1)
                    dve.wait_ge(att_step, 12 * h + (3 * qt + 3))
                    if not isinstance(h, int) or 4 * h + qt >= 2:
                        dve.wait_ge(attt_psum, 4 * h + (qt - 1))
                    STT(att[:, pb, 0:width], prob[:, pb, 0, 0:width], st[:, 6:7],
                        prob[:, pb, 1, 0:width], ALU.mult, ALU.add).then_inc(att_ready, 1)

            def head_norm(h):
                k = [0]

                def lk(ins):
                    k[0] += 1
                    ins.then_inc(hn_step, 1)
                    dve.wait_ge(hn_step, HEAD_STEPS * h + k[0])
                dve.wait_ge(osq_done, h + 1)
                ov = nwt[:, 2, 0:QT]
                lk(nc.vector.tensor_reduce(ov, sq[:, 0, :].rearrange("p (t e) -> p t e", t=QT), AXX, ALU.add))
                rsqrt(nwt[:, 3, 0:QT], ov, 1.0 / P, lk)
                assert k[0] == HEAD_STEPS
                if not isinstance(h, int) or h >= 1:
                    dve.wait_ge(ot_psum, h)
                TT(on[:], psum[:, 7, :].rearrange("p (t e) -> p t e", t=QT),
                   nwt[:, 3, 0:QT].unsqueeze(2).broadcast_to([P, QT, P]), ALU.mult).then_inc(on_ready, 1)

            rotate(0, 0, None)
            rotate_add(0, 0)
            soft(0)
            rotate(1, 1, None)
            head_norm(0)
            rotate_add(1, 1)

            def head(h, s, half):
                soft(h - 1)
                rotate(h, s, half)
                head_norm(h - 1)
                rotate_add(h, s)

            pairs(dve, 2, HEADS, head)
            soft(HEADS - 1)
            head_norm(HEADS - 1)
            for m in range(N_WO):
                n = U_WO + m
                dve.wait_ge(unit_done, n + 1)
                for i in range(2):
                    nc.vector.tensor_copy(y_late[:, 2 * m + i, :], psum[:, 2 * (m % 2) + i, :]).then_inc(y_ready, 1)
                split_low(n + 2, m % 2, None)
            post_norm(2)
            pre_norm(2)
            ffn(1)
            post_norm(3)

        @block.tensor
        def _(pe):
            M = nc.tensor.matmul

            def ada_unit(n, s):
                pe.wait_ge(ada_landed[s], 16 * (n // 2) + 16)
                for f in range(2):
                    for k in range(KT):
                        ins = M(psum[:, 7, 2 * n + f:2 * n + f + 1],
                                ada0_raw[:, s, 256 * k + P * f:256 * k + P * f + P], cond[:, 1, k:k + 1],
                                start=(k == 0), stop=(k == KT - 1))
                ins.then_inc(ada_used, 1)

            def reduce_acc(slot, col0):
                for f in range(THIRD):
                    ins = M(psum[:, 7, col0 + f:col0 + f + 1], ada_acc[:, slot, P * f:P * f + P],
                            ones[:, 0:1], start=True, stop=True)
                ins.then_inc(mod_psum, 1)

            pe.wait_ge(cond_ready, 1)
            for n in range(N_ADA_PE):
                ada_unit(n, n % 2)
                if n == 3:
                    pe.wait_ge(usum_ready, 1)
                    M(psum[:, 6, 0:NB], blk16[:].rearrange("p g c -> p (g c)"), nwt[:, 2, :],
                      start=True, stop=True).then_inc(uvar_psum, 1)
            pe.wait_ge(cl_ready, 1)
            pe.wait_ge(bd_ready, 4)
            for t in range(KT):
                for q in range(4):
                    gp = 4 * t + q
                    out = psum[32 * q:32 * q + 32, 4 + t // 4, P * (t % 4):P * (t % 4) + P]
                    for i, cl in enumerate((cl_re, cl_im)):
                        ins = M(out, bd[i][:, gp, :], cl[:, gp, 0:BL, :].rearrange("p k c -> p (k c)"),
                                start=(i == 0), stop=(i == 1), skip_group_check=True)
            ins.then_inc(k_psum, 1)
            pe.wait_ge(umod_rhs, 2)
            M(psum[:, 6, NB:NB + 2 * GROUPS], sel16[:].rearrange("p t c -> p (t c)"),
              ca[:, 0, 0:2 * GROUPS], start=True, stop=True).then_inc(umod_psum, 1)
            pe.wait_ge(lb_ready, 2 * BL)
            for t in range(16):
                wait(pe, inb_ready, t - 1)
                lb = lb_re if t < 8 else lb_im
                for q in range(4):
                    ins = nc.tensor.transpose(psum[:, 2 + t % 2, P * q:P * q + P],
                                              lb[:, 4 * (t % 8) + q].rearrange("p t c -> p (t c)"), ident[:])
                ins.then_inc(inb_psum, 1)
            pe.wait_ge(inb_ready, 16)

            def inputs(piece):
                pe.wait_ge(u_ready, piece + 1)
                wait(pe, in_read, piece)
                for i, inb in enumerate((inb_re, inb_im)):
                    for j in range(PO):
                        for g2 in range(2):
                            gp = PO * piece + j
                            ins = M(psum[64 * g2:64 * g2 + 64, i, NB * j:NB * j + NB],
                                    inb[:, gp, 64 * g2:64 * g2 + 64], u[:, 2 * gp + g2, :],
                                    start=True, stop=True)
                ins.then_inc(in_psum, 1)

            def outputs(piece):
                pe.wait_ge(toep_in[piece % 2], 16 * BL * (piece // 2 + 1))
                wait(pe, z_ready, 2 * piece)
                pe.wait_ge(hx_ready, piece + 1)
                for j in range(PO):
                    gp = PO * piece + j
                    for g2 in range(2):
                        rows = slice(64 * g2, 64 * g2 + 64)
                        out = psum[rows, 4 + j // 4, P * (j % 4):P * (j % 4) + P]
                        M(out, u[:, 2 * gp + g2, :], toep[piece % 2][:, 2 * j + g2, :], start=True,
                          stop=False, skip_group_check=True)
                        for i, cl in enumerate((cl_re, cl_im)):
                            ins = M(out, hx[piece % 2][rows, i, j, 0:NB],
                                    cl[rows, gp, 1:, :].rearrange("p k c -> p (k c)"), start=False,
                                    stop=(i == 1), skip_group_check=True)
                ins.then_inc(y5_psum, 1)

            def back(piece):
                pe.wait_ge(z_ready, 2 * piece + 2)
                wait(pe, zt_lo, 2 * piece)
                for t in range(BL):
                    ins = nc.tensor.transpose(psum[:, 2 + t // 4, P * (t % 4):P * (t % 4) + P],
                                              z[:, t].rearrange("p g c -> p (g c)"), ident[:])
                ins.then_inc(zt_psum, 1)

            inputs(0)
            for piece in range(OCTS):
                if piece + 1 < OCTS:
                    inputs(piece + 1)
                outputs(piece)
                back(piece)

            def gemm_step(s, step, hi, lo, n_cols=None):
                half, k = divmod(step, KT)
                w = slice(P * step, P * step + P)
                out = psum[:, 2 * s + half, :]
                M(out, whi[:, s, w], hi[:, k, :], start=(k == 0), stop=False)
                M(out, whi[:, s, w], lo[:, k, :], start=False, stop=False)
                return M(out, wlo[:, s, w], hi[:, k, :], start=False, stop=(k == KT - 1))

            def gemm(n, s, hi, lo, ready=None):
                pe.wait_ge(split_lo, n + 1)
                for step in range(2 * KT):
                    if ready and step < KT:
                        ready(step)
                    ins = gemm_step(s, step, hi, lo)
                ins.then_inc(unit_done, 1)

            def glu(i, s, half):
                if not isinstance(i, int) or i >= 2:
                    pe.wait_ge(y_ready, i - 1)
                gemm(i, s, hhi, hlo)

            pe.wait_ge(zt_lo, 2 * OCTS)
            glu(0, 0, 0)
            glu(1, 1, 0)
            pairs(pe, 2, N_GLU, glu)

            def statistic(stat_):
                pe.wait_ge(sq_added, KT * (stat_ + 1))
                for t in range(QT):
                    ins = M(psum[:, 4, t:t + 1], ssum[:, P * t:P * t + P], col[:, 0:1], start=True, stop=True)
                ins.then_inc(stat_psum, 1)
                if stat_ == 0:
                    reduce_acc(1, 2 * THIRD)
                pe.wait_ge(diag_ready, stat_ + 1)
                M(psum[:, 5, :], ones[:], diag[:].rearrange("p t s -> p (t s)"), start=True,
                  stop=True).then_inc(rs_psum, 1)

            def ffn(layer):
                n0, g0 = U_FIN[layer], layer * JT

                def body(j, s, half):
                    if not isinstance(j, int) or j >= 2:
                        pe.wait_ge(conv_done, 2 * j + (2 * g0 - 2))
                    first = isinstance(j, int) and j == 0
                    gemm(j + n0, s, hhi, hlo,
                         (lambda k: pe.wait_ge(h_lo, KT * 2 * layer + k + 1)) if first else None)

                body(0, 0, 0)
                body(1, 1, 0)
                if layer == 0:
                    for third in range(3):
                        pairs(pe, max(4 * third + 2, 2), 4 * third + 6, body)
                        pe.wait_ge(ada_added, 2 * N_GLU + 8 * third + 8)
                        reduce_acc(third % 2, THIRD * (3 + third))
                    pairs(pe, 14, JT, body)
                    pe.wait_ge(mod_ready, 1)
                else:
                    pairs(pe, 2, JT, body)

                for hf in range(2):
                    m0 = U_FOUT[layer] + 6 * hf
                    b0 = 4 * (1 - hf)

                    def down(v, s, half, m0=m0, b0=b0):
                        fixed = isinstance(v, int)
                        n_k = min(FOUT_K, JT - FOUT_K * v) if fixed else FOUT_K
                        pe.wait_ge(split_lo, v + (m0 + 1))
                        for k in range(n_k):
                            row = FOUT_K * v + k
                            pe.wait_ge(g_lo, row + (g0 + 1))
                            for f in range(4):
                                w = slice(512 * k + P * f, 512 * k + P * f + P)
                                out = psum[:, b0 + f, :]
                                st = fixed and v == 0 and k == 0
                                sp_ = fixed and row == JT - 1
                                M(out, whi[:, s, w], ghi[:, row, :], start=st, stop=False)
                                M(out, whi[:, s, w], glo[:, row, :], start=False, stop=False)
                                ins = M(out, wlo[:, s, w], ghi[:, row, :], start=False, stop=sp_)
                        ins.then_inc(unit_done, 1)

                    down(0, 0, 0)
                    down(1, 1, 0)
                    pairs(pe, 2, 4, down)
                    down(4, 0, 0)
                    down(5, 1, 0)

            pe.wait_ge(ada_added, 2 * N_GLU)
            reduce_acc(0, THIRD)
            statistic(0)
            statistic(1)
            ffn(0)
            statistic(2)
            statistic(3)

            for m in range(N_V):
                s = m % 2
                pe.wait_ge(split_lo, U_V + m + 1)
                if m == 0:
                    pe.wait_ge(h_lo, 2 * KT)
                wait(pe, v_copied, 2 * (m - 1))
                for t in range(QT):
                    out = psum[:, 2 * s + t // 2, 256 * (t % 2):256 * (t % 2) + 256]
                    tok = slice(P * t, P * t + P)
                    for k in range(KT):
                        w = slice(256 * k, 256 * k + 256)
                        M(out, hhi[:, k, tok], whi[:, s, w], start=(k == 0), stop=False)
                        M(out, hlo[:, k, tok], whi[:, s, w], start=False, stop=False)
                        ins = M(out, hhi[:, k, tok], wlo[:, s, w], start=False, stop=(k == KT - 1))
                ins.then_inc(unit_done, 1)
            pe.wait_ge(v_copied, 2 * N_V)
            pe.wait_ge(mask_ready, 3)

            def scores(h, s, qt):
                if qt == 0:
                    pe.wait_ge(qk_ready, 2 * h + 2)
                if not isinstance(h, int) or 4 * h + qt >= 1:
                    pe.wait_ge(exp_done, 8 * h + 2 * qt)
                width = (qt + 1) * P
                for c in range(2):
                    rows = slice(HD * c, HD * c + HD)
                    M(psum[:, 4 + c, 0:width], qk[rows, s, 0, P * qt:P * qt + P], qk[rows, s, 1, 0:width],
                      start=True, stop=True)
                    ins = M(psum[:, 4 + c, width - HD:width], maskw[0:1, 0, :], maskw[0:1, 1, 0:HD],
                            start=False, stop=True, skip_group_check=True)
                ins.then_inc(s_psum, 1)

            def turn(h, qt):
                pb = qt % 2
                pe.wait_ge(att_ready, 4 * h + (qt + 1))
                if not isinstance(h, int) or 4 * h + qt >= 1:
                    pe.wait_ge(attt_copied, 4 * h + qt)
                for kb in range(qt + 1):
                    ins = nc.tensor.transpose(psum[:, 6, P * kb:P * kb + P], att[:, pb, P * kb:P * kb + P], ident[:])
                ins.then_inc(attt_psum, 1)

            def weigh(h, qt):
                pb = qt % 2
                pe.wait_ge(attt_copied, 4 * h + (qt + 1))
                if qt == 0 and (not isinstance(h, int) or h >= 1):
                    pe.wait_ge(on_ready, h)
                for kb in range(qt + 1):
                    ins = M(psum[:, 7, P * qt:P * qt + P], att_t[:, pb, P * kb:P * kb + P],
                            v_sb[:, kb, bass.ds(h * P, P)] if not isinstance(h, int)
                            else v_sb[:, kb, P * h:P * h + P], start=(kb == 0), stop=(kb == qt))
                ins.then_inc(o_psum, 1)

            def turn_out(h):
                pe.wait_ge(on_ready, h + 1)
                pe.wait_ge(attt_copied, 4 * h + 4)
                for t in range(QT):
                    ins = nc.tensor.transpose(psum[:, 6, P * t:P * t + P], on[:, t, :], ident[:])
                ins.then_inc(ot_psum, 1)

            def head(h, s, half, gemm_on=True, att_on=True, out_on=True):
                if gemm_on:
                    pe.wait_ge(split_lo, h + (U_QK + 1))
                    if not isinstance(h, int) or h >= 2:
                        pe.wait_ge(sw_copied, 2 * h - 2)
                        pe.wait_ge(cos_mul, 2 * h - 2)

                def steps(lo_, hi_):
                    if gemm_on:
                        for step in range(lo_, hi_):
                            ins = gemm_step(s, step, hhi, hlo)
                            if step == 2 * KT - 1:
                                ins.then_inc(unit_done, 1)

                if not att_on:
                    steps(0, 16)
                    return
                b = 1 - s
                steps(0, 4)
                if out_on:
                    turn_out(h - 2)
                scores(h - 1, b, 0)
                steps(4, 7)
                if out_on:
                    pe.wait_ge(ot_copied, h - 1)
                turn(h - 1, 0)
                scores(h - 1, b, 1)
                weigh(h - 1, 0)
                steps(7, 10)
                turn(h - 1, 1)
                scores(h - 1, b, 2)
                weigh(h - 1, 1)
                steps(10, 13)
                turn(h - 1, 2)
                scores(h - 1, b, 3)
                weigh(h - 1, 2)
                steps(13, 16)
                turn(h - 1, 3)
                weigh(h - 1, 3)

            head(0, 0, 0, att_on=False)
            head(1, 1, 0, out_on=False)
            pairs(pe, 2, HEADS, head)
            head(HEADS, 0, 0, gemm_on=False)
            turn_out(HEADS - 1)
            pe.wait_ge(cos_mul, 2 * HEADS)
            pe.wait_ge(sw_copied, 2 * HEADS)
            for m in range(N_WO):
                wait(pe, y_ready, KT * 2 + 2 * (m - 1) if m >= 2 else 0)
                gemm(U_WO + m, m % 2, ohi, olo, (lambda k: pe.wait_ge(ot_lo, k + 3)) if m == 0 else None)
            statistic(4)
            statistic(5)
            ffn(1)
            statistic(6)


def _pair_units(w, rows, left, right, n):
    w = w.reshape(KT, P, -1) if rows is None else rows(w)
    out = np.empty((n, P, 2, KT, P), np.float32)
    for i in range(n):
        for q, c in enumerate((left(i), right(i))):
            out[i, :, q] = w[:, :, c:c + P].transpose(1, 0, 2)
    return out.reshape(n, P, UNIT)


def _units(inp):
    def glu_rows(w):
        return w.reshape(OCTS, PO, 2, CG, -1).transpose(0, 2, 1, 3, 4).reshape(KT, P, -1)

    def down_units(w):
        w = w.reshape(JT, P, D)
        padded = np.concatenate([w, np.zeros((2, P, D), np.float32)])
        return padded.reshape(6, FOUT_K, P, 2, 512).transpose(3, 0, 2, 1, 4).reshape(N_FOUT, P, UNIT)

    w_in, w_out = inp["ffn_w_in"], inp["ffn_w_out"]
    qkv, wo = inp["da_w_qkv"][0], inp["da_w_o"][0]
    ups = [_pair_units(w_in[i], None, lambda j: P * j, lambda j: DFF + P * j, N_FIN) for i in range(2)]
    values = qkv[:, 2 * D:].reshape(KT, P, N_V, 256).transpose(2, 1, 0, 3).reshape(N_V, P, UNIT)
    return np.concatenate([
        _pair_units(inp["s5_w_glu"][0], glu_rows, lambda j: P * j, lambda j: D + P * j, N_GLU),
        ups[0], down_units(w_out[0]), values,
        _pair_units(qkv, None, lambda j: P * j, lambda j: D + P * j, N_QK),
        _pair_units(wo, None, lambda j: 2 * P * j, lambda j: 2 * P * j + P, N_WO),
        ups[1], down_units(w_out[1])])


def _ada_units(w):
    first = w[0].reshape(KT, P, -1)[:, :, :UNIT].reshape(KT, P, N_ADA_PE, 256).transpose(2, 1, 0, 3)
    rows = w.reshape(2, KT, P, 3, UNIT)
    rest = rows[0, :, :, 1:].transpose(0, 2, 1, 3)
    second = rows[1].transpose(2, 0, 1, 3)
    return np.concatenate([v.reshape(-1, P, UNIT) for v in (first, rest, second)])


def _cols(v):
    return v.reshape(-1, P).T


def _layout(inp):
    def state(v):
        v = v.reshape(PAIRS, 2, 64, *v.shape[2:])
        return v.transpose(1, 2, 0, *range(3, v.ndim)).reshape(P, PAIRS, *v.shape[3:])

    x0 = inp["x"][0]
    log_dt = np.broadcast_to(inp["s5_log_dt"][0][:, None], (GROUPS, 64))
    half = HD // 2
    inv = (ROPE_THETA ** (-np.arange(half, dtype=np.float32) / np.float32(half)).astype(np.float64)).astype(np.float32)
    sign = np.where(np.arange(P) % HD < half, -1.0, 1.0).astype(np.float32)
    conv = np.concatenate([inp["ffn_conv_w"], inp["ffn_conv_b"][:, None]], axis=1)
    return {
        "x_t": x0.T,
        "x_blocks": x0.reshape(NB, BL, GROUPS, CG)[:, ::-1].transpose(1, 3, 2, 0).reshape(P, GROUPS * NB),
        "s5_par": np.stack([state(inp["s5_a_re"][0]), state(inp["s5_a_im"][0]), state(log_dt)], axis=1),
        "s5_bc": np.stack([state(inp["s5_b_re"][0]), state(inp["s5_b_im"][0]),
                           state(inp["s5_c_re"][0].transpose(0, 2, 1)),
                           state(inp["s5_c_im"][0].transpose(0, 2, 1))], axis=1),
        "c_cols": _cols(inp["c"][0]),
        "d_cols": _cols(inp["s5_d"][0]),
        "ada_b": np.stack([_cols(v) for v in inp["ada_b"]], axis=1),
        "norm_g": np.stack([np.stack([_cols(v) for v in g], axis=1) for g in inp["norm_g"]], axis=1),
        "conv_par": conv.reshape(2, 4, 2, JT, P).transpose(4, 0, 3, 2, 1),
        "sub_g": inp["da_subln_g"][0][:, None],
        "rope_c": np.stack([np.tile(inv, P // half), sign], axis=1),
        "positions": inp["positions"][0],
        "lam_par": np.concatenate([inp[n][0] for n in ("da_lq1", "da_lk1", "da_lq2", "da_lk2")]),
        "ada_w": _ada_units(inp["ada_w"]),
        "units": _units(inp),
    }


def kernel(**inputs):
    import concourse.bacc as _bacc
    from concourse import mybir as _mybir
    from concourse.bass_utils import run_bass_kernel_spmd as _run

    inp = {k: np.asarray(v) for k, v in inputs.items()}
    arrays = {k: np.ascontiguousarray(v) for k, v in _layout(inp).items()}
    nc = _bacc.Bacc("TRN2", target_bir_lowering=False, num_devices=1)
    aps = {k: nc.dram_tensor(f"in_{k}", v.shape, _mybir.dt.from_np(v.dtype), kind="ExternalInput").ap()
           for k, v in arrays.items()}
    out = nc.dram_tensor("out_t", (D, SEQ), F32, kind="ExternalOutput").ap()
    build(nc, aps, out)
    r = _run(nc, [{f"in_{k}": v for k, v in arrays.items()}], core_ids=[0])
    return r.results[0]["out_t"].T.reshape(1, SEQ, D)
```

```python
import math
from contextlib import ExitStack
from functools import partial

import numpy as np

import concourse.bass as bass
from concourse import mybir

F32 = mybir.dt.float32
F32R = mybir.dt.float32r
I32 = mybir.dt.int32
ALU = mybir.AluOpType
ACT = mybir.ActivationFunctionType
AXX = mybir.AxisListType.X

P = 128
D = 1024
SEQ = 512
KT = D // P
UNIT = 2048
DFF = 2816
JT = DFF // P
EPS = 1e-6

CG = 16
GROUPS = D // CG
PAIRS = GROUPS // 2
BL = 8
NB = SEQ // BL
OCTS = 4
PO = PAIRS // OCTS
LAM_MAX = -1e-4

HEADS = 8
HD = 64
QT = SEQ // P
LAMBDA_INIT = 0.8 - 0.6 * math.exp(-0.3)
ROPE_THETA = 10000.0
MASKED = -1e30

N_GLU, N_FIN, N_FOUT, N_V, N_QK, N_WO = KT, JT, 12, 4, HEADS, 4
U_GLU = 0
U_FIN = (N_GLU, N_GLU + N_FIN + N_FOUT + N_V + N_QK + N_WO)
U_FOUT = (U_FIN[0] + N_FIN, U_FIN[1] + N_FIN)
U_V = U_FOUT[0] + N_FOUT
U_QK = U_V + N_V
U_WO = U_QK + N_QK
N_UNITS = U_FOUT[1] + N_FOUT
N_ADA_PE = 8
THIRD = UNIT // P
FOUT_K = 4

TWO_PI = 2.0 * math.pi
PI_A = 6.28125
PI_B = float(np.float32(round((TWO_PI - PI_A) * 2.0 ** 19) / 2.0 ** 19))
PI_C = float(np.float32(TWO_PI - PI_A - PI_B))
PI_CLAMP = float(np.nextafter(np.float32(math.pi), np.float32(0)))
ROUND = 1.5 * 2.0 ** 23
HEAD_STEPS = 13
RSQRT_MAGIC = float(0x5F3759DF)


def build(nc, a, out_t):
    ctx = ExitStack()
    with ctx:
        base = [nc.sbuf_base]

        def at(name, shape, dt, offset):
            return nc.alloc_sbuf_tensor_at(name, shape, dt, offset=offset)

        def place(nbytes):
            o = (base[0] + 31) // 32 * 32
            base[0] = o + nbytes
            return o

        def sb(name, shape, dt=F32):
            n = int(np.prod(shape[1:])) * 4
            return at(name, shape, dt, place(n))

        def sem(name):
            return ctx.enter_context(nc.semaphore(name))

        raw_at = place(2 * UNIT * 4)
        raw = at("raw", [P, 2, UNIT], F32, raw_at)
        w_at = place(4 * UNIT * 4)
        whi = at("whi", [P, 2, UNIT], F32R, w_at)
        wlo = at("wlo", [P, 2, UNIT], F32R, w_at + 2 * UNIT * 4)
        x_at = place(KT * SEQ * 4)
        x = at("x", [P, KT, SEQ], F32, x_at)
        h_at = place(2 * KT * SEQ * 4)
        hhi = at("hhi", [P, KT, SEQ], F32R, h_at)
        hlo = at("hlo", [P, KT, SEQ], F32R, h_at + KT * SEQ * 4)
        big_at = place(2 * JT * SEQ * 4)

        ghi = at("ghi", [P, JT, SEQ], F32R, big_at)
        glo = at("glo", [P, JT, SEQ], F32R, big_at + JT * SEQ * 4)
        y_late = at("y_late", [P, KT, SEQ], F32, h_at + KT * SEQ * 4)
        y_glu = at("y_glu", [P, KT, SEQ], F32, big_at)
        ada_ring = at("ada_ring", [P, 2, UNIT], F32, big_at + (JT - 8) * SEQ * 4)
        ada_acc = at("ada_acc", [P, 2, UNIT], F32, big_at + (2 * JT - 8) * SEQ * 4)

        ada0_raw = at("ada0_raw", [P, 2, UNIT], F32, raw_at)
        inb_re = at("inb_re", [P, PAIRS, P], F32, w_at)
        inb_im = at("inb_im", [P, PAIRS, P], F32, w_at + PAIRS * P * 4)
        rot_c = at("rot_c", [P, PAIRS, NB], F32, x_at)
        rot_s = at("rot_s", [P, PAIRS, NB], F32, x_at + PAIRS * NB * 4)
        lb_re = at("lb_re", [P, PAIRS, BL, CG], F32, h_at)
        lb_im = at("lb_im", [P, PAIRS, BL, CG], F32, h_at + PAIRS * BL * CG * 4)
        o = big_at
        u = at("u", [P, GROUPS, NB], F32, o); o += GROUPS * NB * 4
        cl_re = at("cl_re", [P, PAIRS, BL + 1, CG], F32, o); o += PAIRS * (BL + 1) * CG * 4
        cl_im = at("cl_im", [P, PAIRS, BL + 1, CG], F32, o); o += PAIRS * (BL + 1) * CG * 4
        toep, kpad, bd = [], None, []
        for i in range(2):
            toep.append(at(f"toep{i}", [P, 2 * PO, BL * CG], F32, o))
            if i == 0:
                bd = [at("bd_re", [P, PAIRS, 2 * CG], F32, o),
                      at("bd_im", [P, PAIRS, 2 * CG], F32, o + PAIRS * 2 * CG * 4)]
            else:
                kpad = at("kpad", [P, KT, (2 * BL - 1) * CG], F32, o)
            o += 2 * PO * BL * CG * 4
        pw_re = at("pw_re", [P, BL + 1, PAIRS], F32, o)
        pw_im = at("pw_im", [P, BL + 1, PAIRS], F32, o + (BL + 1) * PAIRS * 4)
        v_re = at("v_re", [P, PO * NB], F32, o); o += PO * NB * 4
        v_ni = at("v_ni", [P, PO * NB], F32, o); o += PO * NB * 4
        bc_par = at("bc_par", [P, 4, PAIRS, CG], F32, o)
        hx = []
        for i in range(2):
            hx.append(at(f"hx{i}", [P, 2, PO, NB + 1], F32, o)); o += 2 * PO * (NB + 1) * 4
        bb = at("bb", [P, 2, PAIRS, CG], F32, o)
        z = at("z", [P, BL, PO, CG], F32, o); o += BL * PO * CG * 4
        decay = at("decay", [P, PO, NB], F32, o); o += PO * NB * 4
        sel16 = at("sel16", [P, BL, CG], F32, o); o += P * 4
        blk16 = at("blk16", [P, KT, CG], F32, o); o += P * 4
        assert o <= big_at + 2 * JT * SEQ * 4

        o = big_at
        cosb = at("cosb", [P, SEQ], F32, o); o += SEQ * 4
        sinb = at("sinb", [P, SEQ], F32, o); o += SEQ * 4
        v_sb = at("v_sb", [P, QT, D], F32, o); o += QT * D * 4
        ohi = at("ohi", [P, HEADS, SEQ], F32R, o); o += HEADS * SEQ * 4
        olo = at("olo", [P, HEADS, SEQ], F32R, o); o += HEADS * SEQ * 4
        qk = at("qk", [P, 2, 2, SEQ], F32, o); o += 4 * SEQ * 4
        qk_sw = at("qk_sw", [P, 2, SEQ], F32, o); o += 2 * SEQ * 4
        prob = at("prob", [P, 2, 2, SEQ], F32, o); o += 4 * SEQ * 4
        att = at("att", [P, 2, SEQ], F32, o); o += 2 * SEQ * 4
        att_t = at("att_t", [P, 2, SEQ], F32, o); o += 2 * SEQ * 4
        pos_i = at("pos_i", [P, SEQ], I32, o); o += SEQ * 4
        lam_par = at("lam_par", [P, 4 * HD], F32, o); o += 4 * HD * 4
        maskw = at("maskw", [1, 2, P], F32, o); o += 2 * P * 4
        assert o <= big_at + 2 * JT * SEQ * 4

        ca = sb("ca", [P, 2, SEQ])
        cb = sb("cb", [P, 2, SEQ])
        sq = sb("sq", [P, 2, SEQ])
        ssum = sb("ssum", [P, SEQ])
        qk_raw, o_sb = ca, sq[:, 1, :]
        s5_at = place(2 * SEQ * 4)
        s5s = at("s5s", [P, 32, PAIRS], F32, s5_at)
        diag = at("diag", [P, QT, P], F32, s5_at)
        on = at("on", [P, QT, P], F32, s5_at + SEQ * 4)
        ident = sb("ident", [P, P])
        ones = sb("ones", [P, P])
        modt = sb("modt", [P, 2, 48])
        ada_b = sb("ada_b", [P, 2, 48])
        norm_g = sb("norm_g", [P, 2, 4, KT])
        pre_a = sb("pre_a", [P, 4, KT])
        gate = sb("gate", [P, 4, KT])
        convp = sb("convp", [P, 2, JT, 2, 4])
        cond = sb("cond", [P, 2, KT])
        dskip = sb("dskip", [P, KT])
        col = sb("col", [P, 8])
        nwt = sb("nwt", [P, 4, NB])
        stat = sb("stat", [P, 48])
        gmask = sb("gmask", [P, BL])
        sub_g = sb("sub_g", [P, 1])
        rope_c = sb("rope_c", [P, 2])
        assert base[0] <= nc.sbuf_usable_end, (base[0], nc.sbuf_usable_end)

        psum = ctx.enter_context(nc.psum_tensor("psum", [P, 8, 512], F32))
        krows = nc.dram_tensor("toeplitz_rows", [D, (2 * BL - 1) * CG], F32).ap()

        raw_landed = [sem("raw_landed0"), sem("raw_landed1")]
        split_hi, split_lo, unit_done = sem("split_hi"), sem("split_lo"), sem("unit_done")
        ada_landed = [sem("ada_landed0"), sem("ada_landed1")]
        ada_used, ada_added, acc_clear = sem("ada_used"), sem("ada_added"), sem("acc_clear")
        par_in, small_in, u_in, x_in, bc_in = (sem("par_in"), sem("small_in"), sem("u_in"),
                                               sem("x_in"), sem("bc_in"))
        pos_in, lam_in = sem("pos_in"), sem("lam_in")
        out_stored = sem("out_stored")
        dve_step, act_step, pool_step = sem("dve_step"), sem("act_step"), sem("pool_step")
        ident_ready, const_ready, cond_ready = (sem("ident_ready"), sem("const_ready"),
                                                sem("cond_ready"))
        tanh_ready, sine_arg, sine_ready = sem("tanh_ready"), sem("sine_arg"), sem("sine_ready")
        tanh_arg = sem("tanh_arg")
        pw_ready, bb_ready, bd_ready, cl_ready = (sem("pw_ready"), sem("bb_ready"),
                                                  sem("bd_ready"), sem("cl_ready"))
        lb_ready, rot_ready = sem("lb_ready"), sem("rot_ready")
        inb_psum, inb_ready = sem("inb_psum"), sem("inb_ready")
        k_psum, k_copied, k_ready, k_stored = (sem("k_psum"), sem("k_copied"), sem("k_ready"),
                                               sem("k_stored"))
        kzero = sem("kzero")
        toep_in = [sem("toep_in0"), sem("toep_in1")]
        usq_ready, usq_added, usum_ready, uvar_psum = (sem("usq_ready"), sem("usq_added"),
                                                       sem("usum_ready"), sem("uvar_psum"))
        mod_psum, mod_ready = sem("mod_psum"), sem("mod_ready")
        umod_rhs, umod_psum, u_ready = sem("umod_rhs"), sem("umod_psum"), sem("u_ready")
        in_psum, in_read, hx_ready = sem("in_psum"), sem("in_read"), sem("hx_ready")
        y5_psum, z_ready, zt_psum, zt_hi, zt_lo = (sem("y5_psum"), sem("z_ready"),
                                                   sem("zt_psum"), sem("zt_hi"), sem("zt_lo"))
        sig_ready, y_ready = sem("sig_ready"), sem("y_ready")
        sq_ready, sq_added, stat_psum, diag_ready, rs_psum = (
            sem("sq_ready"), sem("sq_added"), sem("stat_psum"), sem("diag_ready"), sem("rs_psum"))
        x_ready, t_ready, h_aff, h_hi, h_lo = (sem("x_ready"), sem("t_ready"), sem("h_aff"),
                                               sem("h_hi"), sem("h_lo"))
        tap2, conv_done, gelu_done, g_ready, g_hi, g_lo = (
            sem("tap2"), sem("conv_done"), sem("gelu_done"), sem("g_ready"), sem("g_hi"),
            sem("g_lo"))
        conv_step = sem("conv_step")
        v_copied = sem("v_copied")
        rope_arg, rope_sin, rope_table, lam_exp, lam_arg, lam_ready = (
            sem("rope_arg"), sem("rope_sin"), sem("rope_table"), sem("lam_exp"), sem("lam_arg"),
            sem("lam_ready"))
        raw_copied, swapped, sw_mul, cos_mul, qk_ready = (
            sem("raw_copied"), sem("swapped"), sem("sw_mul"), sem("cos_mul"), sem("qk_ready"))
        half_hi, half_lo, o_copied = sem("half_hi"), sem("half_lo"), sem("o_copied")
        s_psum, nmax_ready, exp_done, att_ready = (sem("s_psum"), sem("nmax_ready"),
                                                   sem("exp_done"), sem("att_ready"))
        mask_ready = sem("mask_ready")
        att_step, smax, hn_step = sem("att_step"), sem("smax"), sem("hn_step")
        rot_init, rot_first, rot_copy = sem("rot_init"), sem("rot_first"), sem("rot_copy")
        attt_psum, attt_copied, o_psum, osq_done = (sem("attt_psum"), sem("attt_copied"),
                                                    sem("o_psum"), sem("osq_done"))
        on_ready, ot_psum, ot_copied, ot_hi, ot_lo = (sem("on_ready"), sem("ot_psum"),
                                                      sem("ot_copied"), sem("ot_hi"),
                                                      sem("ot_lo"))

        def wait(eng, s, n):
            if isinstance(n, int) and n <= 0:
                return
            eng.wait_ge(s, n)

        def pairs(eng, lo, hi, body):
            with eng.Fori(0, (hi - lo) // 2) as i:
                for s in range(2):
                    body(2 * i + (lo + s), s, i + lo // 2)

        def y_of(r):
            return y_glu if r == 0 else y_late

        def shift_col(r):
            layer, ffn = (r + 1) // 2, (r + 1) % 2
            return layer, 24 * ffn

        block = ctx.enter_context(nc.Block())

        @block.sync
        def _(sp):
            sp.dma_start(s5s[:, 0:3, :], a["s5_par"]).then_inc(par_in, 16)
            sp.dma_start(bc_par[:], a["s5_bc"]).then_inc(bc_in, 16)
            sp.dma_start(u[:], a["x_blocks"].rearrange("p (g b) -> p g b", g=GROUPS)).then_inc(u_in, 16)

            def load_ada0(n):
                wait(sp, ada_used, n - 1)
                sp.dma_start(ada0_raw[:, n % 2, :], a["ada_w"][n]).then_inc(ada_landed[n % 2], 16)

            for n in range(N_ADA_PE):
                load_ada0(n)
            sp.wait_ge(k_ready, 1)
            sp.dma_start(krows.rearrange("(t p) k -> p t k", p=P), kpad[:]).then_inc(k_stored, 16)
            sp.wait_ge(k_stored, 16)

            def load_toeplitz(piece):
                wait(sp, y5_psum, piece - 1)
                for s in range(BL):
                    src = krows[2 * PO * CG * piece:2 * PO * CG * (piece + 1), CG * s:CG * s + BL * CG]
                    sp.dma_start(toep[piece % 2][CG * s:CG * (s + 1), :, :],
                                 src.rearrange("(g c) k -> c g k", c=CG)).then_inc(toep_in[piece % 2], 16)

            load_toeplitz(0)
            load_toeplitz(1)
            sp.wait_ge(ada_used, N_ADA_PE)
            for n in range(2):
                sp.dma_start(raw[:, n, :], a["units"][n]).then_inc(raw_landed[n], 16)
            for piece in range(2, OCTS):
                load_toeplitz(piece)
            sp.wait_ge(hx_ready, OCTS)
            sp.dma_start(x[:], a["x_t"].rearrange("(t p) s -> p t s", p=P)).then_inc(x_in, 16)

            def load_unit(n, s, half):
                sp.wait_ge(split_lo, n - 1)
                sp.dma_start(raw[:, s, :], a["units"][n]).then_inc(raw_landed[s], 16)

            def load_ada(m, s):
                wait(sp, ada_added, m - 1)
                sp.dma_start(ada_ring[:, s, :], a["ada_w"][m + N_ADA_PE]).then_inc(ada_landed[s], 16)

            sp.wait_ge(y5_psum, OCTS)
            load_ada(0, 0)
            load_ada(1, 1)
            load_unit(2, 0, None)
            load_unit(3, 1, None)

            def load_both(i, s, half):
                load_unit(i + 4, s, half)
                for e in range(2):
                    load_ada(2 * i + (2 + e), e)

            pairs(sp, 0, N_GLU + 10, load_both)
            load_both(N_GLU + 10, 0, None)
            load_unit(N_GLU + 15, 1, None)
            pairs(sp, N_GLU + 16, U_V + 2, load_unit)
            sp.wait_ge(unit_done, U_V)
            sp.dma_start(pos_i[:], a["positions"].partition_broadcast(P)).then_inc(pos_in, 16)
            sp.dma_start(lam_par[:], a["lam_par"].partition_broadcast(P)).then_inc(lam_in, 16)
            pairs(sp, U_V + 2, U_QK + 4, load_unit)

            def swap(h, s, half):
                sp.wait_ge(raw_copied, 2 * h + 2)
                if not isinstance(h, int) or h >= 1:
                    sp.wait_ge(qk_ready, 2 * h)
                for q in range(4):
                    sp.dma_start(qk_sw[32 * (q ^ 1):32 * (q ^ 1) + 32, :, :],
                                 qk_raw[32 * q:32 * q + 32, :, :]).then_inc(swapped, 16)
                load_unit(h + (U_QK + 4), s, None)

            swap(0, 0, None)
            swap(1, 1, None)
            pairs(sp, 2, HEADS, swap)
            pairs(sp, U_WO + 4, N_UNITS, load_unit)
            for f in range(KT):
                sp.wait_ge(x_ready, 3 * KT + f + 1)
                sp.dma_start(out_t[P * f:P * (f + 1), :], x[:, f, :]).then_inc(out_stored, 16)
            sp.wait_ge(out_stored, 16 * KT)

        @block.gpsimd
        def _(pool):
            steps = [0]

            def link(ins):
                steps[0] += 1
                ins.then_inc(pool_step, 1)
                pool.wait_ge(pool_step, steps[0])

            link(nc.gpsimd.memset(ident[:], 0.0))
            nc.gpsimd.affine_select(out=ident[:], in_=ident[:], compare_op=ALU.not_equal, fill=1.0,
                                    base=0, pattern=[[-1, P]], channel_multiplier=1).then_inc(ident_ready, 1)
            nc.gpsimd.memset(ones[:], 1.0).then_inc(const_ready, 1)
            nc.gpsimd.memset(col[:, 0:1], 1.0 / D).then_inc(const_ready, 1)
            nc.gpsimd.memset(rot_c[:, :, 0], 1.0).then_inc(rot_init, 1)
            nc.gpsimd.memset(rot_s[:, :, 0], 0.0).then_inc(rot_init, 1)

            for q in range(8):
                pool.wait_ge(usq_ready, q + 1)
                if q == 0:
                    nc.gpsimd.tensor_copy(ssum[:], sq[:, 0, :]).then_inc(usq_added, 1)
                else:
                    pool.wait_ge(usq_added, q)
                    nc.gpsimd.tensor_tensor(ssum[:], ssum[:], sq[:, q % 2, :], ALU.add).then_inc(usq_added, 1)

            pool.wait_ge(pw_ready, 1)
            pool.wait_ge(bb_ready, 1)
            ta = cb[:, 0, :].rearrange("p (g c) -> p g c", c=CG)
            tb = cb[:, 1, :].rearrange("p (g c) -> p g c", c=CG)

            def over_c(v):
                return v.unsqueeze(2).broadcast_to([P, PAIRS, CG])

            for s in range(BL):
                pr, pi = over_c(pw_re[:, s, :]), over_c(pw_im[:, s, :])
                nc.gpsimd.tensor_tensor(lb_re[:, :, s, :], pr, bb[:, 0], ALU.mult).then_inc(pool_step, 1)
                nc.gpsimd.tensor_tensor(ta, pi, bb[:, 1], ALU.mult).then_inc(pool_step, 1)
                nc.gpsimd.tensor_tensor(lb_im[:, :, s, :], pr, bb[:, 1], ALU.mult).then_inc(pool_step, 1)
                steps[0] += 3
                link(nc.gpsimd.tensor_tensor(tb, pi, bb[:, 0], ALU.mult))
                nc.gpsimd.tensor_tensor(lb_re[:, :, s, :], lb_re[:, :, s, :], ta, ALU.subtract).then_inc(lb_ready, 1)
                nc.gpsimd.tensor_tensor(lb_im[:, :, s, :], lb_im[:, :, s, :], tb, ALU.add).then_inc(lb_ready, 1)
                pool.wait_ge(lb_ready, 2 * s + 2)

            pool.wait_ge(rot_first, 1)
            pool.wait_ge(rot_init, 2)
            m = 1
            while m < NB:
                n = min(m, NB - 1 - m)
                t = cb[:, :, :].rearrange("p a s -> p (a s)")[:, 0:PAIRS * n].rearrange("p (g b) -> p g b", b=n)
                em_c = rot_c[:, :, m:m + 1].broadcast_to([P, PAIRS, n])
                em_s = rot_s[:, :, m:m + 1].broadcast_to([P, PAIRS, n])
                oc, os = rot_c[:, :, m + 1:m + 1 + n], rot_s[:, :, m + 1:m + 1 + n]
                ic, is_ = rot_c[:, :, 1:1 + n], rot_s[:, :, 1:1 + n]
                if n > 0:
                    link(nc.gpsimd.tensor_tensor(oc, ic, em_c, ALU.mult))
                    link(nc.gpsimd.tensor_tensor(t, is_, em_s, ALU.mult))
                    link(nc.gpsimd.tensor_tensor(oc, oc, t, ALU.subtract))
                    link(nc.gpsimd.tensor_tensor(os, ic, em_s, ALU.mult))
                    link(nc.gpsimd.tensor_tensor(t, is_, em_c, ALU.mult))
                    link(nc.gpsimd.tensor_tensor(os, os, t, ALU.add))
                m *= 2
            nc.gpsimd.memset(col[:, 7:8], 0.0).then_inc(rot_ready, 1)

            def add_squares(stat_):
                for f in range(KT):
                    q = KT * stat_ + f
                    pool.wait_ge(sq_ready, q + 1)
                    if f == 0:
                        wait(pool, stat_psum, stat_)
                        nc.gpsimd.tensor_copy(ssum[:], sq[:, q % 2, :]).then_inc(sq_added, 1)
                    else:
                        pool.wait_ge(sq_added, q)
                        nc.gpsimd.tensor_tensor(ssum[:], ssum[:], sq[:, q % 2, :], ALU.add).then_inc(sq_added, 1)

            def h_low(k):
                for f in range(KT):
                    pool.wait_ge(h_hi, KT * k + f + 1)
                    nc.gpsimd.tensor_tensor(hlo[:, f, :], cb[:, f % 2, :], hhi[:, f, :].bitcast(F32),
                                            ALU.subtract).then_inc(h_lo, 1)

            def ffn_low(layer, lo=0, hi=JT):
                def body(j, s, half):
                    pool.wait_ge(g_hi, j + (layer * JT + 1))
                    nc.gpsimd.tensor_tensor(glo[:, j, :], ca[:, s, :], ghi[:, j, :].bitcast(F32),
                                            ALU.subtract).then_inc(g_lo, 1)
                pairs(pool, lo, hi, body)

            pool.wait_ge(zt_psum, OCTS)
            for i in range(2):
                nc.gpsimd.memset(ada_acc[:, i, :], 0.0).then_inc(acc_clear, 1)
            add_squares(0)
            pool.wait_ge(mod_psum, 2)
            for i in range(2):
                nc.gpsimd.memset(ada_acc[:, i, :], 0.0).then_inc(acc_clear, 1)
            add_squares(1)
            h_low(0)
            ffn_low(0, 0, 6)
            pool.wait_ge(mod_psum, 3)
            nc.gpsimd.memset(ada_acc[:, 0, :], 0.0).then_inc(acc_clear, 1)
            ffn_low(0, 6, JT)
            add_squares(2)
            add_squares(3)
            h_low(1)
            nc.gpsimd.memset(maskw[0:1, 0, 0:HD], MASKED).then_inc(mask_ready, 1)
            nc.gpsimd.memset(maskw[0:1, 0, HD:P], 0.0).then_inc(mask_ready, 1)
            nc.gpsimd.memset(maskw[0:1, 1, :], 1.0).then_inc(mask_ready, 1)

            def rope(h, s):
                for i in range(2):
                    pool.wait_ge(raw_copied, 2 * h + (i + 1))
                    if not isinstance(h, int) or h >= 2:
                        pool.wait_ge(s_psum, 4 * h - 4)
                    nc.gpsimd.tensor_tensor(qk[:, s, i, :], qk_raw[:, i, :], cosb[:], ALU.mult).then_inc(cos_mul, 1)
                pool.wait_ge(swapped, 64 * h + 64)
                for i in range(2):
                    nc.gpsimd.tensor_tensor(qk_sw[:, i, :], qk_sw[:, i, :], sinb[:], ALU.mult).then_inc(sw_mul, 1)
                for i in range(2):
                    pool.wait_ge(sw_mul, 2 * h + (i + 1))
                    pool.wait_ge(cos_mul, 2 * h + (i + 1))
                    nc.gpsimd.tensor_tensor(qk[:, s, i, :], qk[:, s, i, :], qk_sw[:, i, :], ALU.add).then_inc(qk_ready, 1)

            def o_low(h, s):
                pool.wait_ge(ot_hi, h + 1)
                nc.gpsimd.tensor_tensor(olo[:, h, :], cb[:, s, :], ohi[:, h, :].bitcast(F32),
                                        ALU.subtract).then_inc(ot_lo, 1)

            pool.sem_inc(ot_lo, 2)
            pool.wait_ge(rope_table, 1)
            for h in range(3):
                rope(h, h % 2)

            def head(h, s, half):
                o_low(h - 4, s)
                rope(h - 1, 1 - s)

            pairs(pool, 4, HEADS, head)
            o_low(HEADS - 4, 0)
            rope(HEADS - 1, 1)
            for h in range(HEADS - 3, HEADS):
                o_low(h, h % 2)
            add_squares(4)
            add_squares(5)
            h_low(2)
            ffn_low(1)
            add_squares(6)

        @block.scalar
        def _(act):
            A = nc.scalar.activation
            for i, (dst, name) in enumerate(((cond[:, 0, :], "c_cols"), (ada_b[:], "ada_b"),
                                             (norm_g[:], "norm_g"), (dskip[:], "d_cols"),
                                             (convp[:], "conv_par"), (sub_g[:], "sub_g"),
                                             (rope_c[:], "rope_c"))):
                act.dma_start(dst, a[name]).then_inc(small_in, 16)
            act.wait_ge(par_in, 16)
            A(s5s[:, 3, :], s5s[:, 2, :], ACT.Tanh, scale=1.0 / 16).then_inc(tanh_ready, 1)
            act.wait_ge(small_in, 16 * 7)
            A(cond[:, 1, :], cond[:, 0, :], ACT.Silu).then_inc(cond_ready, 1)
            act.wait_ge(u_in, 16)
            uf = u[:, :, :].rearrange("p g b -> p (g b)")
            for q in range(8):
                wait(act, usq_added, q - 1)
                A(sq[:, q % 2, :], uf[:, SEQ * q:SEQ * (q + 1)], ACT.Square).then_inc(usq_ready, 1)
            act.wait_ge(tanh_arg, 1)
            A(s5s[:, 8, :], s5s[:, 6, :], ACT.Tanh, scale=0.5).then_inc(tanh_ready, 1)
            act.wait_ge(sine_arg, 1)
            A(s5s[:, 13:17, :], s5s[:, 9:13, :], ACT.Sin).then_inc(sine_ready, 1)
            act.wait_ge(k_psum, 1)
            act.wait_ge(kzero, 1)
            for b in range(2):
                A(kpad[:, 4 * b:4 * b + 4, (BL - 1) * CG:],
                  psum[:, 4 + b, :].rearrange("p (t k) -> p t k", t=4), ACT.Copy).then_inc(k_copied, 1)
            for t in range(16):
                act.wait_ge(inb_psum, t + 1)
                dst = (inb_re if t < 8 else inb_im)[:, 4 * (t % 8):4 * (t % 8) + 4, :]
                A(dst, psum[:, 2 + t % 2, :].rearrange("p (g k) -> p g k", g=4), ACT.Copy).then_inc(inb_ready, 1)

            def split_high(n, s, half):
                act.wait_ge(raw_landed[s], 16 * half + 16)
                if not isinstance(n, int) or n >= 2:
                    act.wait_ge(unit_done, n - 1)
                A(whi[:, s, :], raw[:, s, :], ACT.Copy).then_inc(split_hi, 1)

            def z_steps(piece):
                act.wait_ge(y5_psum, piece + 1)
                wait(act, zt_psum, piece)
                for b in range(2):
                    A(z[:, :, 4 * b:4 * b + 4, :].rearrange("p t g c -> p g t c"),
                      psum[:, 4 + b, :].rearrange("p (g t c) -> p g t c", g=4, t=BL),
                      ACT.Gelu_apprx_tanh).then_inc(z_ready, 1)

            def zt_steps(piece):
                for b in range(2):
                    act.wait_ge(zt_psum, piece + 1)
                    for g2 in range(2):
                        dst = hhi[:, 2 * piece + g2, :].rearrange("p (b t) -> p t b", t=BL)
                        src = psum[:, 2 + b, :].rearrange("p (t g b) -> p g t b", t=4, g=2)
                        ins = A(dst[:, 4 * b:4 * b + 4, :], src[:, g2], ACT.Copy)
                    ins.then_inc(zt_hi, 1)

            for piece in range(OCTS):
                z_steps(piece)
                zt_steps(piece)
            act.wait_ge(in_psum, OCTS)
            for n in range(2):
                split_high(n, n, 0)

            def square(q, src):
                wait(act, sq_added, q - 1)
                A(sq[:, q % 2, :], src, ACT.Square).then_inc(sq_ready, 1)

            def glu(i, s, half):
                act.wait_ge(unit_done, i + 1)
                if not isinstance(i, int) or i >= 2:
                    act.wait_ge(y_ready, i - 1)
                A(ca[:, s, :], psum[:, 2 * s + 1, :], ACT.Sigmoid).then_inc(sig_ready, 1)
                split_high(i + 2, s, half + 1)
                act.wait_ge(y_ready, i + 1)
                if not isinstance(i, int) or i >= 2:
                    act.wait_ge(sq_added, i - 1)
                A(sq[:, s, :], y_glu[:, i, :], ACT.Square).then_inc(sq_ready, 1)

            glu(0, 0, 0)
            glu(1, 1, 0)
            pairs(act, 2, N_GLU, glu)

            def next_input(r):
                k = r
                for f in range(KT):
                    act.wait_ge(x_ready, KT * r + f + 1)
                    square(KT * (2 * r + 1) + f, x[:, f, :])
                layer, c0 = shift_col(r)
                for f in range(KT):
                    n = KT * k + f
                    act.wait_ge(t_ready, n + 1)
                    wait(act, h_lo, n - 1)
                    A(cb[:, f % 2, :], ca[:, f % 2, :], ACT.Identity, scale=pre_a[:, r + 1, f:f + 1],
                      bias=modt[:, layer, c0 + f:c0 + f + 1]).then_inc(h_aff, 1)
                    act.wait_ge(h_aff, n + 1)
                    A(hhi[:, f, :], cb[:, f % 2, :], ACT.Copy).then_inc(h_hi, 1)

            def ffn(layer):
                n0, g0 = U_FIN[layer], layer * JT

                def body(j, s, half):
                    act.wait_ge(unit_done, j + (n0 + 1))
                    if not isinstance(j, int) or j >= 2:
                        act.wait_ge(g_lo, j + (g0 - 1))
                    for i, dst in enumerate((ca, cb)):
                        A(dst[:, s, :], psum[:, 2 * s + i, :], ACT.Identity,
                          scale=convp[:, layer, j, i, 2:3], bias=convp[:, layer, j, i, 3:4]).then_inc(tap2, 1)
                    split_high(j + (n0 + 2), s, half + n0 // 2 + 1)
                    act.wait_ge(conv_done, 2 * j + (2 * g0 + 1))
                    A(ca[:, s, :], ca[:, s, :], ACT.Gelu_apprx_tanh).then_inc(gelu_done, 1)
                    act.wait_ge(g_ready, j + (g0 + 1))
                    A(ghi[:, j, :], ca[:, s, :], ACT.Copy).then_inc(g_hi, 1)

                body(0, 0, 0)
                body(1, 1, 0)
                pairs(act, 2, JT, body)
                r, m0 = 2 * layer + 1, U_FOUT[layer]
                for hf in range(2):
                    last = min(m0 + 6 * hf + 8, N_UNITS)
                    pairs(act, m0 + 6 * hf + 2, last, split_high)
                    for f in range(4):
                        act.wait_ge(y_ready, KT * r + 4 * hf + f + 1)
                        square(KT * 2 * r + 4 * hf + f, y_late[:, 4 * hf + f, :])

            next_input(0)
            ffn(0)
            next_input(1)

            n = U_V
            split_high(n + 2, 0, (n + 2) // 2)
            act.wait_ge(rope_arg, 1)
            A(sinb[:], sinb[:], ACT.Sin).then_inc(rope_sin, 1)
            A(cosb[:], cosb[:], ACT.Sin).then_inc(rope_sin, 1)
            act.wait_ge(lam_arg, 1)
            A(col[:, 3:5], col[:, 1:3], ACT.Exp).then_inc(lam_exp, 1)
            for m in range(1, N_V):
                split_high(n + m + 2, m % 2, (n + m + 2) // 2)

            def copy_projections(h, s):
                act.wait_ge(unit_done, h + (U_QK + 1))
                if not isinstance(h, int) or h >= 1:
                    act.wait_ge(cos_mul, 2 * h)
                    act.wait_ge(swapped, 64 * h)
                for i in range(2):
                    A(qk_raw[:, i, :], psum[:, 2 * s + i, :], ACT.Copy,
                      scale=HD ** -0.5 if i == 0 else 1.0).then_inc(raw_copied, 1)

            def half_high(h, s, half, part):
                n = h + (U_QK + 1)
                act.wait_ge(raw_landed[1 - s], 16 * (half + (U_QK // 2 + 1) + s))
                act.wait_ge(unit_done, n - 1)
                c = slice(part * UNIT // 2, (part + 1) * UNIT // 2)
                ins = A(whi[:, 1 - s, c], raw[:, 1 - s, c], ACT.Copy)
                ins.then_inc(split_hi if part else half_hi, 1)

            def out_copy(h, s):
                act.wait_ge(ot_psum, h + 1)
                act.wait_ge(ot_lo, h + 1)
                A(cb[:, s, :], psum[:, 6, :], ACT.Copy, scale=sub_g[:, 0:1]).then_inc(ot_copied, 1)

            def out_high(h, s):
                act.wait_ge(ot_copied, h + 1)
                A(ohi[:, h, :], cb[:, s, :], ACT.Copy).then_inc(ot_hi, 1)

            def exps(h, qt):
                pb, width = qt % 2, (qt + 1) * P
                act.wait_ge(nmax_ready, 4 * h + (qt + 1))
                if not isinstance(h, int) or 4 * h + qt >= 2:
                    act.wait_ge(att_ready, 4 * h + (qt - 1))
                for c in range(2):
                    ins = A(prob[:, pb, c, 0:width], psum[:, 4 + c, 0:width], ACT.Exp,
                            bias=stat[:, 8 * pb + 2 + c:8 * pb + 3 + c],
                            accum_out=stat[:, 8 * pb + 4 + c:8 * pb + 5 + c])
                    ins.then_inc(exp_done, 1)

            def turned(h, qt):
                pb, width = qt % 2, (qt + 1) * P
                act.wait_ge(attt_psum, 4 * h + (qt + 1))
                if not isinstance(h, int) or 4 * h + qt >= 2:
                    act.wait_ge(o_psum, 4 * h + (qt - 1))
                A(att_t[:, pb, 0:width], psum[:, 6, 0:width], ACT.Copy).then_inc(attt_copied, 1)

            def copy_output(h):
                act.wait_ge(o_psum, 4 * h + 4)
                if not isinstance(h, int) or h >= 1:
                    act.wait_ge(on_ready, h)
                A(sq[:, 0, :], psum[:, 7, :], ACT.Square).then_inc(osq_done, 1)
                A(o_sb, psum[:, 7, :], ACT.Copy).then_inc(o_copied, 1)

            def head(h, s, half, first=False, older=True, gemm_on=True, split=True):
                a_ = h - 2
                if older:
                    out_copy(a_ - 2, s)
                exps(a_, 0)
                if not first:
                    turned(a_ - 1, 3)
                if gemm_on:
                    copy_projections(h - 1, 1 - s)
                if older:
                    out_high(a_ - 2, s)
                if not first:
                    copy_output(a_ - 1)
                exps(a_, 1)
                turned(a_, 0)
                if split:
                    half_high(h, s, half, 0)
                exps(a_, 2)
                turned(a_, 1)
                if split:
                    half_high(h, s, half, 1)
                exps(a_, 3)
                turned(a_, 2)

            act.wait_ge(lam_ready, 1)
            copy_projections(0, 0)
            half_high(1, 1, 0, 0)
            half_high(1, 1, 0, 1)
            head(2, 0, 1, first=True, older=False)
            head(3, 1, 1, older=False)
            pairs(act, 4, HEADS, head)
            head(HEADS, 0, HEADS // 2)
            head(HEADS + 1, 1, None, gemm_on=False, split=False)
            out_copy(HEADS - 2, 0)
            turned(HEADS - 1, 3)
            out_high(HEADS - 2, 0)
            copy_output(HEADS - 1)
            out_copy(HEADS - 1, 1)
            out_high(HEADS - 1, 1)
            for m in range(N_WO):
                n = U_WO + m
                for i in range(2):
                    act.wait_ge(y_ready, KT * 2 + 2 * m + i + 1)
                    square(KT * 4 + 2 * m + i, y_late[:, 2 * m + i, :])
                split_high(n + 2, m % 2, (n + 2) // 2)
            next_input(2)
            ffn(1)

        @block.vector
        def _(dve):
            steps = [0]
            TT, TS, STT = nc.vector.tensor_tensor, nc.vector.tensor_scalar, nc.vector.scalar_tensor_tensor

            def count(ins):
                steps[0] += 1
                return ins.then_inc(dve_step, 1)

            def here():
                dve.wait_ge(dve_step, steps[0])

            def link(ins):
                count(ins)
                here()

            def signal(s):
                here()
                dve.sem_inc(s, 1)

            def rsqrt(dst, src, scale, lk):
                w = dst.shape[1]
                v, t = nwt[:, 0, 0:w], nwt[:, 1, 0:w]
                lk(TS(v, src, scale, EPS, ALU.mult, ALU.add))
                lk(TS(t.bitcast(I32), v.bitcast(I32), 1, None, ALU.logical_shift_right))
                lk(TS(dst.bitcast(I32), t.bitcast(I32), -1.0, RSQRT_MAGIC, ALU.mult, ALU.add))
                for i in range(3):
                    lk(TT(t, dst, dst, ALU.mult))
                    lk(STT(t, t, -0.5, v, ALU.mult, ALU.mult))
                    lk(STT(dst, t, 1.5, dst, ALU.add, ALU.mult))

            def reduced(dst_sin, dst_cos, ang, t, lk):
                lk(TS(t, ang, 1.0 / TWO_PI, ROUND, ALU.mult, ALU.add))
                lk(TS(t, t, -ROUND, None, ALU.add))
                lk(STT(dst_sin, t, -PI_A, ang, ALU.mult, ALU.add))
                lk(STT(dst_sin, t, -PI_B, dst_sin, ALU.mult, ALU.add))
                lk(STT(dst_sin, t, -PI_C, dst_sin, ALU.mult, ALU.add))
                lk(TS(dst_sin, dst_sin, PI_CLAMP, -PI_CLAMP, ALU.min, ALU.max))
                lk(STT(dst_cos, dst_sin, -1.0, dst_sin, ALU.mult, ALU.max))
                lk(TS(dst_cos, dst_cos, -1.0, math.pi / 2, ALU.mult, ALU.add))

            dve.wait_ge(ident_ready, 1)
            link(nc.vector.tensor_reduce(sel16[:, 0, :], ident[:].rearrange("p (b c) -> p c b", c=CG), AXX, ALU.add))
            link(nc.vector.tensor_copy(sel16[:, 1:, :], sel16[:, 0:1, :].broadcast_to([P, BL - 1, CG])))
            link(nc.vector.tensor_reduce(gmask[:], ident[:].rearrange("p (b c) -> p b c", c=CG), AXX, ALU.add))
            count(TS(blk16[:], gmask[:].unsqueeze(2).broadcast_to([P, KT, CG]), 1.0 / D, None, ALU.mult))
            count(nc.vector.memset(bd[0][:], 0.0))
            count(nc.vector.memset(bd[1][:], 0.0))
            nc.vector.memset(kpad[:, :, 0:(BL - 1) * CG], 0.0).then_inc(kzero, 1)

            S = [s5s[:, i, :] for i in range(32)]
            a_re, a_im = S[0], S[1]
            dt, lam_re, dre, dim_ = S[4], S[5], S[6], S[7]
            t0, t1, t2, t3 = S[28], S[29], S[30], S[31]

            def exp_from_tanh(dst, t):
                link(TS(t0, t, -1.0, 1.0, ALU.mult, ALU.add))
                link(nc.vector.reciprocal(t1, t0))
                link(TS(t0, t, 1.0, None, ALU.add))
                link(TT(dst, t0, t1, ALU.mult))

            dve.wait_ge(tanh_ready, 1)
            exp_from_tanh(dt, S[3])
            for i in range(3):
                link(TT(dt, dt, dt, ALU.mult))
            link(TS(lam_re, a_re, LAM_MAX, None, ALU.min))
            TT(dre, lam_re, dt, ALU.mult).then_inc(tanh_arg, 1)
            link(TT(dim_, a_im, dt, ALU.mult))
            link(TS(S[27], dim_, float(BL), None, ALU.mult))
            reduced(S[9], S[10], dim_, t0, link)
            reduced(S[11], S[12], S[27], t0, link)
            signal(sine_arg)
            dve.wait_ge(tanh_ready, 2)
            mag = S[17]
            exp_from_tanh(mag, S[8])
            link(TT(S[18], mag, mag, ALU.mult))
            link(TT(S[18], S[18], S[18], ALU.mult))
            link(TT(S[18], S[18], S[18], ALU.mult))
            dve.wait_ge(sine_ready, 1)
            count(nc.vector.memset(pw_re[:, 0, :], 1.0))
            count(nc.vector.memset(pw_im[:, 0, :], 0.0))
            count(TT(pw_re[:, 1, :], mag, S[14], ALU.mult))
            link(TT(pw_im[:, 1, :], mag, S[13], ALU.mult))
            dve.wait_ge(rot_init, 2)
            nc.vector.tensor_copy(rot_s[:, :, 1], S[15]).then_inc(rot_copy, 1)
            dve.wait_ge(rot_copy, 1)
            nc.vector.tensor_copy(rot_c[:, :, 1], S[16]).then_inc(rot_first, 1)
            for m in (1, 2, 4):
                def over(v):
                    return v.broadcast_to([P, m, PAIRS])
                qr, qi = over(pw_re[:, m:m + 1, :]), over(pw_im[:, m:m + 1, :])
                pr, pi = pw_re[:, 1:1 + m, :], pw_im[:, 1:1 + m, :]
                nr, ni = pw_re[:, m + 1:2 * m + 1, :], pw_im[:, m + 1:2 * m + 1, :]
                ta, tb = s5s[:, 20:20 + m, :], s5s[:, 24:24 + m, :]
                count(TT(nr, pr, qr, ALU.mult))
                count(TT(ta, pi, qi, ALU.mult))
                count(TT(ni, pr, qi, ALU.mult))
                link(TT(tb, pi, qr, ALU.mult))
                count(TT(nr, nr, ta, ALU.subtract))
                link(TT(ni, ni, tb, ALU.add))
            f_re, f_im = S[20], S[21]
            count(TT(t0, lam_re, lam_re, ALU.mult))
            link(TT(t1, a_im, a_im, ALU.mult))
            link(TT(t0, t0, t1, ALU.add))
            link(nc.vector.reciprocal(t0, t0))
            link(TS(t1, pw_re[:, 1, :], -1.0, None, ALU.add))
            count(TT(f_re, t1, lam_re, ALU.mult))
            link(TT(t2, pw_im[:, 1, :], a_im, ALU.mult))
            link(TT(f_re, f_re, t2, ALU.add))
            count(TT(f_re, f_re, t0, ALU.mult))
            count(TT(f_im, pw_im[:, 1, :], lam_re, ALU.mult))
            link(TT(t2, t1, a_im, ALU.mult))
            link(TT(f_im, f_im, t2, ALU.subtract))
            link(TT(f_im, f_im, t0, ALU.mult))
            signal(pw_ready)

            def over_c(v):
                return v.unsqueeze(2).broadcast_to([P, PAIRS, CG])

            ta = ca[:, 0, :].rearrange("p (g c) -> p g c", c=CG)
            tb = ca[:, 1, :].rearrange("p (g c) -> p g c", c=CG)

            def complex_rows(dr, di, pr, pi, vr, vi, done=None):
                count(TT(dr, pr, vr, ALU.mult))
                count(TT(ta, pi, vi, ALU.mult))
                count(TT(di, pr, vi, ALU.mult))
                link(TT(tb, pi, vr, ALU.mult))
                count(TT(dr, dr, ta, ALU.subtract))
                link(TT(di, di, tb, ALU.add))

            dve.wait_ge(bc_in, 16)
            complex_rows(bb[:, 0], bb[:, 1], over_c(f_re), over_c(f_im), bc_par[:, 0], bc_par[:, 1])
            for g2 in range(2):
                rows = slice(64 * g2, 64 * g2 + 64)
                cols = slice(CG * g2, CG * g2 + CG)
                nc.vector.tensor_copy(bd[0][rows, :, cols], bb[rows, 0]).then_inc(bd_ready, 1)
                TS(bd[1][rows, :, cols], bb[rows, 1], -1.0, None, ALU.mult).then_inc(bd_ready, 1)
            dve.wait_ge(bd_ready, 4)
            signal(bb_ready)
            dve.wait_ge(usq_added, 8)
            us = nwt[:, 2, :]
            nc.vector.tensor_reduce(us, ssum[:].rearrange("p (g b) -> p b g", g=8), AXX, ALU.add).then_inc(usum_ready, 1)
            dve.wait_ge(uvar_psum, 1)
            urs = nwt[:, 3, :]
            rsqrt(urs, psum[:, 6, 0:NB], 1.0, link)
            G = 2 * PO
            for piece in range(OCTS):
                g = slice(G * piece, G * piece + G)
                count(TT(u[:, g, :], u[:, g, :], urs.unsqueeze(1).broadcast_to([P, G, NB]), ALU.mult))

            for k in range(BL + 1):
                complex_rows(cl_re[:, :, k, :], cl_im[:, :, k, :], over_c(pw_re[:, k, :]),
                             over_c(pw_im[:, k, :]), bc_par[:, 2], bc_par[:, 3])
                if k == BL - 1:
                    signal(cl_ready)
            dve.wait_ge(k_copied, 2)
            dve.wait_ge(small_in, 16 * 7)
            tk = ca[:, 0, 0:KT * CG].rearrange("p (t c) -> p t c", c=CG)
            link(TT(tk, sel16[:, 0:1, :].broadcast_to([P, KT, CG]),
                    dskip[:].unsqueeze(2).broadcast_to([P, KT, CG]), ALU.mult))
            k0 = kpad[:, :, (BL - 1) * CG:BL * CG]
            TT(k0, k0, tk, ALU.add).then_inc(k_ready, 1)

            def modulation(layer, chunks):
                for ch in chunks:
                    c = slice(KT * ch, KT * ch + KT)
                    link(TT(modt[:, layer, c], psum[:, 7, 48 * layer + KT * ch:48 * layer + KT * ch + KT],
                            ada_b[:, layer, c], ALU.add))
                for ch in chunks:
                    sub, kind = ch // 3, ch % 3
                    c = slice(KT * ch, KT * ch + KT)
                    if kind == 1:
                        link(STT(pre_a[:, 2 * layer + sub, :], modt[:, layer, c], 1.0,
                                 norm_g[:, layer, 2 * sub, :], ALU.add, ALU.mult))
                    if kind == 2:
                        link(TT(gate[:, 2 * layer + sub, :], modt[:, layer, c],
                                norm_g[:, layer, 2 * sub + 1, :], ALU.mult))

            dve.wait_ge(ada_used, N_ADA_PE)
            modulation(0, (0, 1))
            um = ca[:, 0, 0:2 * GROUPS].rearrange("p (a t g) -> p a t g", a=2, t=KT)
            for i, v in enumerate((pre_a[:, 0, :], modt[:, 0, 0:KT])):
                TT(um[:, i], v.unsqueeze(2).broadcast_to([P, KT, BL]),
                   gmask[:].unsqueeze(1).broadcast_to([P, KT, BL]), ALU.mult).then_inc(umod_rhs, 1)
            dve.wait_ge(umod_psum, 1)
            here()
            for piece in range(OCTS):
                g = slice(G * piece, G * piece + G)
                for i, op in enumerate((ALU.mult, ALU.add)):
                    c0 = NB + GROUPS * i + G * piece
                    ins = TT(u[:, g, :], u[:, g, :],
                             psum[:, 6, c0:c0 + G].unsqueeze(2).broadcast_to([P, G, NB]), op)
                    if i == 0:
                        link(ins)
                    else:
                        ins.then_inc(u_ready, 1)

            for i in range(2):
                count(nc.vector.memset(hx[i][:, :, :, 0], 0.0))
            dve.wait_ge(rot_ready, 1)
            W = PO * NB

            def flat(v):
                return v.rearrange("p g b -> p (g b)")

            def split_low(n, s, half):
                dve.wait_ge(split_hi, n + 1)
                TT(wlo[:, s, :], raw[:, s, :], whi[:, s, :].bitcast(F32), ALU.subtract).then_inc(split_lo, 1)

            def zt_low(piece):
                for b in range(2):
                    dve.wait_ge(zt_hi, 2 * piece + b + 1)
                    for g2 in range(2):
                        src = psum[:, 2 + b, :].rearrange("p (t g b) -> p g t b", t=4, g=2)[:, g2]
                        dst = hlo[:, 2 * piece + g2, :].rearrange("p (b t) -> p t b", t=BL)
                        hi = hhi[:, 2 * piece + g2, :].bitcast(F32).rearrange("p (b t) -> p t b", t=BL)
                        ins = TT(dst[:, 4 * b:4 * b + 4, :], src, hi[:, 4 * b:4 * b + 4, :], ALU.subtract)
                    ins.then_inc(zt_lo, 1)

            for piece in range(OCTS):
                g = slice(PO * piece, PO * piece + PO)
                rc, rs = rot_c[:, g, :], rot_s[:, g, :]
                here()
                link(nc.vector.tensor_copy(decay[:], S[18][:, g].unsqueeze(2).broadcast_to([P, PO, NB])))
                count(nc.vector.memset(decay[:, :, 0], 0.0))
                dve.wait_ge(in_psum, piece + 1)
                ire = psum[:, 0, :].rearrange("p (g b) -> p g b", g=PO)
                iim = psum[:, 1, :].rearrange("p (g b) -> p g b", g=PO)
                vr = v_re[:].rearrange("p (g b) -> p g b", g=PO)
                vn = v_ni[:].rearrange("p (g b) -> p g b", g=PO)
                t_a = ca[:, 0, :].rearrange("p (g b) -> p g b", g=PO)
                t_b = ca[:, 1, :].rearrange("p (g b) -> p g b", g=PO)
                count(TT(vr, ire, rc, ALU.mult))
                count(TT(t_a, iim, rs, ALU.mult))
                count(TT(vn, ire, rs, ALU.mult))
                TT(t_b, iim, rc, ALU.mult).then_inc(in_read, 1)
                dve.wait_ge(in_read, piece + 1)
                here()
                count(TT(vr, vr, t_a, ALU.add))
                link(TT(vn, vn, t_b, ALU.subtract))
                count(nc.vector.tensor_tensor_scan(v_re[:], flat(decay[:]), v_re[:], 0.0, ALU.mult, ALU.add))
                link(nc.vector.tensor_tensor_scan(v_ni[:], flat(decay[:]), v_ni[:], 0.0, ALU.mult, ALU.add))
                wait(dve, y5_psum, piece - 1)
                n1 = NB - 1
                hr, hn = hx[piece % 2][:, 0, :, 1:NB], hx[piece % 2][:, 1, :, 1:NB]
                vr1, vn1, rc1, rs1 = vr[:, :, 0:n1], vn[:, :, 0:n1], rc[:, :, 0:n1], rs[:, :, 0:n1]
                ta1, tb1 = t_a[:, :, 0:n1], t_b[:, :, 0:n1]
                count(TT(hr, vr1, rc1, ALU.mult))
                count(TT(ta1, vn1, rs1, ALU.mult))
                count(TT(hn, vn1, rc1, ALU.mult))
                link(TT(tb1, vr1, rs1, ALU.mult))
                link(TT(hr, hr, ta1, ALU.add))
                TT(hn, hn, tb1, ALU.subtract).then_inc(hx_ready, 1)
                dve.wait_ge(hx_ready, piece + 1)
                if piece >= 1:
                    zt_low(piece - 1)
            zt_low(OCTS - 1)
            for n in range(2):
                split_low(n, n, 0)

            def ada_step(m, e, k, slot):
                dve.wait_ge(ada_landed[e], 16 * k[1])
                wait(dve, ada_added, m)
                STT(ada_acc[:, slot, :], ada_ring[:, e, :], cond[:, 1, bass.ds(k[0], 1)],
                    ada_acc[:, slot, :], ALU.mult, ALU.add).then_inc(ada_added, 1)

            dve.wait_ge(acc_clear, 2)

            def glu(i, s, half):
                for e in range(2):
                    ada_step(2 * i + e, e, (i, i + (N_ADA_PE // 2 + 1)), e)
                dve.wait_ge(sig_ready, i + 1)
                TT(y_glu[:, i, :], psum[:, 2 * s, :], ca[:, s, :], ALU.mult).then_inc(y_ready, 1)
                split_low(i + 2, s, half)

            glu(0, 0, 0)
            glu(1, 1, 0)
            pairs(dve, 2, N_GLU, glu)

            def spread_rsqrt(stat_):
                dve.wait_ge(stat_psum, stat_ + 1)
                rsqrt(stat[:, 16:16 + QT], psum[:, 4, 0:QT], 1.0, link)
                TT(diag[:], ident[:].unsqueeze(1).broadcast_to([P, QT, P]),
                   stat[:, 16:16 + QT].unsqueeze(2).broadcast_to([P, QT, P]), ALU.mult).then_inc(diag_ready, 1)
                dve.wait_ge(rs_psum, stat_ + 1)

            def post_norm(r):
                spread_rsqrt(2 * r)
                if r == 0:
                    dve.wait_ge(mod_psum, 2)
                    modulation(0, (2, 3, 4, 5))
                y = y_of(r)
                if r == 0:
                    dve.wait_ge(x_in, 16)
                dve.wait_ge(y_ready, KT * (r + 1))
                dve.wait_ge(sq_ready, KT * (2 * r + 1))
                count(TT(y[:, 0, :], y[:, 0, :], psum[:, 5, :], ALU.mult))
                for f in range(KT):
                    if f + 1 < KT:
                        count(TT(y[:, f + 1, :], y[:, f + 1, :], psum[:, 5, :], ALU.mult))
                    dve.wait_ge(dve_step, steps[0] - (1 if f + 1 < KT else 0))
                    STT(x[:, f, :], y[:, f, :], gate[:, r, f:f + 1], x[:, f, :], ALU.mult,
                        ALU.add).then_inc(x_ready, 1)

            def pre_norm(r):
                spread_rsqrt(2 * r + 1)
                for f in range(KT):
                    n = KT * r + f
                    wait(dve, h_aff, n - 1)
                    dve.wait_ge(x_ready, n + 1)
                    TT(ca[:, f % 2, :], x[:, f, :], psum[:, 5, :], ALU.mult).then_inc(t_ready, 1)

            def ffn(layer):
                n0, g0 = U_FIN[layer], layer * JT

                def body(j, s, half, third=None):
                    for i, dst in enumerate((ca, cb)):
                        dve.wait_ge(tap2, 2 * j + (2 * g0 + i + 1))
                        STT(dst[:, s, 1:], psum[:, 2 * s + i, 0:SEQ - 1], convp[:, layer, j, i, 1:2],
                            dst[:, s, 1:], ALU.mult, ALU.add).then_inc(conv_step, 1)
                    for i, dst in enumerate((ca, cb)):
                        dve.wait_ge(conv_step, 2 * j + (2 * g0 + i + 1))
                        STT(dst[:, s, 2:], psum[:, 2 * s + i, 0:SEQ - 2], convp[:, layer, j, i, 0:1],
                            dst[:, s, 2:], ALU.mult, ALU.add).then_inc(conv_done, 1)
                    split_low(j + (n0 + 2), s, half)
                    dve.wait_ge(gelu_done, j + (g0 + 1))
                    dve.wait_ge(conv_done, 2 * j + (2 * g0 + 2))
                    if third is not None:
                        for e in range(2):
                            k = 2 * j + (e - 8 * third)
                            ada_step(2 * j + (2 * N_GLU + e), e, (k, j + (N_ADA_PE // 2 + N_GLU + 1)), third % 2)
                    TT(ca[:, s, :], ca[:, s, :], cb[:, s, :], ALU.mult).then_inc(g_ready, 1)

                if layer == 0:
                    for third in range(3):
                        dve.wait_ge(acc_clear, (4, 4, 5)[third])
                        pairs(dve, 4 * third, 4 * third + 4, partial(body, third=third))
                    pairs(dve, 12, 16, body)
                    dve.wait_ge(mod_psum, 5)
                    modulation(1, range(6))
                    signal(mod_ready)
                    pairs(dve, 16, JT, body)
                else:
                    pairs(dve, 0, JT, body)
                r, m0 = 2 * layer + 1, U_FOUT[layer]
                for hf in range(2):
                    last = min(m0 + 6 * hf + 8, N_UNITS)
                    pairs(dve, m0 + 6 * hf + 2, last, split_low)
                    dve.wait_ge(unit_done, m0 + 6 * (hf + 1))
                    for f in range(4):
                        nc.vector.tensor_copy(y_late[:, 4 * hf + f, :], psum[:, 4 * (1 - hf) + f, :]).then_inc(y_ready, 1)

            post_norm(0)
            pre_norm(0)
            ffn(0)
            post_norm(1)
            pre_norm(1)

            def value_copies(m):
                dve.wait_ge(unit_done, U_V + m + 1)
                for b in range(2):
                    nc.vector.tensor_copy(v_sb[:, 2 * b:2 * b + 2, 256 * m:256 * m + 256],
                                          psum[:, 2 * (m % 2) + b, :].rearrange("p (t e) -> p t e", t=2)).then_inc(v_copied, 1)

            split_low(U_V + 2, 0, None)
            dve.wait_ge(pos_in, 16)
            ang, rt = prob[:, 0, 0, :], prob[:, 0, 1, :]
            link(nc.vector.tensor_copy(ang, pos_i[:]))
            link(TS(ang, ang, rope_c[:, 0:1], None, ALU.mult))
            reduced(sinb[:], cosb[:], ang, rt, link)
            signal(rope_arg)
            dve.wait_ge(lam_in, 16)
            lp = prob[:, 1, 0, 0:2 * HD].rearrange("p (a d) -> p a d", a=2)
            lq = lam_par[:].rearrange("p (a b d) -> p a b d", a=2, b=2)
            link(TT(lp, lq[:, :, 0, :], lq[:, :, 1, :], ALU.mult))
            nc.vector.tensor_reduce(col[:, 1:3], lp, AXX, ALU.add).then_inc(lam_arg, 1)
            value_copies(0)
            dve.wait_ge(rope_sin, 2)
            TS(sinb[:], sinb[:], rope_c[:, 1:2], None, ALU.mult).then_inc(rope_table, 1)
            dve.wait_ge(lam_exp, 1)
            link(TT(col[:, 5:6], col[:, 4:5], col[:, 3:4], ALU.subtract))
            link(TS(col[:, 6:7], col[:, 5:6], -LAMBDA_INIT, None, ALU.add))
            TS(sub_g[:], sub_g[:], 1.0 - LAMBDA_INIT, None, ALU.mult).then_inc(lam_ready, 1)
            for m in range(1, N_V):
                split_low(U_V + m + 2, m % 2, None)
                value_copies(m)

            def row_max(h, qt):
                pb, width = qt % 2, (qt + 1) * P
                dve.wait_ge(s_psum, 4 * h + (qt + 1))
                nc.vector.tensor_reduce(stat[:, 8 * pb + 2:8 * pb + 4], psum[:, 4:6, 0:width], AXX, ALU.max,
                                        negate=True).then_inc(nmax_ready, 1)

            def combine(h, qt):
                pb, width = qt % 2, (qt + 1) * P
                st = stat[:, 8 * pb:8 * pb + 8]
                dve.wait_ge(exp_done, 8 * h + (2 * qt + 2))
                nc.vector.reciprocal(st[:, 6:8], st[:, 4:6]).then_inc(att_step, 1)
                dve.wait_ge(att_step, 8 * h + (2 * qt + 1))
                TS(prob[:, pb, 1, 0:width], prob[:, pb, 1, 0:width], st[:, 7:8], col[:, 6:7],
                   ALU.mult, ALU.mult).then_inc(att_step, 1)
                dve.wait_ge(att_step, 8 * h + (2 * qt + 2))
                if not isinstance(h, int) or 4 * h + qt >= 2:
                    dve.wait_ge(attt_psum, 4 * h + (qt - 1))
                STT(att[:, pb, 0:width], prob[:, pb, 0, 0:width], st[:, 6:7],
                    prob[:, pb, 1, 0:width], ALU.mult, ALU.add).then_inc(att_ready, 1)

            def head_norm(h):
                k = [0]

                def lk(ins):
                    k[0] += 1
                    ins.then_inc(hn_step, 1)
                    dve.wait_ge(hn_step, HEAD_STEPS * h + k[0])
                dve.wait_ge(osq_done, h + 1)
                v, d, t = nwt[:, 2, 0:QT], nwt[:, 3, 0:QT], nwt[:, 1, 0:QT]
                lk(nc.vector.tensor_reduce(v, sq[:, 0, :].rearrange("p (t e) -> p t e", t=QT), AXX, ALU.add))
                lk(TS(v, v, 1.0 / P, EPS, ALU.mult, ALU.add))
                lk(TS(t.bitcast(I32), v.bitcast(I32), 1, None, ALU.logical_shift_right))
                lk(TS(d.bitcast(I32), t.bitcast(I32), -1.0, RSQRT_MAGIC, ALU.mult, ALU.add))
                yield
                for i in range(3):
                    lk(TT(t, d, d, ALU.mult))
                    lk(STT(t, t, -0.5, v, ALU.mult, ALU.mult))
                    lk(STT(d, t, 1.5, d, ALU.add, ALU.mult))
                    if i == 0:
                        yield
                assert k[0] == HEAD_STEPS
                dve.wait_ge(o_copied, h + 1)
                if not isinstance(h, int) or h >= 1:
                    dve.wait_ge(ot_psum, h)
                TT(on[:], o_sb.rearrange("p (t e) -> p t e", t=QT),
                   d.unsqueeze(2).broadcast_to([P, QT, P]), ALU.mult).then_inc(on_ready, 1)
                yield

            def half_low(h, s, part):
                n = h + (U_QK + 1)
                c = slice(part * UNIT // 2, (part + 1) * UNIT // 2)
                if part:
                    dve.wait_ge(split_hi, n + 1)
                else:
                    dve.wait_ge(half_hi, h)
                ins = TT(wlo[:, 1 - s, c], raw[:, 1 - s, c], whi[:, 1 - s, c].bitcast(F32), ALU.subtract)
                ins.then_inc(split_lo if part else half_lo, 1)

            def head(h, s, half, first=False, split=True):
                a_ = h - 2
                norm = iter(()) if first else head_norm(a_ - 1)
                row_max(a_, 0)
                combine(a_, 0)
                row_max(a_, 1)
                next(norm, None)
                combine(a_, 1)
                row_max(a_, 2)
                if split:
                    half_low(h, s, 0)
                next(norm, None)
                combine(a_, 2)
                row_max(a_, 3)
                next(norm, None)
                if split:
                    half_low(h, s, 1)
                combine(a_, 3)

            half_low(1, 1, 0)
            half_low(1, 1, 1)
            head(2, 0, None, first=True)
            head(3, 1, None)
            pairs(dve, 4, HEADS, head)
            head(HEADS, 0, None)
            head(HEADS + 1, 1, None, split=False)
            for _ in head_norm(HEADS - 1):
                pass
            for m in range(N_WO):
                n = U_WO + m
                dve.wait_ge(unit_done, n + 1)
                for i in range(2):
                    nc.vector.tensor_copy(y_late[:, 2 * m + i, :], psum[:, 2 * (m % 2) + i, :]).then_inc(y_ready, 1)
                split_low(n + 2, m % 2, None)
            post_norm(2)
            pre_norm(2)
            ffn(1)
            post_norm(3)

        @block.tensor
        def _(pe):
            M = nc.tensor.matmul

            def ada_unit(n, s):
                pe.wait_ge(ada_landed[s], 16 * (n // 2) + 16)
                for f in range(2):
                    for k in range(KT):
                        ins = M(psum[:, 7, 2 * n + f:2 * n + f + 1],
                                ada0_raw[:, s, 256 * k + P * f:256 * k + P * f + P], cond[:, 1, k:k + 1],
                                start=(k == 0), stop=(k == KT - 1))
                ins.then_inc(ada_used, 1)

            def reduce_acc(slot, col0):
                for f in range(THIRD):
                    ins = M(psum[:, 7, col0 + f:col0 + f + 1], ada_acc[:, slot, P * f:P * f + P],
                            ones[:, 0:1], start=True, stop=True)
                ins.then_inc(mod_psum, 1)

            pe.wait_ge(cond_ready, 1)
            for n in range(N_ADA_PE):
                ada_unit(n, n % 2)
                if n == 3:
                    pe.wait_ge(usum_ready, 1)
                    M(psum[:, 6, 0:NB], blk16[:].rearrange("p g c -> p (g c)"), nwt[:, 2, :],
                      start=True, stop=True).then_inc(uvar_psum, 1)
            pe.wait_ge(cl_ready, 1)
            pe.wait_ge(bd_ready, 4)
            for t in range(KT):
                for q in range(4):
                    gp = 4 * t + q
                    out = psum[32 * q:32 * q + 32, 4 + t // 4, P * (t % 4):P * (t % 4) + P]
                    for i, cl in enumerate((cl_re, cl_im)):
                        ins = M(out, bd[i][:, gp, :], cl[:, gp, 0:BL, :].rearrange("p k c -> p (k c)"),
                                start=(i == 0), stop=(i == 1), skip_group_check=True)
            ins.then_inc(k_psum, 1)
            pe.wait_ge(umod_rhs, 2)
            M(psum[:, 6, NB:NB + 2 * GROUPS], sel16[:].rearrange("p t c -> p (t c)"),
              ca[:, 0, 0:2 * GROUPS], start=True, stop=True).then_inc(umod_psum, 1)
            pe.wait_ge(lb_ready, 2 * BL)
            for t in range(16):
                wait(pe, inb_ready, t - 1)
                lb = lb_re if t < 8 else lb_im
                for q in range(4):
                    ins = nc.tensor.transpose(psum[:, 2 + t % 2, P * q:P * q + P],
                                              lb[:, 4 * (t % 8) + q].rearrange("p t c -> p (t c)"), ident[:])
                ins.then_inc(inb_psum, 1)
            pe.wait_ge(inb_ready, 16)

            def inputs(piece):
                pe.wait_ge(u_ready, piece + 1)
                wait(pe, in_read, piece)
                for i, inb in enumerate((inb_re, inb_im)):
                    for j in range(PO):
                        for g2 in range(2):
                            gp = PO * piece + j
                            ins = M(psum[64 * g2:64 * g2 + 64, i, NB * j:NB * j + NB],
                                    inb[:, gp, 64 * g2:64 * g2 + 64], u[:, 2 * gp + g2, :],
                                    start=True, stop=True)
                ins.then_inc(in_psum, 1)

            def outputs(piece):
                pe.wait_ge(toep_in[piece % 2], 16 * BL * (piece // 2 + 1))
                wait(pe, z_ready, 2 * piece)
                pe.wait_ge(hx_ready, piece + 1)
                for j in range(PO):
                    gp = PO * piece + j
                    for g2 in range(2):
                        rows = slice(64 * g2, 64 * g2 + 64)
                        out = psum[rows, 4 + j // 4, P * (j % 4):P * (j % 4) + P]
                        M(out, u[:, 2 * gp + g2, :], toep[piece % 2][:, 2 * j + g2, :], start=True,
                          stop=False, skip_group_check=True)
                        for i, cl in enumerate((cl_re, cl_im)):
                            ins = M(out, hx[piece % 2][rows, i, j, 0:NB],
                                    cl[rows, gp, 1:, :].rearrange("p k c -> p (k c)"), start=False,
                                    stop=(i == 1), skip_group_check=True)
                ins.then_inc(y5_psum, 1)

            def back(piece):
                pe.wait_ge(z_ready, 2 * piece + 2)
                wait(pe, zt_lo, 2 * piece)
                for t in range(BL):
                    ins = nc.tensor.transpose(psum[:, 2 + t // 4, P * (t % 4):P * (t % 4) + P],
                                              z[:, t].rearrange("p g c -> p (g c)"), ident[:])
                ins.then_inc(zt_psum, 1)

            inputs(0)
            for piece in range(OCTS):
                if piece + 1 < OCTS:
                    inputs(piece + 1)
                outputs(piece)
                back(piece)

            def gemm_step(s, step, hi, lo, n_cols=None):
                half, k = divmod(step, KT)
                w = slice(P * step, P * step + P)
                out = psum[:, 2 * s + half, :]
                M(out, whi[:, s, w], hi[:, k, :], start=(k == 0), stop=False)
                M(out, whi[:, s, w], lo[:, k, :], start=False, stop=False)
                return M(out, wlo[:, s, w], hi[:, k, :], start=False, stop=(k == KT - 1))

            def gemm(n, s, hi, lo, ready=None):
                pe.wait_ge(split_lo, n + 1)
                for step in range(2 * KT):
                    if ready and step < KT:
                        ready(step)
                    ins = gemm_step(s, step, hi, lo)
                ins.then_inc(unit_done, 1)

            def glu(i, s, half):
                if not isinstance(i, int) or i >= 2:
                    pe.wait_ge(y_ready, i - 1)
                gemm(i, s, hhi, hlo)

            pe.wait_ge(zt_lo, 2 * OCTS)
            glu(0, 0, 0)
            glu(1, 1, 0)
            pairs(pe, 2, N_GLU, glu)

            def statistic(stat_):
                pe.wait_ge(sq_added, KT * (stat_ + 1))
                for t in range(QT):
                    ins = M(psum[:, 4, t:t + 1], ssum[:, P * t:P * t + P], col[:, 0:1], start=True, stop=True)
                ins.then_inc(stat_psum, 1)
                if stat_ == 0:
                    reduce_acc(1, 2 * THIRD)
                pe.wait_ge(diag_ready, stat_ + 1)
                M(psum[:, 5, :], ones[:], diag[:].rearrange("p t s -> p (t s)"), start=True,
                  stop=True).then_inc(rs_psum, 1)

            def ffn(layer):
                n0, g0 = U_FIN[layer], layer * JT

                def body(j, s, half):
                    if not isinstance(j, int) or j >= 2:
                        pe.wait_ge(conv_done, 2 * j + (2 * g0 - 2))
                    first = isinstance(j, int) and j == 0
                    gemm(j + n0, s, hhi, hlo,
                         (lambda k: pe.wait_ge(h_lo, KT * 2 * layer + k + 1)) if first else None)

                body(0, 0, 0)
                body(1, 1, 0)
                if layer == 0:
                    for third in range(3):
                        pairs(pe, max(4 * third + 2, 2), 4 * third + 6, body)
                        pe.wait_ge(ada_added, 2 * N_GLU + 8 * third + 8)
                        reduce_acc(third % 2, THIRD * (3 + third))
                    pairs(pe, 14, JT, body)
                    pe.wait_ge(mod_ready, 1)
                else:
                    pairs(pe, 2, JT, body)

                for hf in range(2):
                    m0 = U_FOUT[layer] + 6 * hf
                    b0 = 4 * (1 - hf)

                    def down(v, s, half, m0=m0, b0=b0):
                        fixed = isinstance(v, int)
                        n_k = min(FOUT_K, JT - FOUT_K * v) if fixed else FOUT_K
                        pe.wait_ge(split_lo, v + (m0 + 1))
                        for k in range(n_k):
                            row = FOUT_K * v + k
                            pe.wait_ge(g_lo, row + (g0 + 1))
                            for f in range(4):
                                w = slice(512 * k + P * f, 512 * k + P * f + P)
                                out = psum[:, b0 + f, :]
                                st = fixed and v == 0 and k == 0
                                sp_ = fixed and row == JT - 1
                                M(out, whi[:, s, w], ghi[:, row, :], start=st, stop=False)
                                M(out, whi[:, s, w], glo[:, row, :], start=False, stop=False)
                                ins = M(out, wlo[:, s, w], ghi[:, row, :], start=False, stop=sp_)
                        ins.then_inc(unit_done, 1)

                    down(0, 0, 0)
                    down(1, 1, 0)
                    pairs(pe, 2, 4, down)
                    down(4, 0, 0)
                    down(5, 1, 0)

            pe.wait_ge(ada_added, 2 * N_GLU)
            reduce_acc(0, THIRD)
            statistic(0)
            statistic(1)
            ffn(0)
            statistic(2)
            statistic(3)

            for m in range(N_V):
                s = m % 2
                pe.wait_ge(split_lo, U_V + m + 1)
                if m == 0:
                    pe.wait_ge(h_lo, 2 * KT)
                wait(pe, v_copied, 2 * (m - 1))
                for t in range(QT):
                    out = psum[:, 2 * s + t // 2, 256 * (t % 2):256 * (t % 2) + 256]
                    tok = slice(P * t, P * t + P)
                    for k in range(KT):
                        w = slice(256 * k, 256 * k + 256)
                        M(out, hhi[:, k, tok], whi[:, s, w], start=(k == 0), stop=False)
                        M(out, hlo[:, k, tok], whi[:, s, w], start=False, stop=False)
                        ins = M(out, hhi[:, k, tok], wlo[:, s, w], start=False, stop=(k == KT - 1))
                ins.then_inc(unit_done, 1)
            pe.wait_ge(v_copied, 2 * N_V)
            pe.wait_ge(mask_ready, 3)

            def scores(h, s, qt):
                if qt == 0:
                    pe.wait_ge(qk_ready, 2 * h + 2)
                if not isinstance(h, int) or 4 * h + qt >= 1:
                    pe.wait_ge(exp_done, 8 * h + 2 * qt)
                width = (qt + 1) * P
                for c in range(2):
                    rows = slice(HD * c, HD * c + HD)
                    M(psum[:, 4 + c, 0:width], qk[rows, s, 0, P * qt:P * qt + P], qk[rows, s, 1, 0:width],
                      start=True, stop=True)
                    ins = M(psum[:, 4 + c, width - HD:width], maskw[0:1, 0, :], maskw[0:1, 1, 0:HD],
                            start=False, stop=True, skip_group_check=True)
                ins.then_inc(s_psum, 1)

            def turn(h, qt):
                pb = qt % 2
                pe.wait_ge(att_ready, 4 * h + (qt + 1))
                if not isinstance(h, int) or 4 * h + qt >= 1:
                    pe.wait_ge(attt_copied, 4 * h + qt)
                if qt == 3 and (not isinstance(h, int) or h >= 1):
                    pe.wait_ge(ot_copied, h)
                for kb in range(qt + 1):
                    ins = nc.tensor.transpose(psum[:, 6, P * kb:P * kb + P], att[:, pb, P * kb:P * kb + P], ident[:])
                ins.then_inc(attt_psum, 1)

            def weigh(h, qt):
                pb = qt % 2
                pe.wait_ge(attt_copied, 4 * h + (qt + 1))
                if qt == 0 and (not isinstance(h, int) or h >= 1):
                    pe.wait_ge(o_copied, h)
                for kb in range(qt + 1):
                    ins = M(psum[:, 7, P * qt:P * qt + P], att_t[:, pb, P * kb:P * kb + P],
                            v_sb[:, kb, bass.ds(h * P, P)] if not isinstance(h, int)
                            else v_sb[:, kb, P * h:P * h + P], start=(kb == 0), stop=(kb == qt))
                ins.then_inc(o_psum, 1)

            def turn_out(h):
                pe.wait_ge(on_ready, h + 1)
                pe.wait_ge(attt_copied, min(4 * h + 7, 4 * HEADS) if isinstance(h, int) else 4 * h + 7)
                for t in range(QT):
                    ins = nc.tensor.transpose(psum[:, 6, P * t:P * t + P], on[:, t, :], ident[:])
                ins.then_inc(ot_psum, 1)

            def project(h, s):
                pe.wait_ge(split_lo, h + (U_QK + 1))
                if not isinstance(h, int) or h >= 2:
                    pe.wait_ge(raw_copied, 2 * h - 2)
                for step in range(2 * KT):
                    ins = gemm_step(s, step, hhi, hlo)
                    if step == 2 * KT - 1:
                        ins.then_inc(unit_done, 1)
                    if step % 2:
                        yield

            def wo_step(m, k):
                pe.wait_ge(ot_lo, k + 3)
                for half in range(2):
                    ins = gemm_step(m % 2, KT * half + k, ohi, olo)
                return ins

            def attend(a_, s, fill, first=False):
                for qt in range(QT):
                    scores(a_, s, qt)
                    next(fill, None)
                    last, q = (a_ - 1, 3) if qt == 0 else (a_, qt - 1)
                    if not (first and qt == 0):
                        turn(last, q)
                    next(fill, None)
                    if not (first and qt == 0):
                        weigh(last, q)
                if not first:
                    turn_out(a_ - 1)

            def head(h, s, half, first=False):
                attend(h - 2, s, project(h, s), first)

            def early_output(steps_):
                for m, k in steps_:
                    if k == 0:
                        pe.wait_ge(split_lo, U_WO + m + 1)
                        pe.wait_ge(raw_copied, 2 * (HEADS - 1 + m))
                    wo_step(m, k)
                    yield

            for h in range(2):
                for _ in project(h, h):
                    pass
            head(2, 0, None, first=True)
            head(3, 1, None)
            pairs(pe, 4, HEADS, head)
            attend(HEADS - 2, 0, early_output([(0, k) for k in range(5)]))
            attend(HEADS - 1, 1, early_output([(1, k) for k in range(5)] + [(0, 5), (1, 5)]))
            turn(HEADS - 1, 3)
            weigh(HEADS - 1, 3)
            turn_out(HEADS - 1)
            for m in range(2):
                wo_step(m, KT - 2)
            for m in range(2):
                wo_step(m, KT - 1).then_inc(unit_done, 1)
            for m in range(2, N_WO):
                pe.wait_ge(y_ready, KT * 2 + 2 * (m - 1))
                gemm(U_WO + m, m % 2, ohi, olo)
            statistic(4)
            statistic(5)
            ffn(1)
            statistic(6)


def _pair_units(w, rows, left, right, n):
    w = w.reshape(KT, P, -1) if rows is None else rows(w)
    out = np.empty((n, P, 2, KT, P), np.float32)
    for i in range(n):
        for q, c in enumerate((left(i), right(i))):
            out[i, :, q] = w[:, :, c:c + P].transpose(1, 0, 2)
    return out.reshape(n, P, UNIT)


def _units(inp):
    def glu_rows(w):
        return w.reshape(OCTS, PO, 2, CG, -1).transpose(0, 2, 1, 3, 4).reshape(KT, P, -1)

    def down_units(w):
        w = w.reshape(JT, P, D)
        padded = np.concatenate([w, np.zeros((2, P, D), np.float32)])
        return padded.reshape(6, FOUT_K, P, 2, 512).transpose(3, 0, 2, 1, 4).reshape(N_FOUT, P, UNIT)

    w_in, w_out = inp["ffn_w_in"], inp["ffn_w_out"]
    qkv, wo = inp["da_w_qkv"][0], inp["da_w_o"][0]
    ups = [_pair_units(w_in[i], None, lambda j: P * j, lambda j: DFF + P * j, N_FIN) for i in range(2)]
    values = qkv[:, 2 * D:].reshape(KT, P, N_V, 256).transpose(2, 1, 0, 3).reshape(N_V, P, UNIT)
    return np.concatenate([
        _pair_units(inp["s5_w_glu"][0], glu_rows, lambda j: P * j, lambda j: D + P * j, N_GLU),
        ups[0], down_units(w_out[0]), values,
        _pair_units(qkv, None, lambda j: P * j, lambda j: D + P * j, N_QK),
        _pair_units(wo, None, lambda j: 2 * P * j, lambda j: 2 * P * j + P, N_WO),
        ups[1], down_units(w_out[1])])


def _ada_units(w):
    first = w[0].reshape(KT, P, -1)[:, :, :UNIT].reshape(KT, P, N_ADA_PE, 256).transpose(2, 1, 0, 3)
    rows = w.reshape(2, KT, P, 3, UNIT)
    rest = rows[0, :, :, 1:].transpose(0, 2, 1, 3)
    second = rows[1].transpose(2, 0, 1, 3)
    return np.concatenate([v.reshape(-1, P, UNIT) for v in (first, rest, second)])


def _cols(v):
    return v.reshape(-1, P).T


def _layout(inp):
    def state(v):
        v = v.reshape(PAIRS, 2, 64, *v.shape[2:])
        return v.transpose(1, 2, 0, *range(3, v.ndim)).reshape(P, PAIRS, *v.shape[3:])

    x0 = inp["x"][0]
    log_dt = np.broadcast_to(inp["s5_log_dt"][0][:, None], (GROUPS, 64))
    half = HD // 2
    inv = (ROPE_THETA ** (-np.arange(half, dtype=np.float32) / np.float32(half)).astype(np.float64)).astype(np.float32)
    sign = np.where(np.arange(P) % HD < half, -1.0, 1.0).astype(np.float32)
    conv = np.concatenate([inp["ffn_conv_w"], inp["ffn_conv_b"][:, None]], axis=1)
    return {
        "x_t": x0.T,
        "x_blocks": x0.reshape(NB, BL, GROUPS, CG)[:, ::-1].transpose(1, 3, 2, 0).reshape(P, GROUPS * NB),
        "s5_par": np.stack([state(inp["s5_a_re"][0]), state(inp["s5_a_im"][0]), state(log_dt)], axis=1),
        "s5_bc": np.stack([state(inp["s5_b_re"][0]), state(inp["s5_b_im"][0]),
                           state(inp["s5_c_re"][0].transpose(0, 2, 1)),
                           state(inp["s5_c_im"][0].transpose(0, 2, 1))], axis=1),
        "c_cols": _cols(inp["c"][0]),
        "d_cols": _cols(inp["s5_d"][0]),
        "ada_b": np.stack([_cols(v) for v in inp["ada_b"]], axis=1),
        "norm_g": np.stack([np.stack([_cols(v) for v in g], axis=1) for g in inp["norm_g"]], axis=1),
        "conv_par": conv.reshape(2, 4, 2, JT, P).transpose(4, 0, 3, 2, 1),
        "sub_g": inp["da_subln_g"][0][:, None],
        "rope_c": np.stack([np.tile(inv, P // half), sign], axis=1),
        "positions": inp["positions"][0],
        "lam_par": np.concatenate([inp[n][0] for n in ("da_lq1", "da_lk1", "da_lq2", "da_lk2")]),
        "ada_w": _ada_units(inp["ada_w"]),
        "units": _units(inp),
    }


def kernel(**inputs):
    import concourse.bacc as _bacc
    from concourse import mybir as _mybir
    from concourse.bass_utils import run_bass_kernel_spmd as _run

    inp = {k: np.asarray(v) for k, v in inputs.items()}
    arrays = {k: np.ascontiguousarray(v) for k, v in _layout(inp).items()}
    nc = _bacc.Bacc("TRN2", target_bir_lowering=False, num_devices=1)
    aps = {k: nc.dram_tensor(f"in_{k}", v.shape, _mybir.dt.from_np(v.dtype), kind="ExternalInput").ap()
           for k, v in arrays.items()}
    out = nc.dram_tensor("out_t", (D, SEQ), F32, kind="ExternalOutput").ap()
    build(nc, aps, out)
    r = _run(nc, [{f"in_{k}": v for k, v in arrays.items()}], core_ids=[0])
    return r.results[0]["out_t"].T.reshape(1, SEQ, D)
```

```python
import math
from contextlib import ExitStack
from functools import partial

import numpy as np

import concourse.bass as bass
from concourse import mybir

F32 = mybir.dt.float32
F32R = mybir.dt.float32r
I32 = mybir.dt.int32
ALU = mybir.AluOpType
ACT = mybir.ActivationFunctionType
AXX = mybir.AxisListType.X

P = 128
D = 1024
SEQ = 512
KT = D // P
UNIT = 2048
DFF = 2816
JT = DFF // P
EPS = 1e-6

CG = 16
GROUPS = D // CG
PAIRS = GROUPS // 2
BL = 8
NB = SEQ // BL
OCTS = 4
PO = PAIRS // OCTS
LAM_MAX = -1e-4

HEADS = 8
HD = 64
QT = SEQ // P
LAMBDA_INIT = 0.8 - 0.6 * math.exp(-0.3)
ROPE_THETA = 10000.0
MASKED = -1e30

N_GLU, N_FIN, N_FOUT, N_V, N_QK, N_WO = KT, JT, 12, 4, HEADS, 4
U_GLU = 0
U_FIN = (N_GLU, N_GLU + N_FIN + N_FOUT + N_V + N_QK + N_WO)
U_FOUT = (U_FIN[0] + N_FIN, U_FIN[1] + N_FIN)
U_V = U_FOUT[0] + N_FOUT
U_QK = U_V + N_V
U_WO = U_QK + N_QK
N_UNITS = U_FOUT[1] + N_FOUT
N_ADA_PE = KT
N_ADA0 = 5
THIRD = UNIT // P
FOUT_K = 4

TWO_PI = 2.0 * math.pi
PI_A = 6.28125
PI_B = float(np.float32(round((TWO_PI - PI_A) * 2.0 ** 19) / 2.0 ** 19))
PI_C = float(np.float32(TWO_PI - PI_A - PI_B))
PI_CLAMP = float(np.nextafter(np.float32(math.pi), np.float32(0)))
ROUND = 1.5 * 2.0 ** 23
HEAD_STEPS = 13
RSQRT_MAGIC = float(0x5F3759DF)


def build(nc, a, out_t):
    ctx = ExitStack()
    with ctx:
        base = [nc.sbuf_base]

        def at(name, shape, dt, offset):
            return nc.alloc_sbuf_tensor_at(name, shape, dt, offset=offset)

        def place(nbytes):
            o = (base[0] + 31) // 32 * 32
            base[0] = o + nbytes
            return o

        def sb(name, shape, dt=F32):
            n = int(np.prod(shape[1:])) * 4
            return at(name, shape, dt, place(n))

        def sem(name):
            return ctx.enter_context(nc.semaphore(name))

        raw_at = place(2 * UNIT * 4)
        raw = at("raw", [P, 2, UNIT], F32, raw_at)
        w_at = place(4 * UNIT * 4)
        whi = at("whi", [P, 2, UNIT], F32R, w_at)
        wlo = at("wlo", [P, 2, UNIT], F32R, w_at + 2 * UNIT * 4)
        x_at = place(KT * SEQ * 4)
        x = at("x", [P, KT, SEQ], F32, x_at)
        h_at = place(2 * KT * SEQ * 4)
        hhi = at("hhi", [P, KT, SEQ], F32R, h_at)
        hlo = at("hlo", [P, KT, SEQ], F32R, h_at + KT * SEQ * 4)
        big_at = place(2 * JT * SEQ * 4)

        ghi = at("ghi", [P, JT, SEQ], F32R, big_at)
        glo = at("glo", [P, JT, SEQ], F32R, big_at + JT * SEQ * 4)
        y_late = at("y_late", [P, KT, SEQ], F32, h_at + KT * SEQ * 4)
        y_glu = at("y_glu", [P, KT, SEQ], F32, big_at)
        ada_ring = at("ada_ring", [P, 2, UNIT], F32, big_at + (JT - 8) * SEQ * 4)
        ada_acc = at("ada_acc", [P, 2, UNIT], F32, big_at + (2 * JT - 8) * SEQ * 4)

        ada0_raw = at("ada0_raw", [P, N_ADA0, UNIT], F32, raw_at)
        mod_row = at("mod_row", [1, UNIT], F32, w_at + 3 * UNIT * 4)
        inb_re = at("inb_re", [P, PAIRS, P], F32, w_at)
        inb_im = at("inb_im", [P, PAIRS, P], F32, w_at + PAIRS * P * 4)
        rot_c = at("rot_c", [P, PAIRS, NB], F32, x_at)
        rot_s = at("rot_s", [P, PAIRS, NB], F32, x_at + PAIRS * NB * 4)
        lb_re = at("lb_re", [P, PAIRS, BL, CG], F32, h_at)
        lb_im = at("lb_im", [P, PAIRS, BL, CG], F32, h_at + PAIRS * BL * CG * 4)
        o = big_at
        u = at("u", [P, GROUPS, NB], F32, o); o += GROUPS * NB * 4
        cl_re = at("cl_re", [P, PAIRS, BL + 1, CG], F32, o); o += PAIRS * (BL + 1) * CG * 4
        cl_im = at("cl_im", [P, PAIRS, BL + 1, CG], F32, o); o += PAIRS * (BL + 1) * CG * 4
        toep, kpad, bd = [], None, []
        for i in range(2):
            toep.append(at(f"toep{i}", [P, 2 * PO, BL * CG], F32, o))
            if i == 0:
                bd = [at("bd_re", [P, PAIRS, 2 * CG], F32, o),
                      at("bd_im", [P, PAIRS, 2 * CG], F32, o + PAIRS * 2 * CG * 4)]
            else:
                kpad = at("kpad", [P, KT, (2 * BL - 1) * CG], F32, o)
            o += 2 * PO * BL * CG * 4
        pw_re = at("pw_re", [P, BL + 1, PAIRS], F32, o)
        pw_im = at("pw_im", [P, BL + 1, PAIRS], F32, o + (BL + 1) * PAIRS * 4)
        v_re = at("v_re", [P, PO * NB], F32, o); o += PO * NB * 4
        v_ni = at("v_ni", [P, PO * NB], F32, o); o += PO * NB * 4
        bc_par = at("bc_par", [P, 4, PAIRS, CG], F32, o)
        hx = []
        for i in range(2):
            hx.append(at(f"hx{i}", [P, 2, PO, NB + 1], F32, o)); o += 2 * PO * (NB + 1) * 4
        bb = at("bb", [P, 2, PAIRS, CG], F32, o)
        z = at("z", [P, BL, PO, CG], F32, o); o += BL * PO * CG * 4
        decay = at("decay", [P, PO, NB], F32, o); o += PO * NB * 4
        sel16 = at("sel16", [P, BL, CG], F32, o); o += P * 4
        blk16 = at("blk16", [P, KT, CG], F32, o); o += P * 4
        assert o <= big_at + 2 * JT * SEQ * 4

        o = big_at
        cosb = at("cosb", [P, SEQ], F32, o); o += SEQ * 4
        sinb = at("sinb", [P, SEQ], F32, o); o += SEQ * 4
        v_sb = at("v_sb", [P, QT, D], F32, o); o += QT * D * 4
        ohi = at("ohi", [P, HEADS, SEQ], F32R, o); o += HEADS * SEQ * 4
        olo = at("olo", [P, HEADS, SEQ], F32R, o); o += HEADS * SEQ * 4
        qk = at("qk", [P, 2, 2, SEQ], F32, o); o += 4 * SEQ * 4
        qk_sw = at("qk_sw", [P, 2, SEQ], F32, o); o += 2 * SEQ * 4
        prob = at("prob", [P, 2, 2, SEQ], F32, o); o += 4 * SEQ * 4
        att = at("att", [P, 2, SEQ], F32, o); o += 2 * SEQ * 4
        att_t = at("att_t", [P, 2, SEQ], F32, o); o += 2 * SEQ * 4
        pos_i = at("pos_i", [P, SEQ], I32, o); o += SEQ * 4
        lam_par = at("lam_par", [P, 4 * HD], F32, o); o += 4 * HD * 4
        maskw = at("maskw", [1, 2, P], F32, o); o += 2 * P * 4
        assert o <= big_at + 2 * JT * SEQ * 4

        ca = sb("ca", [P, 2, SEQ])
        cb = sb("cb", [P, 2, SEQ])
        sq = sb("sq", [P, 2, SEQ])
        ssum = sb("ssum", [P, SEQ])
        qk_raw, o_sb = ca, sq[:, 1, :]
        s5_at = place(2 * SEQ * 4)
        s5s = at("s5s", [P, 32, PAIRS], F32, s5_at)
        diag = at("diag", [P, QT, P], F32, s5_at)
        on = at("on", [P, QT, P], F32, s5_at + SEQ * 4)
        ident = sb("ident", [P, P])
        ones = sb("ones", [P, P])
        modt = sb("modt", [P, 2, 48])
        ada_b = sb("ada_b", [P, 2, 48])
        norm_g = sb("norm_g", [P, 2, 4, KT])
        pre_a = sb("pre_a", [P, 4, KT])
        gate = sb("gate", [P, 4, KT])
        convp = sb("convp", [P, 2, JT, 2, 4])
        cond = sb("cond", [P, 2, KT])
        dskip = sb("dskip", [P, KT])
        col = sb("col", [P, 8])
        nwt = sb("nwt", [P, 4, NB])
        stat = sb("stat", [P, 48])
        gmask = sb("gmask", [P, BL])
        sub_g = sb("sub_g", [P, 1])
        rope_c = sb("rope_c", [P, 2])
        assert base[0] <= nc.sbuf_usable_end, (base[0], nc.sbuf_usable_end)

        psum = ctx.enter_context(nc.psum_tensor("psum", [P, 8, 512], F32))
        krows = nc.dram_tensor("toeplitz_rows", [D, (2 * BL - 1) * CG], F32).ap()

        raw_landed = [sem("raw_landed0"), sem("raw_landed1")]
        split_hi, split_lo, unit_done = sem("split_hi"), sem("split_lo"), sem("unit_done")
        ada0_landed = [sem(f"ada0_landed{i}") for i in range(N_ADA0)]
        ada_landed = [sem("ada_landed0"), sem("ada_landed1")]
        ada_used, ada_added, acc_clear = sem("ada_used"), sem("ada_added"), sem("acc_clear")
        par_in, small_in, u_in, x_in, bc_in = (sem("par_in"), sem("small_in"), sem("u_in"),
                                               sem("x_in"), sem("bc_in"))
        pos_in, lam_in = sem("pos_in"), sem("lam_in")
        out_stored = sem("out_stored")
        dve_step, act_step, pool_step = sem("dve_step"), sem("act_step"), sem("pool_step")
        sel_ready = sem("sel_ready")
        ident_ready, const_ready, cond_ready = (sem("ident_ready"), sem("const_ready"),
                                                sem("cond_ready"))
        tanh_ready, sine_arg, sine_ready = sem("tanh_ready"), sem("sine_arg"), sem("sine_ready")
        tanh_arg = sem("tanh_arg")
        pw_ready, bb_ready, bd_ready = sem("pw_ready"), sem("bb_ready"), sem("bd_ready")
        lb_dve, lb_pool, cl_dve, cl_pool, row0_ready, rot_ready = (
            sem("lb_dve"), sem("lb_pool"), sem("cl_dve"), sem("cl_pool"), sem("row0_ready"),
            sem("rot_ready"))
        row_copied, mod0_psum = sem("row_copied"), sem("mod0_psum")
        u_normed, uab_ready = sem("u_normed"), sem("uab_ready")
        inb_psum, inb_ready = sem("inb_psum"), sem("inb_ready")
        k_psum, k_copied, k_ready, k_stored = (sem("k_psum"), sem("k_copied"), sem("k_ready"),
                                               sem("k_stored"))
        kzero = sem("kzero")
        toep_in = [sem("toep_in0"), sem("toep_in1")]
        usq_ready, usq_added, usum_ready, uvar_psum = (sem("usq_ready"), sem("usq_added"),
                                                       sem("usum_ready"), sem("uvar_psum"))
        mod_psum, mod_ready = sem("mod_psum"), sem("mod_ready")
        umod_rhs, umod_psum, u_ready = sem("umod_rhs"), sem("umod_psum"), sem("u_ready")
        in_psum, in_read, hx_re, hx_im, scanned = (sem("in_psum"), sem("in_read"), sem("hx_re"),
                                                   sem("hx_im"), sem("scanned"))
        y5_psum, z_ready, zt_psum, zt_hi, zt_lo = (sem("y5_psum"), sem("z_ready"),
                                                   sem("zt_psum"), sem("zt_hi"), sem("zt_lo"))
        sig_ready, y_ready = sem("sig_ready"), sem("y_ready")
        sq_ready, sq_added, sq_summed, diag_ready, rs_psum = (
            sem("sq_ready"), sem("sq_added"), sem("sq_summed"), sem("diag_ready"), sem("rs_psum"))
        x_dve, x_pool, gated, t_ready, h_aff, h_hi, h_lo_dve, h_lo_pool = (
            sem("x_dve"), sem("x_pool"), sem("gated"), sem("t_ready"), sem("h_aff"), sem("h_hi"),
            sem("h_lo_dve"), sem("h_lo_pool"))
        tap2, conv_done, gelu_done, g_ready, g_hi, g_lo = (
            sem("tap2"), sem("conv_done"), sem("gelu_done"), sem("g_ready"), sem("g_hi"),
            sem("g_lo"))
        conv_step = sem("conv_step")
        v_copied = sem("v_copied")
        rope_arg, rope_sin, rope_table, lam_exp, lam_arg, lam_ready = (
            sem("rope_arg"), sem("rope_sin"), sem("rope_table"), sem("lam_exp"), sem("lam_arg"),
            sem("lam_ready"))
        raw_copied, swapped, sw_mul, cos_mul, qk_ready = (
            sem("raw_copied"), sem("swapped"), sem("sw_mul"), sem("cos_mul"), sem("qk_ready"))
        half_hi, half_lo, o_copied = sem("half_hi"), sem("half_lo"), sem("o_copied")
        s_psum, nmax_ready, exp_done, att_ready = (sem("s_psum"), sem("nmax_ready"),
                                                   sem("exp_done"), sem("att_ready"))
        mask_ready = sem("mask_ready")
        att_step, smax, hn_step = sem("att_step"), sem("smax"), sem("hn_step")
        rot_init, rot_first, rot_copy = sem("rot_init"), sem("rot_first"), sem("rot_copy")
        attt_psum, attt_copied, o_psum, osq_done = (sem("attt_psum"), sem("attt_copied"),
                                                    sem("o_psum"), sem("osq_done"))
        on_ready, ot_psum, ot_copied, ot_hi, ot_lo = (sem("on_ready"), sem("ot_psum"),
                                                      sem("ot_copied"), sem("ot_hi"),
                                                      sem("ot_lo"))

        def wait(eng, s, n):
            if isinstance(n, int) and n <= 0:
                return
            eng.wait_ge(s, n)

        def pairs(eng, lo, hi, body):
            with eng.Fori(0, (hi - lo) // 2) as i:
                for s in range(2):
                    body(2 * i + (lo + s), s, i + lo // 2)

        def y_of(r):
            return y_glu if r == 0 else y_late

        def pooled(stat_):
            return 0 if stat_ % 2 else 7 if stat_ == 0 else 4

        def n_added(stat_):
            return sum(pooled(i) for i in range(stat_))

        def n_summed(stat_):
            return KT * stat_ - n_added(stat_)

        def copied(r):
            return 0 if r == 0 else KT + 4 * (r - 1)

        POOL_X = (1, 3, 5)

        def wait_x(eng, r, f):
            n = sum(1 for i in POOL_X if i <= f)
            if f in POOL_X:
                eng.wait_ge(x_pool, len(POOL_X) * r + n)
            else:
                eng.wait_ge(x_dve, (KT - len(POOL_X)) * r + f + 1 - n)

        def wait_low(eng, r, f):
            eng.wait_ge(h_lo_pool if f % 2 else h_lo_dve, KT // 2 * r + f // 2 + 1)

        def shift_col(r):
            layer, ffn = (r + 1) // 2, (r + 1) % 2
            return layer, 24 * ffn

        POOL_LB, POOL_CL = (6, 7), (7, 8)

        block = ctx.enter_context(nc.Block())

        @block.sync
        def _(sp):
            sp.dma_start(s5s[:, 0:3, :], a["s5_par"]).then_inc(par_in, 16)
            def load_ada0(n):
                wait(sp, ada_used, n + 1 - N_ADA0)
                sp.dma_start(ada0_raw[:, n % N_ADA0, :], a["ada_w"][n]).then_inc(ada0_landed[n % N_ADA0], 16)

            sp.wait_ge(small_in, 16 * 7)
            load_ada0(0)
            load_ada0(1)
            sp.dma_start(bc_par[:], a["s5_bc"]).then_inc(bc_in, 16)
            sp.dma_start(u[:], a["x_blocks"].rearrange("p (g b) -> p g b", g=GROUPS)).then_inc(u_in, 16)
            for n in range(2, N_ADA_PE):
                load_ada0(n)
            kt = krows.rearrange("(t p) k -> p t k", p=P)
            def store_rows(b):
                sp.wait_ge(k_ready, b + 1)
                sp.dma_start(kt[:, 4 * b:4 * b + 4, :], kpad[:, 4 * b:4 * b + 4, :]).then_inc(k_stored, 16)
                sp.wait_ge(k_stored, 16 * b + 16)

            def load_toeplitz(piece):
                wait(sp, y5_psum, piece - 1)
                for s in range(BL):
                    src = krows[2 * PO * CG * piece:2 * PO * CG * (piece + 1), CG * s:CG * s + BL * CG]
                    sp.dma_start(toep[piece % 2][CG * s:CG * (s + 1), :, :],
                                 src.rearrange("(g c) k -> c g k", c=CG)).then_inc(toep_in[piece % 2], 16)

            store_rows(0)
            sp.wait_ge(k_psum, 2)
            load_toeplitz(0)
            store_rows(1)
            load_toeplitz(1)
            sp.wait_ge(ada_used, N_ADA_PE)
            for n in range(2):
                sp.dma_start(raw[:, n, :], a["units"][n]).then_inc(raw_landed[n], 16)
            for piece in range(2, OCTS):
                load_toeplitz(piece)
            sp.wait_ge(hx_re, OCTS)
            sp.wait_ge(hx_im, OCTS)
            sp.dma_start(x[:], a["x_t"].rearrange("(t p) s -> p t s", p=P)).then_inc(x_in, 16)

            def load_unit(n, s, half):
                sp.wait_ge(split_lo, n - 1)
                sp.dma_start(raw[:, s, :], a["units"][n]).then_inc(raw_landed[s], 16)

            def load_ada(m, s):
                wait(sp, ada_added, m - 1)
                sp.dma_start(ada_ring[:, s, :], a["ada_w"][m + N_ADA_PE]).then_inc(ada_landed[s], 16)

            sp.wait_ge(y5_psum, OCTS)
            load_ada(0, 0)
            load_ada(1, 1)
            load_unit(2, 0, None)
            load_unit(3, 1, None)

            def load_both(i, s, half):
                load_ada(2 * i + 4, 0)
                load_unit(i + 4, s, half)
                load_ada(2 * i + 5, 1)

            load_ada(2, 0)
            load_ada(3, 1)
            pairs(sp, 0, N_GLU + 10, load_both)
            pairs(sp, N_GLU + 14, U_V + 2, load_unit)
            sp.wait_ge(unit_done, U_V)
            sp.dma_start(pos_i[:], a["positions"].partition_broadcast(P)).then_inc(pos_in, 16)
            sp.dma_start(lam_par[:], a["lam_par"].partition_broadcast(P)).then_inc(lam_in, 16)
            pairs(sp, U_V + 2, U_QK + 4, load_unit)

            def swap(h, s, half):
                sp.wait_ge(raw_copied, 2 * h + 2)
                if not isinstance(h, int) or h >= 1:
                    sp.wait_ge(qk_ready, 2 * h)
                for q in range(4):
                    sp.dma_start(qk_sw[32 * (q ^ 1):32 * (q ^ 1) + 32, :, :],
                                 qk_raw[32 * q:32 * q + 32, :, :]).then_inc(swapped, 16)
                load_unit(h + (U_QK + 4), s, None)

            swap(0, 0, None)
            swap(1, 1, None)
            pairs(sp, 2, HEADS, swap)
            pairs(sp, U_WO + 4, N_UNITS, load_unit)
            for f in range(KT):
                wait_x(sp, 3, f)
                sp.dma_start(out_t[P * f:P * (f + 1), :], x[:, f, :]).then_inc(out_stored, 16)
            sp.wait_ge(out_stored, 16 * KT)

        @block.gpsimd
        def _(pool):
            steps = [0]

            def link(ins):
                steps[0] += 1
                ins.then_inc(pool_step, 1)
                pool.wait_ge(pool_step, steps[0])

            link(nc.gpsimd.memset(ident[:], 0.0))
            nc.gpsimd.affine_select(out=ident[:], in_=ident[:], compare_op=ALU.not_equal, fill=1.0,
                                    base=0, pattern=[[-1, P]], channel_multiplier=1).then_inc(ident_ready, 1)
            nc.gpsimd.memset(ones[:], 1.0).then_inc(const_ready, 1)
            nc.gpsimd.memset(col[:, 0:1], 1.0 / D).then_inc(const_ready, 1)
            nc.gpsimd.memset(rot_c[:, :, 0], 1.0).then_inc(rot_init, 1)
            nc.gpsimd.memset(rot_s[:, :, 0], 0.0).then_inc(rot_init, 1)

            for q in range(8):
                pool.wait_ge(usq_ready, q + 1)
                if q == 0:
                    nc.gpsimd.tensor_copy(ssum[:], sq[:, 0, :]).then_inc(usq_added, 1)
                else:
                    pool.wait_ge(usq_added, q)
                    nc.gpsimd.tensor_tensor(ssum[:], ssum[:], sq[:, q % 2, :], ALU.add).then_inc(usq_added, 1)

            pool.wait_ge(pw_ready, 1)
            pool.wait_ge(bb_ready, 1)
            ta = cb[:, 0, :].rearrange("p (g c) -> p g c", c=CG)
            tb = cb[:, 1, :].rearrange("p (g c) -> p g c", c=CG)

            def over_c(v):
                return v.unsqueeze(2).broadcast_to([P, PAIRS, CG])

            n_rows = {}

            def complex_rows(dr, di, pr, pi, vr, vi, done):
                nc.gpsimd.tensor_tensor(dr, pr, vr, ALU.mult).then_inc(pool_step, 1)
                nc.gpsimd.tensor_tensor(ta, pi, vi, ALU.mult).then_inc(pool_step, 1)
                nc.gpsimd.tensor_tensor(di, pr, vi, ALU.mult).then_inc(pool_step, 1)
                steps[0] += 3
                link(nc.gpsimd.tensor_tensor(tb, pi, vr, ALU.mult))
                nc.gpsimd.tensor_tensor(dr, dr, ta, ALU.subtract).then_inc(done, 1)
                nc.gpsimd.tensor_tensor(di, di, tb, ALU.add).then_inc(done, 1)
                n_rows[done] = n_rows.get(done, 0) + 2
                pool.wait_ge(done, n_rows[done])

            for s in POOL_LB:
                pr, pi = over_c(pw_re[:, s, :]), over_c(pw_im[:, s, :])
                complex_rows(lb_re[:, :, s, :], lb_im[:, :, s, :], pr, pi, bb[:, 0], bb[:, 1], lb_pool)

            pool.wait_ge(rot_first, 1)
            pool.wait_ge(rot_init, 2)
            m = 1
            while m < NB:
                n = min(m, NB - 1 - m)
                t = cb[:, :, :].rearrange("p a s -> p (a s)")[:, 0:PAIRS * n].rearrange("p (g b) -> p g b", b=n)
                em_c = rot_c[:, :, m:m + 1].broadcast_to([P, PAIRS, n])
                em_s = rot_s[:, :, m:m + 1].broadcast_to([P, PAIRS, n])
                oc, os = rot_c[:, :, m + 1:m + 1 + n], rot_s[:, :, m + 1:m + 1 + n]
                ic, is_ = rot_c[:, :, 1:1 + n], rot_s[:, :, 1:1 + n]
                if n > 0:
                    link(nc.gpsimd.tensor_tensor(oc, ic, em_c, ALU.mult))
                    link(nc.gpsimd.tensor_tensor(t, is_, em_s, ALU.mult))
                    link(nc.gpsimd.tensor_tensor(oc, oc, t, ALU.subtract))
                    link(nc.gpsimd.tensor_tensor(os, ic, em_s, ALU.mult))
                    link(nc.gpsimd.tensor_tensor(t, is_, em_c, ALU.mult))
                    link(nc.gpsimd.tensor_tensor(os, os, t, ALU.add))
                m *= 2
            nc.gpsimd.memset(col[:, 7:8], 0.0).then_inc(rot_ready, 1)
            for k in POOL_CL:
                complex_rows(cl_re[:, :, k, :], cl_im[:, :, k, :], over_c(pw_re[:, k, :]),
                             over_c(pw_im[:, k, :]), bc_par[:, 2], bc_par[:, 3], cl_pool)
            pool.wait_ge(small_in, 16 * 7)
            pool.wait_ge(sel_ready, 1)
            tk = cb[:, 0, 0:KT * CG].rearrange("p (t c) -> p t c", c=CG)
            link(nc.gpsimd.tensor_tensor(tk, sel16[:, 0:1, :].broadcast_to([P, KT, CG]),
                                         dskip[:].unsqueeze(2).broadcast_to([P, KT, CG]), ALU.mult))
            for b in range(2):
                pool.wait_ge(k_copied, b + 1)
                k0 = kpad[:, 4 * b:4 * b + 4, (BL - 1) * CG:BL * CG]
                nc.gpsimd.tensor_tensor(k0, k0, tk[:, 4 * b:4 * b + 4, :], ALU.add).then_inc(k_ready, 1)
            pool.wait_ge(k_ready, 2)

            for piece in range(OCTS):
                pool.wait_ge(scanned, piece + 1)
                wait(pool, y5_psum, piece - 1)
                g = slice(PO * piece, PO * piece + PO)
                vr = v_re[:].rearrange("p (g b) -> p g b", g=PO)[:, :, 0:NB - 1]
                vn = v_ni[:].rearrange("p (g b) -> p g b", g=PO)[:, :, 0:NB - 1]
                t = cb[:, 1, :].rearrange("p (g b) -> p g b", g=PO)[:, :, 0:NB - 1]
                hn = hx[piece % 2][:, 1, :, 1:NB]
                nc.gpsimd.tensor_tensor(hn, vn, rot_c[:, g, 0:NB - 1], ALU.mult).then_inc(pool_step, 1)
                steps[0] += 1
                link(nc.gpsimd.tensor_tensor(t, vr, rot_s[:, g, 0:NB - 1], ALU.mult))
                nc.gpsimd.tensor_tensor(hn, hn, t, ALU.subtract).then_inc(hx_im, 1)
                pool.wait_ge(hx_im, piece + 1)

            def add_squares(stat_):
                for f in range(pooled(stat_)):
                    q = KT * stat_ + f
                    pool.wait_ge(sq_ready, q + 1)
                    if f == 0:
                        wait(pool, sq_summed, n_summed(stat_))
                        nc.gpsimd.tensor_copy(ssum[:], sq[:, q % 2, :]).then_inc(sq_added, 1)
                    else:
                        pool.wait_ge(sq_added, n_added(stat_) + f)
                        nc.gpsimd.tensor_tensor(ssum[:], ssum[:], sq[:, q % 2, :], ALU.add).then_inc(sq_added, 1)

            def residual(r):
                for f in POOL_X:
                    pool.wait_ge(gated, KT * r + f + 1)
                    nc.gpsimd.tensor_tensor(x[:, f, :], x[:, f, :], y_of(r)[:, f, :], ALU.add).then_inc(x_pool, 1)

            def h_low(k):
                for f in range(1, KT, 2):
                    pool.wait_ge(h_hi, KT * k + f + 1)
                    nc.gpsimd.tensor_tensor(hlo[:, f, :], cb[:, f // 2 % 2, :], hhi[:, f, :].bitcast(F32),
                                            ALU.subtract).then_inc(h_lo_pool, 1)

            def ffn_low(layer, lo=0, hi=JT):
                def body(j, s, half):
                    pool.wait_ge(gelu_done, j + (layer * JT + 1))
                    pool.wait_ge(conv_done, 2 * j + (2 * layer * JT + 2))
                    nc.gpsimd.tensor_tensor(ca[:, s, :], ca[:, s, :], cb[:, s, :], ALU.mult).then_inc(g_ready, 1)
                    pool.wait_ge(g_hi, j + (layer * JT + 1))
                    nc.gpsimd.tensor_tensor(glo[:, j, :], ca[:, s, :], ghi[:, j, :].bitcast(F32),
                                            ALU.subtract).then_inc(g_lo, 1)
                pairs(pool, lo, hi, body)

            pool.wait_ge(zt_psum, OCTS)
            for i in range(2):
                nc.gpsimd.memset(ada_acc[:, i, :], 0.0).then_inc(acc_clear, 1)
            add_squares(0)
            pool.wait_ge(mod_psum, 2)
            for i in range(2):
                nc.gpsimd.memset(ada_acc[:, i, :], 0.0).then_inc(acc_clear, 1)
            residual(0)
            h_low(0)
            ffn_low(0, 0, 6)
            pool.wait_ge(mod_psum, 3)
            nc.gpsimd.memset(ada_acc[:, 0, :], 0.0).then_inc(acc_clear, 1)
            ffn_low(0, 6, JT)
            add_squares(2)
            residual(1)
            h_low(1)
            nc.gpsimd.memset(maskw[0:1, 0, 0:HD], MASKED).then_inc(mask_ready, 1)
            nc.gpsimd.memset(maskw[0:1, 0, HD:P], 0.0).then_inc(mask_ready, 1)
            nc.gpsimd.memset(maskw[0:1, 1, :], 1.0).then_inc(mask_ready, 1)

            def rope(h, s):
                for i in range(2):
                    pool.wait_ge(raw_copied, 2 * h + (i + 1))
                    if not isinstance(h, int) or h >= 2:
                        pool.wait_ge(s_psum, 4 * h - 4)
                    nc.gpsimd.tensor_tensor(qk[:, s, i, :], qk_raw[:, i, :], cosb[:], ALU.mult).then_inc(cos_mul, 1)
                pool.wait_ge(swapped, 64 * h + 64)
                for i in range(2):
                    nc.gpsimd.tensor_tensor(qk_sw[:, i, :], qk_sw[:, i, :], sinb[:], ALU.mult).then_inc(sw_mul, 1)
                for i in range(2):
                    pool.wait_ge(sw_mul, 2 * h + (i + 1))
                    pool.wait_ge(cos_mul, 2 * h + (i + 1))
                    nc.gpsimd.tensor_tensor(qk[:, s, i, :], qk[:, s, i, :], qk_sw[:, i, :], ALU.add).then_inc(qk_ready, 1)

            def o_low(h, s):
                pool.wait_ge(ot_hi, h + 1)
                nc.gpsimd.tensor_tensor(olo[:, h, :], cb[:, s, :], ohi[:, h, :].bitcast(F32),
                                        ALU.subtract).then_inc(ot_lo, 1)

            pool.sem_inc(ot_lo, 2)
            pool.wait_ge(rope_table, 1)
            for h in range(3):
                rope(h, h % 2)

            def head(h, s, half):
                o_low(h - 4, s)
                rope(h - 1, 1 - s)

            pairs(pool, 4, HEADS, head)
            o_low(HEADS - 4, 0)
            rope(HEADS - 1, 1)
            for h in range(HEADS - 3, HEADS):
                o_low(h, h % 2)
            add_squares(4)
            residual(2)
            h_low(2)
            ffn_low(1)
            add_squares(6)
            residual(3)

        @block.scalar
        def _(act):
            A = nc.scalar.activation
            for i, (dst, name) in enumerate(((cond[:, 0, :], "c_cols"), (ada_b[:], "ada_b"),
                                             (norm_g[:], "norm_g"), (dskip[:], "d_cols"),
                                             (convp[:], "conv_par"), (sub_g[:], "sub_g"),
                                             (rope_c[:], "rope_c"))):
                act.dma_start(dst, a[name]).then_inc(small_in, 16)
            act.wait_ge(par_in, 16)
            A(s5s[:, 3, :], s5s[:, 2, :], ACT.Tanh, scale=1.0 / 16).then_inc(tanh_ready, 1)
            act.wait_ge(small_in, 16 * 7)
            A(cond[:, 1, :], cond[:, 0, :], ACT.Silu).then_inc(cond_ready, 1)
            act.wait_ge(tanh_arg, 1)
            A(s5s[:, 8, :], s5s[:, 6, :], ACT.Tanh, scale=0.5).then_inc(tanh_ready, 1)
            act.wait_ge(sine_arg, 1)
            A(s5s[:, 13:17, :], s5s[:, 9:13, :], ACT.Sin).then_inc(sine_ready, 1)
            act.wait_ge(u_in, 16)
            uf = u[:, :, :].rearrange("p g b -> p (g b)")
            for q in range(8):
                wait(act, usq_added, q - 1)
                A(sq[:, q % 2, :], uf[:, SEQ * q:SEQ * (q + 1)], ACT.Square).then_inc(usq_ready, 1)
            act.wait_ge(bc_in, 16)
            for i, cl in enumerate((cl_re, cl_im)):
                A(cl[:, :, 0, :], bc_par[:, 2 + i], ACT.Copy).then_inc(row0_ready, 1)
            act.wait_ge(bb_ready, 1)
            for i, lb in enumerate((lb_re, lb_im)):
                A(lb[:, :, 0, :], bb[:, i], ACT.Copy).then_inc(row0_ready, 1)
            act.wait_ge(ada_used, N_ADA_PE)
            A(mod_row[:].rearrange("p (b k) -> p b k", b=4), psum[0:1, 0:4, :], ACT.Copy).then_inc(row_copied, 1)
            for t in range(16):
                act.wait_ge(inb_psum, t + 1)
                if t == 8:
                    act.wait_ge(mod0_psum, 1)
                dst = (inb_re if t < 8 else inb_im)[:, 4 * (t % 8):4 * (t % 8) + 4, :]
                A(dst, psum[:, 2 + t % 2, :].rearrange("p (g k) -> p g k", g=4), ACT.Copy).then_inc(inb_ready, 1)

            act.wait_ge(umod_psum, 1)
            uab = s5s[:, 22:26, :].rearrange("p a g -> p (a g)")
            A(uab, psum[:, 6, NB:NB + 2 * GROUPS], ACT.Copy).then_inc(uab_ready, 1)
            act.wait_ge(uab_ready, 1)
            for piece in range(OCTS):
                act.wait_ge(u_normed, piece + 1)
                for g in range(2 * PO * piece, 2 * PO * (piece + 1)):
                    ins = A(u[:, g, :], u[:, g, :], ACT.Identity, scale=uab[:, g:g + 1],
                            bias=uab[:, GROUPS + g:GROUPS + g + 1])
                ins.then_inc(u_ready, 1)
                if piece == 1:
                    act.wait_ge(kzero, 1)
                    for b in range(2):
                        act.wait_ge(k_psum, b + 1)
                        A(kpad[:, 4 * b:4 * b + 4, (BL - 1) * CG:],
                          psum[:, 4 + b, :].rearrange("p (t k) -> p t k", t=4), ACT.Copy).then_inc(k_copied, 1)

            def split_high(n, s, half):
                act.wait_ge(raw_landed[s], 16 * half + 16)
                if not isinstance(n, int) or n >= 2:
                    act.wait_ge(unit_done, n - 1)
                A(whi[:, s, :], raw[:, s, :], ACT.Copy).then_inc(split_hi, 1)

            def z_steps(piece):
                act.wait_ge(y5_psum, piece + 1)
                wait(act, zt_psum, piece)
                for b in range(2):
                    A(z[:, :, 4 * b:4 * b + 4, :].rearrange("p t g c -> p g t c"),
                      psum[:, 4 + b, :].rearrange("p (g t c) -> p g t c", g=4, t=BL),
                      ACT.Gelu_apprx_tanh).then_inc(z_ready, 1)

            def zt_steps(piece):
                for b in range(2):
                    act.wait_ge(zt_psum, piece + 1)
                    for g2 in range(2):
                        dst = hhi[:, 2 * piece + g2, :].rearrange("p (b t) -> p t b", t=BL)
                        src = psum[:, 2 + b, :].rearrange("p (t g b) -> p g t b", t=4, g=2)
                        ins = A(dst[:, 4 * b:4 * b + 4, :], src[:, g2], ACT.Copy)
                    ins.then_inc(zt_hi, 1)

            for piece in range(OCTS):
                z_steps(piece)
                zt_steps(piece)
            act.wait_ge(in_psum, OCTS)
            for n in range(2):
                split_high(n, n, 0)

            def square(stat_, f, src):
                q = KT * stat_ + f
                if q >= 2:
                    st, g = divmod(q - 2, KT)
                    if g < pooled(st):
                        act.wait_ge(sq_added, n_added(st) + g + 1)
                    else:
                        act.wait_ge(sq_summed, n_summed(st) + g + 1 - pooled(st))
                A(sq[:, q % 2, :], src, ACT.Square).then_inc(sq_ready, 1)

            def glu(i, s, half, last=False):
                act.wait_ge(unit_done, i + 1)
                if not isinstance(i, int) or i >= 2:
                    act.wait_ge(y_ready, i - 1)
                A(ca[:, s, :], psum[:, 2 * s + 1, :], ACT.Sigmoid).then_inc(sig_ready, 1)
                if not last:
                    split_high(i + 2, s, half + 1)
                act.wait_ge(y_ready, i + 1)
                if not isinstance(i, int) or i >= 2:
                    act.wait_ge(sq_added, i - 1)
                A(sq[:, s, :], y_glu[:, i, :], ACT.Square).then_inc(sq_ready, 1)
                if last:
                    split_high(i + 2, s, half + 1)

            glu(0, 0, 0)
            glu(1, 1, 0)
            pairs(act, 2, N_GLU - 2, glu)
            glu(N_GLU - 2, 0, N_GLU // 2 - 1)
            glu(N_GLU - 1, 1, N_GLU // 2 - 1, last=True)

            def next_input(r):
                for f in range(KT):
                    wait_x(act, r, f)
                    square(2 * r + 1, f, x[:, f, :])
                layer, c0 = shift_col(r)
                for f in range(KT):
                    n = KT * r + f
                    shift = modt[:, layer, c0 + f:c0 + f + 1]
                    act.wait_ge(t_ready, n + 1)
                    if f % 2:
                        if f >= 5:
                            act.wait_ge(h_lo_pool, KT // 2 * r + f // 2 - 1)
                        A(cb[:, f // 2 % 2, :], ca[:, f % 2, :], ACT.Identity, bias=shift)
                    A(hhi[:, f, :], ca[:, f % 2, :], ACT.Identity, bias=shift).then_inc(h_hi, 1)

            def ffn(layer):
                n0, g0 = U_FIN[layer], layer * JT

                def body(j, s, half):
                    act.wait_ge(unit_done, j + (n0 + 1))
                    if not isinstance(j, int) or j >= 2:
                        act.wait_ge(g_lo, j + (g0 - 1))
                    for i, dst in enumerate((ca, cb)):
                        A(dst[:, s, :], psum[:, 2 * s + i, :], ACT.Identity,
                          scale=convp[:, layer, j, i, 2:3], bias=convp[:, layer, j, i, 3:4]).then_inc(tap2, 1)
                    split_high(j + (n0 + 2), s, half + n0 // 2 + 1)
                    act.wait_ge(conv_done, 2 * j + (2 * g0 + 1))
                    A(ca[:, s, :], ca[:, s, :], ACT.Gelu_apprx_tanh).then_inc(gelu_done, 1)
                    act.wait_ge(g_ready, j + (g0 + 1))
                    A(ghi[:, j, :], ca[:, s, :], ACT.Copy).then_inc(g_hi, 1)

                body(0, 0, 0)
                body(1, 1, 0)
                pairs(act, 2, JT, body)
                r, m0 = 2 * layer + 1, U_FOUT[layer]
                pairs(act, m0 + 2, m0 + 8, split_high)
                for f in range(4):
                    act.wait_ge(y_ready, copied(r) + f + 1)
                    square(2 * r, f, y_late[:, f, :])
                pairs(act, m0 + 8, m0 + 12, split_high)
                if layer == 0:
                    split_high(m0 + 12, 0, m0 // 2 + 6)
                act.wait_ge(unit_done, m0 + 12)
                for f in range(4, KT):
                    square(2 * r, f, psum[:, f - 4, :])
                if layer == 0:
                    split_high(m0 + 13, 1, m0 // 2 + 6)

            next_input(0)
            ffn(0)
            next_input(1)

            n = U_V
            split_high(n + 2, 0, (n + 2) // 2)
            act.wait_ge(rope_arg, 1)
            A(sinb[:], sinb[:], ACT.Sin).then_inc(rope_sin, 1)
            A(cosb[:], cosb[:], ACT.Sin).then_inc(rope_sin, 1)
            act.wait_ge(lam_arg, 1)
            A(col[:, 3:5], col[:, 1:3], ACT.Exp).then_inc(lam_exp, 1)
            for m in range(1, N_V):
                split_high(n + m + 2, m % 2, (n + m + 2) // 2)

            def copy_projections(h, s):
                act.wait_ge(unit_done, h + (U_QK + 1))
                if not isinstance(h, int) or h >= 1:
                    act.wait_ge(cos_mul, 2 * h)
                    act.wait_ge(swapped, 64 * h)
                for i in range(2):
                    A(qk_raw[:, i, :], psum[:, 2 * s + i, :], ACT.Copy,
                      scale=HD ** -0.5 if i == 0 else 1.0).then_inc(raw_copied, 1)

            def half_high(h, s, half, part):
                n = h + (U_QK + 1)
                act.wait_ge(raw_landed[1 - s], 16 * (half + (U_QK // 2 + 1) + s))
                act.wait_ge(unit_done, n - 1)
                c = slice(part * UNIT // 2, (part + 1) * UNIT // 2)
                ins = A(whi[:, 1 - s, c], raw[:, 1 - s, c], ACT.Copy)
                ins.then_inc(split_hi if part else half_hi, 1)

            def out_copy(h, s):
                act.wait_ge(ot_psum, h + 1)
                act.wait_ge(ot_lo, h + 1)
                A(cb[:, s, :], psum[:, 6, :], ACT.Copy, scale=sub_g[:, 0:1]).then_inc(ot_copied, 1)

            def out_high(h, s):
                act.wait_ge(ot_copied, h + 1)
                A(ohi[:, h, :], cb[:, s, :], ACT.Copy).then_inc(ot_hi, 1)

            def exps(h, qt):
                pb, width = qt % 2, (qt + 1) * P
                act.wait_ge(nmax_ready, 4 * h + (qt + 1))
                if not isinstance(h, int) or 4 * h + qt >= 2:
                    act.wait_ge(att_ready, 4 * h + (qt - 1))
                for c in range(2):
                    ins = A(prob[:, pb, c, 0:width], psum[:, 4 + c, 0:width], ACT.Exp,
                            bias=stat[:, 8 * pb + 2 + c:8 * pb + 3 + c],
                            accum_out=stat[:, 8 * pb + 4 + c:8 * pb + 5 + c])
                    ins.then_inc(exp_done, 1)

            def turned(h, qt):
                pb, width = qt % 2, (qt + 1) * P
                act.wait_ge(attt_psum, 4 * h + (qt + 1))
                if not isinstance(h, int) or 4 * h + qt >= 2:
                    act.wait_ge(o_psum, 4 * h + (qt - 1))
                A(att_t[:, pb, 0:width], psum[:, 6, 0:width], ACT.Copy).then_inc(attt_copied, 1)

            def copy_output(h):
                act.wait_ge(o_psum, 4 * h + 4)
                if not isinstance(h, int) or h >= 1:
                    act.wait_ge(on_ready, h)
                A(sq[:, 0, :], psum[:, 7, :], ACT.Square).then_inc(osq_done, 1)
                A(o_sb, psum[:, 7, :], ACT.Copy).then_inc(o_copied, 1)

            def head(h, s, half, first=False, older=True, gemm_on=True, split=True):
                a_ = h - 2
                if older:
                    out_copy(a_ - 2, s)
                exps(a_, 0)
                if not first:
                    turned(a_ - 1, 3)
                if gemm_on:
                    copy_projections(h - 1, 1 - s)
                if older:
                    out_high(a_ - 2, s)
                if not first:
                    copy_output(a_ - 1)
                exps(a_, 1)
                turned(a_, 0)
                if split:
                    half_high(h, s, half, 0)
                exps(a_, 2)
                turned(a_, 1)
                if split:
                    half_high(h, s, half, 1)
                exps(a_, 3)
                turned(a_, 2)

            act.wait_ge(lam_ready, 1)
            copy_projections(0, 0)
            half_high(1, 1, 0, 0)
            half_high(1, 1, 0, 1)
            head(2, 0, 1, first=True, older=False)
            head(3, 1, 1, older=False)
            pairs(act, 4, HEADS, head)
            head(HEADS, 0, HEADS // 2)
            head(HEADS + 1, 1, None, gemm_on=False, split=False)
            out_copy(HEADS - 2, 0)
            turned(HEADS - 1, 3)
            out_high(HEADS - 2, 0)
            copy_output(HEADS - 1)
            out_copy(HEADS - 1, 1)
            out_high(HEADS - 1, 1)
            for m in range(N_WO):
                n = U_WO + m
                act.wait_ge(unit_done, n + 1)
                for f in range(2 * m, 2 * m + 2):
                    if m < 2:
                        act.wait_ge(y_ready, copied(2) + f + 1)
                    square(4, f, y_late[:, f, :] if m < 2 else psum[:, f - 4, :])
                split_high(n + 2, m % 2, (n + 2) // 2)
            next_input(2)
            ffn(1)

        @block.vector
        def _(dve):
            steps = [0]
            TT, TS, STT = nc.vector.tensor_tensor, nc.vector.tensor_scalar, nc.vector.scalar_tensor_tensor

            def count(ins):
                steps[0] += 1
                return ins.then_inc(dve_step, 1)

            def here():
                dve.wait_ge(dve_step, steps[0])

            def link(ins):
                count(ins)
                here()

            def signal(s):
                here()
                dve.sem_inc(s, 1)

            def rsqrt(dst, src, scale, lk):
                w = dst.shape[1]
                v, t = nwt[:, 0, 0:w], nwt[:, 1, 0:w]
                lk(TS(v, src, scale, EPS, ALU.mult, ALU.add))
                lk(TS(t.bitcast(I32), v.bitcast(I32), 1, None, ALU.logical_shift_right))
                lk(TS(dst.bitcast(I32), t.bitcast(I32), -1.0, RSQRT_MAGIC, ALU.mult, ALU.add))
                for i in range(3):
                    lk(TT(t, dst, dst, ALU.mult))
                    lk(STT(t, t, -0.5, v, ALU.mult, ALU.mult))
                    lk(STT(dst, t, 1.5, dst, ALU.add, ALU.mult))

            def reduced(dst_sin, dst_cos, ang, t, lk):
                lk(TS(t, ang, 1.0 / TWO_PI, ROUND, ALU.mult, ALU.add))
                lk(TS(t, t, -ROUND, None, ALU.add))
                lk(STT(dst_sin, t, -PI_A, ang, ALU.mult, ALU.add))
                lk(STT(dst_sin, t, -PI_B, dst_sin, ALU.mult, ALU.add))
                lk(STT(dst_sin, t, -PI_C, dst_sin, ALU.mult, ALU.add))
                lk(TS(dst_sin, dst_sin, PI_CLAMP, -PI_CLAMP, ALU.min, ALU.max))
                lk(STT(dst_cos, dst_sin, -1.0, dst_sin, ALU.mult, ALU.max))
                lk(TS(dst_cos, dst_cos, -1.0, math.pi / 2, ALU.mult, ALU.add))

            dve.wait_ge(ident_ready, 1)
            link(nc.vector.tensor_reduce(sel16[:, 0, :], ident[:].rearrange("p (b c) -> p c b", c=CG), AXX, ALU.add))
            link(nc.vector.tensor_copy(sel16[:, 1:, :], sel16[:, 0:1, :].broadcast_to([P, BL - 1, CG])))
            link(nc.vector.tensor_reduce(gmask[:], ident[:].rearrange("p (b c) -> p b c", c=CG), AXX, ALU.add))
            signal(sel_ready)
            count(TS(blk16[:], gmask[:].unsqueeze(2).broadcast_to([P, KT, CG]), 1.0 / D, None, ALU.mult))
            count(nc.vector.memset(bd[0][:], 0.0))
            count(nc.vector.memset(bd[1][:], 0.0))
            nc.vector.memset(kpad[:, :, 0:(BL - 1) * CG], 0.0).then_inc(kzero, 1)

            S = [s5s[:, i, :] for i in range(32)]
            a_re, a_im = S[0], S[1]
            dt, lam_re, dre, dim_ = S[4], S[5], S[6], S[7]
            t0, t1, t2, t3 = S[28], S[29], S[30], S[31]

            def exp_from_tanh(dst, t):
                link(TS(t0, t, -1.0, 1.0, ALU.mult, ALU.add))
                link(nc.vector.reciprocal(t1, t0))
                link(TS(t0, t, 1.0, None, ALU.add))
                link(TT(dst, t0, t1, ALU.mult))

            dve.wait_ge(tanh_ready, 1)
            exp_from_tanh(dt, S[3])
            for i in range(3):
                link(TT(dt, dt, dt, ALU.mult))
            link(TS(lam_re, a_re, LAM_MAX, None, ALU.min))
            TT(dre, lam_re, dt, ALU.mult).then_inc(tanh_arg, 1)
            link(TT(dim_, a_im, dt, ALU.mult))
            link(TS(S[27], dim_, float(BL), None, ALU.mult))
            reduced(S[9], S[10], dim_, t0, link)
            reduced(S[11], S[12], S[27], t0, link)
            signal(sine_arg)
            dve.wait_ge(tanh_ready, 2)
            mag = S[17]
            exp_from_tanh(mag, S[8])
            link(TT(S[18], mag, mag, ALU.mult))
            link(TT(S[18], S[18], S[18], ALU.mult))
            link(TT(S[18], S[18], S[18], ALU.mult))
            dve.wait_ge(sine_ready, 1)
            count(nc.vector.memset(pw_re[:, 0, :], 1.0))
            count(nc.vector.memset(pw_im[:, 0, :], 0.0))
            count(TT(pw_re[:, 1, :], mag, S[14], ALU.mult))
            link(TT(pw_im[:, 1, :], mag, S[13], ALU.mult))
            dve.wait_ge(rot_init, 2)
            nc.vector.tensor_copy(rot_s[:, :, 1], S[15]).then_inc(rot_copy, 1)
            dve.wait_ge(rot_copy, 1)
            nc.vector.tensor_copy(rot_c[:, :, 1], S[16]).then_inc(rot_first, 1)
            for m in (1, 2, 4):
                def over(v):
                    return v.broadcast_to([P, m, PAIRS])
                qr, qi = over(pw_re[:, m:m + 1, :]), over(pw_im[:, m:m + 1, :])
                pr, pi = pw_re[:, 1:1 + m, :], pw_im[:, 1:1 + m, :]
                nr, ni = pw_re[:, m + 1:2 * m + 1, :], pw_im[:, m + 1:2 * m + 1, :]
                ta, tb = s5s[:, 20:20 + m, :], s5s[:, 24:24 + m, :]
                count(TT(nr, pr, qr, ALU.mult))
                count(TT(ta, pi, qi, ALU.mult))
                count(TT(ni, pr, qi, ALU.mult))
                link(TT(tb, pi, qr, ALU.mult))
                count(TT(nr, nr, ta, ALU.subtract))
                link(TT(ni, ni, tb, ALU.add))
            f_re, f_im = S[20], S[21]
            count(TT(t0, lam_re, lam_re, ALU.mult))
            link(TT(t1, a_im, a_im, ALU.mult))
            link(TT(t0, t0, t1, ALU.add))
            link(nc.vector.reciprocal(t0, t0))
            link(TS(t1, pw_re[:, 1, :], -1.0, None, ALU.add))
            count(TT(f_re, t1, lam_re, ALU.mult))
            link(TT(t2, pw_im[:, 1, :], a_im, ALU.mult))
            link(TT(f_re, f_re, t2, ALU.add))
            count(TT(f_re, f_re, t0, ALU.mult))
            count(TT(f_im, pw_im[:, 1, :], lam_re, ALU.mult))
            link(TT(t2, t1, a_im, ALU.mult))
            link(TT(f_im, f_im, t2, ALU.subtract))
            link(TT(f_im, f_im, t0, ALU.mult))
            signal(pw_ready)

            def over_c(v):
                return v.unsqueeze(2).broadcast_to([P, PAIRS, CG])

            ta = ca[:, 0, :].rearrange("p (g c) -> p g c", c=CG)
            tb = ca[:, 1, :].rearrange("p (g c) -> p g c", c=CG)

            def complex_rows(dr, di, pr, pi, vr, vi, done=None):
                count(TT(dr, pr, vr, ALU.mult))
                count(TT(ta, pi, vi, ALU.mult))
                count(TT(di, pr, vi, ALU.mult))
                link(TT(tb, pi, vr, ALU.mult))
                count(TT(dr, dr, ta, ALU.subtract))
                link(TT(di, di, tb, ALU.add))

            dve.wait_ge(bc_in, 16)
            complex_rows(bb[:, 0], bb[:, 1], over_c(f_re), over_c(f_im), bc_par[:, 0], bc_par[:, 1])
            for g2 in range(2):
                rows = slice(64 * g2, 64 * g2 + 64)
                cols = slice(CG * g2, CG * g2 + CG)
                nc.vector.tensor_copy(bd[0][rows, :, cols], bb[rows, 0]).then_inc(bd_ready, 1)
                TS(bd[1][rows, :, cols], bb[rows, 1], -1.0, None, ALU.mult).then_inc(bd_ready, 1)
            dve.wait_ge(bd_ready, 4)
            signal(bb_ready)
            dve.wait_ge(usq_added, 8)
            us = nwt[:, 2, :]
            nc.vector.tensor_reduce(us, ssum[:].rearrange("p (g b) -> p b g", g=8), AXX, ALU.add).then_inc(usum_ready, 1)
            for s in range(1, BL):
                if s not in POOL_LB:
                    complex_rows(lb_re[:, :, s, :], lb_im[:, :, s, :], over_c(pw_re[:, s, :]),
                                 over_c(pw_im[:, s, :]), bb[:, 0], bb[:, 1])
            signal(lb_dve)
            def modulation(layer, chunks):
                for ch in chunks:
                    c = slice(KT * ch, KT * ch + KT)
                    link(TT(modt[:, layer, c], psum[:, 7, 48 * layer + KT * ch:48 * layer + KT * ch + KT],
                            ada_b[:, layer, c], ALU.add))
                for ch in chunks:
                    sub, kind = ch // 3, ch % 3
                    c = slice(KT * ch, KT * ch + KT)
                    if kind == 1:
                        link(STT(pre_a[:, 2 * layer + sub, :], modt[:, layer, c], 1.0,
                                 norm_g[:, layer, 2 * sub, :], ALU.add, ALU.mult))
                    if kind == 2:
                        link(TT(gate[:, 2 * layer + sub, :], modt[:, layer, c],
                                norm_g[:, layer, 2 * sub + 1, :], ALU.mult))

            dve.wait_ge(uvar_psum, 1)
            urs = nwt[:, 3, :]
            rsqrt(urs, psum[:, 6, 0:NB], 1.0, link)
            G = 2 * PO
            for piece in range(OCTS):
                g = slice(G * piece, G * piece + G)
                TT(u[:, g, :], u[:, g, :], urs.unsqueeze(1).broadcast_to([P, G, NB]),
                   ALU.mult).then_inc(u_normed, 1)

            def output_powers(ks):
                for k in ks:
                    if k not in POOL_CL:
                        complex_rows(cl_re[:, :, k, :], cl_im[:, :, k, :], over_c(pw_re[:, k, :]),
                                     over_c(pw_im[:, k, :]), bc_par[:, 2], bc_par[:, 3])

            dve.wait_ge(mod0_psum, 1)
            modulation(0, (0, 1))
            um = ca[:, 0, 0:2 * GROUPS].rearrange("p (a t g) -> p a t g", a=2, t=KT)
            for i, v in enumerate((pre_a[:, 0, :], modt[:, 0, 0:KT])):
                TT(um[:, i], v.unsqueeze(2).broadcast_to([P, KT, BL]),
                   gmask[:].unsqueeze(1).broadcast_to([P, KT, BL]), ALU.mult).then_inc(umod_rhs, 1)
            dve.wait_ge(umod_psum, 1)

            output_powers(range(1, BL // 2))
            signal(cl_dve)
            output_powers(range(BL // 2, BL + 1))
            signal(cl_dve)
            dve.wait_ge(cl_pool, 2 * len(POOL_CL))
            dve.wait_ge(row0_ready, 4)

            for i in range(2):
                count(nc.vector.memset(hx[i][:, :, :, 0], 0.0))
            dve.wait_ge(rot_ready, 1)
            W = PO * NB

            def flat(v):
                return v.rearrange("p g b -> p (g b)")

            def split_low(n, s, half):
                dve.wait_ge(split_hi, n + 1)
                TT(wlo[:, s, :], raw[:, s, :], whi[:, s, :].bitcast(F32), ALU.subtract).then_inc(split_lo, 1)

            def zt_low(piece):
                for b in range(2):
                    dve.wait_ge(zt_hi, 2 * piece + b + 1)
                    for g2 in range(2):
                        src = psum[:, 2 + b, :].rearrange("p (t g b) -> p g t b", t=4, g=2)[:, g2]
                        dst = hlo[:, 2 * piece + g2, :].rearrange("p (b t) -> p t b", t=BL)
                        hi = hhi[:, 2 * piece + g2, :].bitcast(F32).rearrange("p (b t) -> p t b", t=BL)
                        ins = TT(dst[:, 4 * b:4 * b + 4, :], src, hi[:, 4 * b:4 * b + 4, :], ALU.subtract)
                    ins.then_inc(zt_lo, 1)

            for piece in range(OCTS):
                g = slice(PO * piece, PO * piece + PO)
                rc, rs = rot_c[:, g, :], rot_s[:, g, :]
                here()
                link(nc.vector.tensor_copy(decay[:], S[18][:, g].unsqueeze(2).broadcast_to([P, PO, NB])))
                count(nc.vector.memset(decay[:, :, 0], 0.0))
                dve.wait_ge(in_psum, piece + 1)
                ire = psum[:, 0, :].rearrange("p (g b) -> p g b", g=PO)
                iim = psum[:, 1, :].rearrange("p (g b) -> p g b", g=PO)
                vr = v_re[:].rearrange("p (g b) -> p g b", g=PO)
                vn = v_ni[:].rearrange("p (g b) -> p g b", g=PO)
                t_a = ca[:, 0, :].rearrange("p (g b) -> p g b", g=PO)
                t_b = ca[:, 1, :].rearrange("p (g b) -> p g b", g=PO)
                wait(dve, hx_im, piece)
                count(TT(vr, ire, rc, ALU.mult))
                count(TT(t_a, iim, rs, ALU.mult))
                count(TT(vn, ire, rs, ALU.mult))
                TT(t_b, iim, rc, ALU.mult).then_inc(in_read, 1)
                dve.wait_ge(in_read, piece + 1)
                here()
                count(TT(vr, vr, t_a, ALU.add))
                link(TT(vn, vn, t_b, ALU.subtract))
                count(nc.vector.tensor_tensor_scan(v_re[:], flat(decay[:]), v_re[:], 0.0, ALU.mult, ALU.add))
                link(nc.vector.tensor_tensor_scan(v_ni[:], flat(decay[:]), v_ni[:], 0.0, ALU.mult, ALU.add))
                signal(scanned)
                wait(dve, y5_psum, piece - 1)
                n1 = NB - 1
                hr, ta1 = hx[piece % 2][:, 0, :, 1:NB], t_a[:, :, 0:n1]
                count(TT(hr, vr[:, :, 0:n1], rc[:, :, 0:n1], ALU.mult))
                link(TT(ta1, vn[:, :, 0:n1], rs[:, :, 0:n1], ALU.mult))
                TT(hr, hr, ta1, ALU.add).then_inc(hx_re, 1)
                dve.wait_ge(hx_re, piece + 1)
                if piece >= 2:
                    zt_low(piece - 2)
            zt_low(OCTS - 2)
            zt_low(OCTS - 1)
            for n in range(2):
                split_low(n, n, 0)

            def ada_step(m, e, k, slot):
                dve.wait_ge(ada_landed[e], 16 * k[1])
                wait(dve, ada_added, m)
                STT(ada_acc[:, slot, :], ada_ring[:, e, :], cond[:, 1, bass.ds(k[0], 1)],
                    ada_acc[:, slot, :], ALU.mult, ALU.add).then_inc(ada_added, 1)

            def glu_ada(m, k, e):
                ada_step(m, e, (k, k + 1), e)

            dve.wait_ge(acc_clear, 2)
            glu_ada(0, 0, 0)
            glu_ada(1, 0, 1)

            def glu(i, s, half, ada=True):
                dve.wait_ge(sig_ready, i + 1)
                TT(y_glu[:, i, :], psum[:, 2 * s, :], ca[:, s, :], ALU.mult).then_inc(y_ready, 1)
                if ada:
                    glu_ada(2 * i + 2, i + 1, 0)
                if not isinstance(i, int) or i < N_GLU - 1:
                    split_low(i + 2, s, half)
                if ada:
                    glu_ada(2 * i + 3, i + 1, 1)

            pairs(dve, 0, N_GLU - 2, glu)
            glu(N_GLU - 2, 0, None)
            glu(N_GLU - 1, 1, None, ada=False)

            def spread_rsqrt(stat_):
                dve.wait_ge(sq_summed, n_summed(stat_ + 1))
                rsqrt(stat[:, 16:16 + QT], psum[:, 4, 0:QT], 1.0, link)
                TT(diag[:], ident[:].unsqueeze(1).broadcast_to([P, QT, P]),
                   stat[:, 16:16 + QT].unsqueeze(2).broadcast_to([P, QT, P]), ALU.mult).then_inc(diag_ready, 1)
                dve.wait_ge(rs_psum, stat_ + 1)

            def post_norm(r):
                for f in range(4, KT if r else 0):
                    dve.wait_ge(sq_ready, 2 * r * KT + f + 1)
                    count(nc.vector.tensor_copy(y_late[:, f, :], psum[:, f - 4, :]))
                spread_rsqrt(2 * r)
                if r == 0:
                    dve.wait_ge(mod_psum, 2)
                    modulation(0, (2, 3, 4, 5))
                if r == 0:
                    dve.wait_ge(x_in, 16)
                y = y_of(r)

                def add(f):
                    if f not in POOL_X:
                        dve.wait_ge(gated, KT * r + f + 1)
                        TT(x[:, f, :], x[:, f, :], y[:, f, :], ALU.add).then_inc(x_dve, 1)

                for f in range(KT):
                    STT(y[:, f, :], y[:, f, :], gate[:, r, f:f + 1], psum[:, 5, :], ALU.mult,
                        ALU.mult).then_inc(gated, 1)
                    if f:
                        add(f - 1)
                add(KT - 1)

            def pre_norm(r):
                spread_rsqrt(2 * r + 1)
                layer, c0 = shift_col(r)

                def low(f):
                    dve.wait_ge(h_hi, KT * r + f + 1)
                    STT(hlo[:, f, :], ca[:, f % 2, :], modt[:, layer, c0 + f:c0 + f + 1],
                        hhi[:, f, :].bitcast(F32), ALU.add, ALU.subtract).then_inc(h_lo_dve, 1)

                for f in range(KT):
                    wait_x(dve, r, f)
                    if f >= 2:
                        dve.wait_ge(h_hi, KT * r + f - 1)
                        if f % 2 == 0:
                            dve.wait_ge(h_lo_dve, KT // 2 * r + f // 2)
                    STT(ca[:, f % 2, :], x[:, f, :], pre_a[:, r + 1, f:f + 1], psum[:, 5, :], ALU.mult,
                        ALU.mult).then_inc(t_ready, 1)
                    if f % 2:
                        low(f - 1)

            def ffn(layer):
                n0, g0 = U_FIN[layer], layer * JT

                def body(j, s, half, third=None):
                    for i, dst in enumerate((ca, cb)):
                        dve.wait_ge(tap2, 2 * j + (2 * g0 + i + 1))
                        STT(dst[:, s, 1:], psum[:, 2 * s + i, 0:SEQ - 1], convp[:, layer, j, i, 1:2],
                            dst[:, s, 1:], ALU.mult, ALU.add).then_inc(conv_step, 1)
                    for i, dst in enumerate((ca, cb)):
                        dve.wait_ge(conv_step, 2 * j + (2 * g0 + i + 1))
                        STT(dst[:, s, 2:], psum[:, 2 * s + i, 0:SEQ - 2], convp[:, layer, j, i, 0:1],
                            dst[:, s, 2:], ALU.mult, ALU.add).then_inc(conv_done, 1)

                    def ada(e):
                        if third is not None:
                            k = 2 * j + (e - 8 * third)
                            ada_step(2 * j + (2 * N_GLU + e), e, (k, j + (N_GLU + 1)), third % 2)

                    ada(0)
                    split_low(j + (n0 + 2), s, half)
                    ada(1)

                if layer == 0:
                    for third in range(3):
                        dve.wait_ge(acc_clear, (4, 4, 5)[third])
                        pairs(dve, 4 * third, 4 * third + 4, partial(body, third=third))
                    pairs(dve, 12, 16, body)
                    dve.wait_ge(mod_psum, 5)
                    modulation(1, range(6))
                    signal(mod_ready)
                    pairs(dve, 16, JT, body)
                else:
                    pairs(dve, 0, JT, body)
                r, m0 = 2 * layer + 1, U_FOUT[layer]
                pairs(dve, m0 + 2, m0 + 8, split_low)
                dve.wait_ge(unit_done, m0 + 6)
                for f in range(4):
                    nc.vector.tensor_copy(y_late[:, f, :], psum[:, 4 + f, :]).then_inc(y_ready, 1)
                pairs(dve, m0 + 8, m0 + 12, split_low)
                if layer == 0:
                    split_low(m0 + 12, 0, None)

            post_norm(0)
            pre_norm(0)
            split_low(N_GLU + 1, 1, None)
            ffn(0)
            post_norm(1)
            pre_norm(1)
            split_low(U_V + 1, 1, None)

            def value_copies(m):
                dve.wait_ge(unit_done, U_V + m + 1)
                for b in range(2):
                    nc.vector.tensor_copy(v_sb[:, 2 * b:2 * b + 2, 256 * m:256 * m + 256],
                                          psum[:, 2 * (m % 2) + b, :].rearrange("p (t e) -> p t e", t=2)).then_inc(v_copied, 1)

            split_low(U_V + 2, 0, None)
            dve.wait_ge(pos_in, 16)
            ang, rt = prob[:, 0, 0, :], prob[:, 0, 1, :]
            link(nc.vector.tensor_copy(ang, pos_i[:]))
            link(TS(ang, ang, rope_c[:, 0:1], None, ALU.mult))
            reduced(sinb[:], cosb[:], ang, rt, link)
            signal(rope_arg)
            dve.wait_ge(lam_in, 16)
            lp = prob[:, 1, 0, 0:2 * HD].rearrange("p (a d) -> p a d", a=2)
            lq = lam_par[:].rearrange("p (a b d) -> p a b d", a=2, b=2)
            link(TT(lp, lq[:, :, 0, :], lq[:, :, 1, :], ALU.mult))
            nc.vector.tensor_reduce(col[:, 1:3], lp, AXX, ALU.add).then_inc(lam_arg, 1)
            value_copies(0)
            dve.wait_ge(rope_sin, 2)
            TS(sinb[:], sinb[:], rope_c[:, 1:2], None, ALU.mult).then_inc(rope_table, 1)
            dve.wait_ge(lam_exp, 1)
            link(TT(col[:, 5:6], col[:, 4:5], col[:, 3:4], ALU.subtract))
            link(TS(col[:, 6:7], col[:, 5:6], -LAMBDA_INIT, None, ALU.add))
            TS(sub_g[:], sub_g[:], 1.0 - LAMBDA_INIT, None, ALU.mult).then_inc(lam_ready, 1)
            for m in range(1, N_V):
                split_low(U_V + m + 2, m % 2, None)
                value_copies(m)

            def row_max(h, qt):
                pb, width = qt % 2, (qt + 1) * P
                dve.wait_ge(s_psum, 4 * h + (qt + 1))
                nc.vector.tensor_reduce(stat[:, 8 * pb + 2:8 * pb + 4], psum[:, 4:6, 0:width], AXX, ALU.max,
                                        negate=True).then_inc(nmax_ready, 1)

            def combine(h, qt):
                pb, width = qt % 2, (qt + 1) * P
                st = stat[:, 8 * pb:8 * pb + 8]
                dve.wait_ge(exp_done, 8 * h + (2 * qt + 2))
                nc.vector.reciprocal(st[:, 6:8], st[:, 4:6]).then_inc(att_step, 1)
                dve.wait_ge(att_step, 8 * h + (2 * qt + 1))
                TS(prob[:, pb, 1, 0:width], prob[:, pb, 1, 0:width], st[:, 7:8], col[:, 6:7],
                   ALU.mult, ALU.mult).then_inc(att_step, 1)
                dve.wait_ge(att_step, 8 * h + (2 * qt + 2))
                if not isinstance(h, int) or 4 * h + qt >= 2:
                    dve.wait_ge(attt_psum, 4 * h + (qt - 1))
                STT(att[:, pb, 0:width], prob[:, pb, 0, 0:width], st[:, 6:7],
                    prob[:, pb, 1, 0:width], ALU.mult, ALU.add).then_inc(att_ready, 1)

            def head_norm(h):
                k = [0]

                def lk(ins):
                    k[0] += 1
                    ins.then_inc(hn_step, 1)
                    dve.wait_ge(hn_step, HEAD_STEPS * h + k[0])
                dve.wait_ge(osq_done, h + 1)
                v, d, t = nwt[:, 2, 0:QT], nwt[:, 3, 0:QT], nwt[:, 1, 0:QT]
                lk(nc.vector.tensor_reduce(v, sq[:, 0, :].rearrange("p (t e) -> p t e", t=QT), AXX, ALU.add))
                lk(TS(v, v, 1.0 / P, EPS, ALU.mult, ALU.add))
                lk(TS(t.bitcast(I32), v.bitcast(I32), 1, None, ALU.logical_shift_right))
                lk(TS(d.bitcast(I32), t.bitcast(I32), -1.0, RSQRT_MAGIC, ALU.mult, ALU.add))
                yield
                for i in range(3):
                    lk(TT(t, d, d, ALU.mult))
                    lk(STT(t, t, -0.5, v, ALU.mult, ALU.mult))
                    lk(STT(d, t, 1.5, d, ALU.add, ALU.mult))
                    if i == 0:
                        yield
                assert k[0] == HEAD_STEPS
                dve.wait_ge(o_copied, h + 1)
                if not isinstance(h, int) or h >= 1:
                    dve.wait_ge(ot_psum, h)
                TT(on[:], o_sb.rearrange("p (t e) -> p t e", t=QT),
                   d.unsqueeze(2).broadcast_to([P, QT, P]), ALU.mult).then_inc(on_ready, 1)
                yield

            def half_low(h, s, part):
                n = h + (U_QK + 1)
                c = slice(part * UNIT // 2, (part + 1) * UNIT // 2)
                if part:
                    dve.wait_ge(split_hi, n + 1)
                else:
                    dve.wait_ge(half_hi, h)
                ins = TT(wlo[:, 1 - s, c], raw[:, 1 - s, c], whi[:, 1 - s, c].bitcast(F32), ALU.subtract)
                ins.then_inc(split_lo if part else half_lo, 1)

            def head(h, s, half, first=False, split=True):
                a_ = h - 2
                norm = iter(()) if first else head_norm(a_ - 1)
                row_max(a_, 0)
                combine(a_, 0)
                row_max(a_, 1)
                next(norm, None)
                combine(a_, 1)
                row_max(a_, 2)
                if split:
                    half_low(h, s, 0)
                next(norm, None)
                combine(a_, 2)
                row_max(a_, 3)
                next(norm, None)
                if split:
                    half_low(h, s, 1)
                combine(a_, 3)

            half_low(1, 1, 0)
            half_low(1, 1, 1)
            head(2, 0, None, first=True)
            head(3, 1, None)
            pairs(dve, 4, HEADS, head)
            head(HEADS, 0, None)
            head(HEADS + 1, 1, None, split=False)
            for _ in head_norm(HEADS - 1):
                pass
            for m in range(N_WO):
                n = U_WO + m
                dve.wait_ge(unit_done, n + 1)
                for f in range(2 * m, 2 * m + 2 if m < 2 else 0):
                    nc.vector.tensor_copy(y_late[:, f, :], psum[:, f, :]).then_inc(y_ready, 1)
                if m < N_WO - 1:
                    split_low(n + 2, m % 2, None)
            post_norm(2)
            pre_norm(2)
            split_low(U_FIN[1] + 1, 1, None)
            ffn(1)
            post_norm(3)

        @block.tensor
        def _(pe):
            M = nc.tensor.matmul

            def ada_unit(k, s):
                pe.wait_ge(ada0_landed[s], 16 * (k // N_ADA0) + 16)
                for b in range(4):
                    ins = M(psum[0:1, b, :], cond[:, 1, k:k + 1], ada0_raw[:, s, 512 * b:512 * b + 512],
                            start=(k == 0), stop=(k == KT - 1))
                ins.then_inc(ada_used, 1)

            def reduce_acc(slot, col0):
                for f in range(THIRD):
                    ins = M(psum[:, 7, col0 + f:col0 + f + 1], ada_acc[:, slot, P * f:P * f + P],
                            ones[:, 0:1], start=True, stop=True)
                ins.then_inc(mod_psum, 1)

            pe.wait_ge(cond_ready, 1)
            for n in range(N_ADA_PE):
                ada_unit(n, n % N_ADA0)
                if n == 5:
                    pe.wait_ge(usum_ready, 1)
                    M(psum[:, 6, 0:NB], blk16[:].rearrange("p g c -> p (g c)"), nwt[:, 2, :],
                      start=True, stop=True).then_inc(uvar_psum, 1)
            pe.wait_ge(row_copied, 1)
            for f in range(THIRD):
                ins = M(psum[:, 7, f:f + 1], mod_row[0:1, P * f:P * f + P], ones[0:1, 0:1],
                        start=True, stop=True)
            ins.then_inc(mod0_psum, 1)
            pe.wait_ge(lb_pool, 2 * len(POOL_LB))
            pe.wait_ge(lb_dve, 1)
            pe.wait_ge(row0_ready, 4)
            for t in range(16):
                wait(pe, inb_ready, t - 1)
                lb = lb_re if t < 8 else lb_im
                for q in range(4):
                    ins = nc.tensor.transpose(psum[:, 2 + t % 2, P * q:P * q + P],
                                              lb[:, 4 * (t % 8) + q].rearrange("p t c -> p (t c)"), ident[:])
                ins.then_inc(inb_psum, 1)
            pe.wait_ge(umod_rhs, 2)
            M(psum[:, 6, NB:NB + 2 * GROUPS], sel16[:].rearrange("p t c -> p (t c)"),
              ca[:, 0, 0:2 * GROUPS], start=True, stop=True).then_inc(umod_psum, 1)
            pe.wait_ge(inb_ready, 16)

            def inputs(piece):
                pe.wait_ge(u_ready, piece + 1)
                wait(pe, in_read, piece)
                for i, inb in enumerate((inb_re, inb_im)):
                    for j in range(PO):
                        for g2 in range(2):
                            gp = PO * piece + j
                            ins = M(psum[64 * g2:64 * g2 + 64, i, NB * j:NB * j + NB],
                                    inb[:, gp, 64 * g2:64 * g2 + 64], u[:, 2 * gp + g2, :],
                                    start=True, stop=True)
                ins.then_inc(in_psum, 1)

            def outputs(piece):
                pe.wait_ge(toep_in[piece % 2], 16 * BL * (piece // 2 + 1))
                wait(pe, z_ready, 2 * piece)
                pe.wait_ge(hx_re, piece + 1)
                pe.wait_ge(hx_im, piece + 1)
                if piece == 0:
                    pe.wait_ge(k_copied, 2)
                for j in range(PO):
                    gp = PO * piece + j
                    for g2 in range(2):
                        rows = slice(64 * g2, 64 * g2 + 64)
                        out = psum[rows, 4 + j // 4, P * (j % 4):P * (j % 4) + P]
                        M(out, u[:, 2 * gp + g2, :], toep[piece % 2][:, 2 * j + g2, :], start=True,
                          stop=False, skip_group_check=True)
                        for i, cl in enumerate((cl_re, cl_im)):
                            ins = M(out, hx[piece % 2][rows, i, j, 0:NB],
                                    cl[rows, gp, 1:, :].rearrange("p k c -> p (k c)"), start=False,
                                    stop=(i == 1), skip_group_check=True)
                ins.then_inc(y5_psum, 1)

            def back(piece):
                pe.wait_ge(z_ready, 2 * piece + 2)
                wait(pe, zt_lo, 2 * piece)
                for t in range(BL):
                    ins = nc.tensor.transpose(psum[:, 2 + t // 4, P * (t % 4):P * (t % 4) + P],
                                              z[:, t].rearrange("p g c -> p (g c)"), ident[:])
                ins.then_inc(zt_psum, 1)

            inputs(0)
            for kh in range(2):
                pe.wait_ge(cl_dve, kh + 1)
                if kh:
                    pe.wait_ge(cl_pool, 2)
                ks = slice(kh * BL // 2, (kh + 1) * BL // 2)
                for t in range(KT):
                    for q in range(4):
                        gp = 4 * t + q
                        c0 = P * (t % 4) + kh * P // 2
                        out = psum[32 * q:32 * q + 32, 4 + t // 4, c0:c0 + P // 2]
                        for i, cl in enumerate((cl_re, cl_im)):
                            ins = M(out, bd[i][:, gp, :], cl[:, gp, ks, :].rearrange("p k c -> p (k c)"),
                                    start=(i == 0), stop=(i == 1), skip_group_check=True)
                    if kh and t % 4 == 3:
                        ins.then_inc(k_psum, 1)
            pe.wait_ge(cl_pool, 2 * len(POOL_CL))
            for piece in range(OCTS):
                if piece + 1 < OCTS:
                    inputs(piece + 1)
                if piece:
                    back(piece - 1)
                outputs(piece)
            back(OCTS - 1)

            def gemm_step(s, step, hi, lo, n_cols=None):
                half, k = divmod(step, KT)
                w = slice(P * step, P * step + P)
                out = psum[:, 2 * s + half, :]
                M(out, whi[:, s, w], hi[:, k, :], start=(k == 0), stop=False)
                M(out, whi[:, s, w], lo[:, k, :], start=False, stop=False)
                return M(out, wlo[:, s, w], hi[:, k, :], start=False, stop=(k == KT - 1))

            def gemm(n, s, hi, lo, ready=None):
                pe.wait_ge(split_lo, n + 1)
                if ready:
                    for k in range(KT):
                        ready(k)
                        for half in range(2):
                            ins = gemm_step(s, KT * half + k, hi, lo)
                else:
                    for step in range(2 * KT):
                        ins = gemm_step(s, step, hi, lo)
                ins.then_inc(unit_done, 1)

            def glu(i, s, half):
                if not isinstance(i, int) or i >= 2:
                    pe.wait_ge(y_ready, i - 1)
                gemm(i, s, hhi, hlo)

            pe.wait_ge(zt_lo, 2 * OCTS)
            glu(0, 0, 0)
            glu(1, 1, 0)
            pairs(pe, 2, N_GLU, glu)

            def statistic(stat_):
                tiles = [ssum[:]] if pooled(stat_) else []
                if tiles:
                    pe.wait_ge(sq_added, n_added(stat_ + 1))
                direct = range(pooled(stat_), KT)
                for i, (tile_, f) in enumerate([(v, None) for v in tiles]
                                               + [(sq[:, f % 2, :], f) for f in direct]):
                    if f is not None:
                        pe.wait_ge(sq_ready, KT * stat_ + f + 1)
                    for t in range(QT):
                        ins = M(psum[:, 4, t:t + 1], tile_[:, P * t:P * t + P], col[:, 0:1],
                                start=(i == t == 0), stop=(f == KT - 1), skip_group_check=True)
                    if f is not None:
                        ins.then_inc(sq_summed, 1)
                if stat_ == 0:
                    reduce_acc(1, 2 * THIRD)
                pe.wait_ge(diag_ready, stat_ + 1)
                M(psum[:, 5, :], ones[:], diag[:].rearrange("p t s -> p (t s)"), start=True,
                  stop=True).then_inc(rs_psum, 1)

            def ffn(layer):
                n0, g0 = U_FIN[layer], layer * JT

                def body(j, s, half):
                    if not isinstance(j, int) or j >= 2:
                        pe.wait_ge(conv_done, 2 * j + (2 * g0 - 2))
                    first = isinstance(j, int) and j == 0
                    gemm(j + n0, s, hhi, hlo,
                         (lambda k: wait_low(pe, 2 * layer, k)) if first else None)

                body(0, 0, 0)
                body(1, 1, 0)
                if layer == 0:
                    for third in range(3):
                        pairs(pe, max(4 * third + 2, 2), 4 * third + 6, body)
                        pe.wait_ge(ada_added, 2 * N_GLU + 8 * third + 8)
                        reduce_acc(third % 2, THIRD * (3 + third))
                    pairs(pe, 14, JT, body)
                    pe.wait_ge(mod_ready, 1)
                else:
                    pairs(pe, 2, JT, body)

                for hf in range(2):
                    m0 = U_FOUT[layer] + 6 * hf
                    b0 = 4 * (1 - hf)

                    def down(v, s, half, m0=m0, b0=b0):
                        fixed = isinstance(v, int)
                        n_k = min(FOUT_K, JT - FOUT_K * v) if fixed else FOUT_K
                        pe.wait_ge(split_lo, v + (m0 + 1))
                        for k in range(n_k):
                            row = FOUT_K * v + k
                            pe.wait_ge(g_lo, row + (g0 + 1))
                            for f in range(4):
                                w = slice(512 * k + P * f, 512 * k + P * f + P)
                                out = psum[:, b0 + f, :]
                                st = fixed and v == 0 and k == 0
                                sp_ = fixed and row == JT - 1
                                M(out, whi[:, s, w], ghi[:, row, :], start=st, stop=False)
                                M(out, whi[:, s, w], glo[:, row, :], start=False, stop=False)
                                ins = M(out, wlo[:, s, w], ghi[:, row, :], start=False, stop=sp_)
                        ins.then_inc(unit_done, 1)

                    down(0, 0, 0)
                    down(1, 1, 0)
                    pairs(pe, 2, 4, down)
                    down(4, 0, 0)
                    down(5, 1, 0)

            pe.wait_ge(ada_added, 2 * N_GLU)
            reduce_acc(0, THIRD)
            statistic(0)
            statistic(1)
            ffn(0)
            statistic(2)
            statistic(3)

            for m in range(N_V):
                s = m % 2
                pe.wait_ge(split_lo, U_V + m + 1)
                wait(pe, v_copied, 2 * (m - 1))
                order = [(t, k) for t in range(QT) for k in range(KT)]
                if m == 0:
                    order.sort(key=lambda v: v[1])
                for t, k in order:
                    if m == 0 and t == 0:
                        wait_low(pe, 1, k)
                    out = psum[:, 2 * s + t // 2, 256 * (t % 2):256 * (t % 2) + 256]
                    tok = slice(P * t, P * t + P)
                    w = slice(256 * k, 256 * k + 256)
                    M(out, hhi[:, k, tok], whi[:, s, w], start=(k == 0 and t % 2 == 0), stop=False,
                      skip_group_check=True)
                    M(out, hlo[:, k, tok], whi[:, s, w], start=False, stop=False, skip_group_check=True)
                    ins = M(out, hhi[:, k, tok], wlo[:, s, w], start=False, stop=(k == KT - 1),
                            skip_group_check=True)
                ins.then_inc(unit_done, 1)
            pe.wait_ge(v_copied, 2 * N_V)
            pe.wait_ge(mask_ready, 3)

            def scores(h, s, qt):
                if qt == 0:
                    pe.wait_ge(qk_ready, 2 * h + 2)
                if not isinstance(h, int) or 4 * h + qt >= 1:
                    pe.wait_ge(exp_done, 8 * h + 2 * qt)
                width = (qt + 1) * P
                for c in range(2):
                    rows = slice(HD * c, HD * c + HD)
                    M(psum[:, 4 + c, 0:width], qk[rows, s, 0, P * qt:P * qt + P], qk[rows, s, 1, 0:width],
                      start=True, stop=True)
                    ins = M(psum[:, 4 + c, width - HD:width], maskw[0:1, 0, :], maskw[0:1, 1, 0:HD],
                            start=False, stop=True, skip_group_check=True)
                ins.then_inc(s_psum, 1)

            def turn(h, qt):
                pb = qt % 2
                pe.wait_ge(att_ready, 4 * h + (qt + 1))
                if not isinstance(h, int) or 4 * h + qt >= 1:
                    pe.wait_ge(attt_copied, 4 * h + qt)
                if qt == 3 and (not isinstance(h, int) or h >= 1):
                    pe.wait_ge(ot_copied, h)
                for kb in range(qt + 1):
                    ins = nc.tensor.transpose(psum[:, 6, P * kb:P * kb + P], att[:, pb, P * kb:P * kb + P], ident[:])
                ins.then_inc(attt_psum, 1)

            def weigh(h, qt):
                pb = qt % 2
                pe.wait_ge(attt_copied, 4 * h + (qt + 1))
                if qt == 0 and (not isinstance(h, int) or h >= 1):
                    pe.wait_ge(o_copied, h)
                for kb in range(qt + 1):
                    ins = M(psum[:, 7, P * qt:P * qt + P], att_t[:, pb, P * kb:P * kb + P],
                            v_sb[:, kb, bass.ds(h * P, P)] if not isinstance(h, int)
                            else v_sb[:, kb, P * h:P * h + P], start=(kb == 0), stop=(kb == qt))
                ins.then_inc(o_psum, 1)

            def turn_out(h):
                pe.wait_ge(on_ready, h + 1)
                pe.wait_ge(attt_copied, min(4 * h + 7, 4 * HEADS) if isinstance(h, int) else 4 * h + 7)
                for t in range(QT):
                    ins = nc.tensor.transpose(psum[:, 6, P * t:P * t + P], on[:, t, :], ident[:])
                ins.then_inc(ot_psum, 1)

            def project(h, s):
                pe.wait_ge(split_lo, h + (U_QK + 1))
                if not isinstance(h, int) or h >= 2:
                    pe.wait_ge(raw_copied, 2 * h - 2)
                for step in range(2 * KT):
                    ins = gemm_step(s, step, hhi, hlo)
                    if step == 2 * KT - 1:
                        ins.then_inc(unit_done, 1)
                    if step % 2:
                        yield

            def wo_step(m, k):
                pe.wait_ge(ot_lo, k + 3)
                for half in range(2):
                    ins = gemm_step(m % 2, KT * half + k, ohi, olo)
                return ins

            def attend(a_, s, fill, first=False):
                for qt in range(QT):
                    scores(a_, s, qt)
                    next(fill, None)
                    last, q = (a_ - 1, 3) if qt == 0 else (a_, qt - 1)
                    if not (first and qt == 0):
                        turn(last, q)
                    next(fill, None)
                    if not (first and qt == 0):
                        weigh(last, q)
                if not first:
                    turn_out(a_ - 1)

            def head(h, s, half, first=False):
                attend(h - 2, s, project(h, s), first)

            def early_output(steps_):
                for m, k in steps_:
                    if k == 0:
                        pe.wait_ge(split_lo, U_WO + m + 1)
                        pe.wait_ge(raw_copied, 2 * (HEADS - 1 + m))
                    wo_step(m, k)
                    yield

            for h in range(2):
                for _ in project(h, h):
                    pass
            head(2, 0, None, first=True)
            head(3, 1, None)
            pairs(pe, 4, HEADS, head)
            attend(HEADS - 2, 0, early_output([(0, k) for k in range(5)]))
            attend(HEADS - 1, 1, early_output([(1, k) for k in range(5)] + [(0, 5), (1, 5)]))
            turn(HEADS - 1, 3)
            weigh(HEADS - 1, 3)
            turn_out(HEADS - 1)
            for m in range(2):
                wo_step(m, KT - 2)
            for m in range(2):
                wo_step(m, KT - 1).then_inc(unit_done, 1)
            for m in range(2, N_WO):
                pe.wait_ge(y_ready, copied(2) + 2 * (m - 1))
                gemm(U_WO + m, m % 2, ohi, olo)
            statistic(4)
            statistic(5)
            ffn(1)
            statistic(6)


def _pair_units(w, rows, left, right, n):
    w = w.reshape(KT, P, -1) if rows is None else rows(w)
    out = np.empty((n, P, 2, KT, P), np.float32)
    for i in range(n):
        for q, c in enumerate((left(i), right(i))):
            out[i, :, q] = w[:, :, c:c + P].transpose(1, 0, 2)
    return out.reshape(n, P, UNIT)


def _units(inp):
    def glu_rows(w):
        return w.reshape(OCTS, PO, 2, CG, -1).transpose(0, 2, 1, 3, 4).reshape(KT, P, -1)

    def down_units(w):
        w = w.reshape(JT, P, D)
        padded = np.concatenate([w, np.zeros((2, P, D), np.float32)])
        return padded.reshape(6, FOUT_K, P, 2, 512).transpose(3, 0, 2, 1, 4).reshape(N_FOUT, P, UNIT)

    w_in, w_out = inp["ffn_w_in"], inp["ffn_w_out"]
    qkv, wo = inp["da_w_qkv"][0], inp["da_w_o"][0]
    ups = [_pair_units(w_in[i], None, lambda j: P * j, lambda j: DFF + P * j, N_FIN) for i in range(2)]
    values = qkv[:, 2 * D:].reshape(KT, P, N_V, 256).transpose(2, 1, 0, 3).reshape(N_V, P, UNIT)
    return np.concatenate([
        _pair_units(inp["s5_w_glu"][0], glu_rows, lambda j: P * j, lambda j: D + P * j, N_GLU),
        ups[0], down_units(w_out[0]), values,
        _pair_units(qkv, None, lambda j: P * j, lambda j: D + P * j, N_QK),
        _pair_units(wo, None, lambda j: 2 * P * j, lambda j: 2 * P * j + P, N_WO),
        ups[1], down_units(w_out[1])])


def _ada_units(w):
    rows = w.reshape(2, KT, P, 3, UNIT)
    first = rows[0, :, :, 0]
    rest = rows[0, :, :, 1:].transpose(0, 2, 1, 3)
    second = rows[1].transpose(2, 0, 1, 3)
    return np.concatenate([v.reshape(-1, P, UNIT) for v in (first, rest, second)])


def _cols(v):
    return v.reshape(-1, P).T


def _layout(inp):
    def state(v):
        v = v.reshape(PAIRS, 2, 64, *v.shape[2:])
        return v.transpose(1, 2, 0, *range(3, v.ndim)).reshape(P, PAIRS, *v.shape[3:])

    x0 = inp["x"][0]
    log_dt = np.broadcast_to(inp["s5_log_dt"][0][:, None], (GROUPS, 64))
    half = HD // 2
    inv = (ROPE_THETA ** (-np.arange(half, dtype=np.float32) / np.float32(half)).astype(np.float64)).astype(np.float32)
    sign = np.where(np.arange(P) % HD < half, -1.0, 1.0).astype(np.float32)
    conv = np.concatenate([inp["ffn_conv_w"], inp["ffn_conv_b"][:, None]], axis=1)
    return {
        "x_t": x0.T,
        "x_blocks": x0.reshape(NB, BL, GROUPS, CG)[:, ::-1].transpose(1, 3, 2, 0).reshape(P, GROUPS * NB),
        "s5_par": np.stack([state(inp["s5_a_re"][0]), state(inp["s5_a_im"][0]), state(log_dt)], axis=1),
        "s5_bc": np.stack([state(inp["s5_b_re"][0]), state(inp["s5_b_im"][0]),
                           state(inp["s5_c_re"][0].transpose(0, 2, 1)),
                           state(inp["s5_c_im"][0].transpose(0, 2, 1))], axis=1),
        "c_cols": _cols(inp["c"][0]),
        "d_cols": _cols(inp["s5_d"][0]),
        "ada_b": np.stack([_cols(v) for v in inp["ada_b"]], axis=1),
        "norm_g": np.stack([np.stack([_cols(v) for v in g], axis=1) for g in inp["norm_g"]], axis=1),
        "conv_par": conv.reshape(2, 4, 2, JT, P).transpose(4, 0, 3, 2, 1),
        "sub_g": inp["da_subln_g"][0][:, None],
        "rope_c": np.stack([np.tile(inv, P // half), sign], axis=1),
        "positions": inp["positions"][0],
        "lam_par": np.concatenate([inp[n][0] for n in ("da_lq1", "da_lk1", "da_lq2", "da_lk2")]),
        "ada_w": _ada_units(inp["ada_w"]),
        "units": _units(inp),
    }


def kernel(**inputs):
    import concourse.bacc as _bacc
    from concourse import mybir as _mybir
    from concourse.bass_utils import run_bass_kernel_spmd as _run

    inp = {k: np.asarray(v) for k, v in inputs.items()}
    arrays = {k: np.ascontiguousarray(v) for k, v in _layout(inp).items()}
    nc = _bacc.Bacc("TRN2", target_bir_lowering=False, num_devices=1)
    aps = {k: nc.dram_tensor(f"in_{k}", v.shape, _mybir.dt.from_np(v.dtype), kind="ExternalInput").ap()
           for k, v in arrays.items()}
    out = nc.dram_tensor("out_t", (D, SEQ), F32, kind="ExternalOutput").ap()
    build(nc, aps, out)
    r = _run(nc, [{f"in_{k}": v for k, v in arrays.items()}], core_ids=[0])
    return r.results[0]["out_t"].T.reshape(1, SEQ, D)
```
